# Optimizing a Trainium2 kernel written in Bass

```python
import math
import jax, jax.numpy as jnp
from jax import lax
import numpy as np

D_MODEL = 1024
BATCH = 1
SEQ = 256
DEPTH = 2
DEC_BATCH = 8
DEC_SEQ = 8
PAST_LEN = 1024
PAGE_SIZE = 128

N_MIXERS = 2
N_LAYERS_A = (DEPTH + 1) // 2
N_LAYERS_B = DEPTH // 2
H_A = 8
HD_A = 64
A_IN = 2 * H_A * HD_A + 2 * H_A * HD_A + H_A * 2 * HD_A
H_B = 16
KV_B = 4
HD_B = 64
H_I = 8
D_I = 64
IDX_ROT = D_I // 2
TOPK_MAX = 256
B_IN = H_B * HD_B + 2 * KV_B * HD_B + H_I * D_I + D_I + H_I
ROPE_THETA = 500000.0
ROT_FRAC = 4
N_EXPERTS = 16
N_GROUPS = 4
E_PER_GROUP = N_EXPERTS // N_GROUPS
TOP_K = 2
D_FF = 512
P_DIM = 256
ALPHA = (2 * DEPTH) ** 0.25
BETA = (8 * DEPTH) ** -0.25
LN_EPS = 1e-5
RMS_EPS = 1e-5
Q_BLOCK = 128

kernel_name = 'hybrid_diffattn_dsa_moe_step'

F32 = jnp.float32

def _layer_norm(x, g, b):
    xf = x.astype(F32)
    mu = jnp.mean(xf, axis=-1, keepdims=True)
    var = jnp.mean(jnp.square(xf - mu), axis=-1, keepdims=True)
    return ((xf - mu) * lax.rsqrt(var + LN_EPS) * g.astype(F32) + b.astype(F32)).astype(x.dtype)

def _rope(x, pos, rot_dim):
    half = rot_dim // 2
    inv_freq = ROPE_THETA ** (-jnp.arange(half, dtype=F32) / half)
    ang = pos.astype(F32)[:, None] * inv_freq[None, :]
    cos = jnp.cos(ang)[:, None, :]
    sin = jnp.sin(ang)[:, None, :]
    xr = x[..., :rot_dim].astype(F32)
    x1, x2 = xr[..., :half], xr[..., half:]
    rot = jnp.concatenate([x1 * cos - x2 * sin, x2 * cos + x1 * sin], axis=-1)
    return jnp.concatenate([rot.astype(x.dtype), x[..., rot_dim:]], axis=-1)

def _block(n):
    return Q_BLOCK if n % Q_BLOCK == 0 else n

def _to_blocks(x, qb):
    b, n = x.shape[:2]
    return x.reshape(b, n // qb, qb, *x.shape[2:]).swapaxes(0, 1)

def _from_blocks(y):
    nb, b, qb = y.shape[:3]
    return y.swapaxes(0, 1).reshape(b, nb * qb, *y.shape[3:])

def _gather_pages(pool, page_table):
    g = pool[page_table]
    return g.reshape(g.shape[0], g.shape[1] * g.shape[2], *g.shape[3:])

def _diff_attention(q, k, v, lam, q_pos):
    qb = _block(q.shape[1])
    k_pos = jnp.arange(k.shape[1])

    def one(blk):
        bq, bpos = blk
        mask = k_pos[None, :] <= bpos[:, None]
        s = jnp.einsum('bqhcd,bkhcd->bhcqk', bq, k).astype(F32) * (HD_A ** -0.5)
        p = jax.nn.softmax(jnp.where(mask, s, -jnp.inf), axis=-1)
        a = p[:, :, 0] - lam * p[:, :, 1]
        return jnp.einsum('bhqk,bkhe->bqhe', a.astype(v.dtype), v)

    out = lax.map(one, (_to_blocks(q, qb), q_pos.reshape(-1, qb)))
    return _from_blocks(out)

def _mixer_a(x, pos, past_k, past_v, w_in, w_out, lam_q1, lam_k1, lam_q2, lam_k2, subln, lam_init):
    b, n, _ = x.shape
    qkv = x @ w_in
    q, k, v = jnp.split(qkv, [2 * H_A * HD_A, 4 * H_A * HD_A], axis=-1)
    q = _rope(q.reshape(b, n, 2 * H_A, HD_A), pos, HD_A // ROT_FRAC)
    k = _rope(k.reshape(b, n, 2 * H_A, HD_A), pos, HD_A // ROT_FRAC)
    v = v.reshape(b, n, H_A, 2 * HD_A)
    k_all = k if past_k is None else jnp.concatenate([past_k, k], axis=1)
    v_all = v if past_v is None else jnp.concatenate([past_v, v], axis=1)
    lam = (jnp.exp(jnp.sum(lam_q1.astype(F32) * lam_k1.astype(F32)))
           - jnp.exp(jnp.sum(lam_q2.astype(F32) * lam_k2.astype(F32))) + lam_init)
    o = _diff_attention(q.reshape(b, n, H_A, 2, HD_A), k_all.reshape(b, -1, H_A, 2, HD_A), v_all, lam, pos)
    of = o.astype(F32)
    of = of * lax.rsqrt(jnp.mean(of * of, axis=-1, keepdims=True) + RMS_EPS) * subln.astype(F32) * (1.0 - lam_init)
    y = of.astype(x.dtype).reshape(b, n, H_A * 2 * HD_A) @ w_out
    return y, k, v

def _dsa_attention(q, k, v, qi, ki, wi, q_pos):
    b, nq = q.shape[:2]
    nk = k.shape[1]
    n_sel = min(TOPK_MAX, nk // 4)
    qb = _block(nq)
    grp = H_B // KV_B
    k_pos = jnp.arange(nk)
    idx_scale = (H_I ** -0.5) * (D_I ** -0.5)

    def one(blk):
        bq, bqi, bwi, bpos = blk
        mask = k_pos[None, :] <= bpos[:, None]
        dots = jnp.einsum('bqhd,bkd->bqhk', bqi, ki).astype(F32)
        score = jnp.einsum('bqh,bqhk->bqk', bwi.astype(F32) * idx_scale, jax.nn.relu(dots))
        score = jnp.where(mask[None], score, -jnp.inf)
        _, idx = lax.top_k(score, n_sel)
        valid = k_pos[idx] <= bpos[None, :, None]
        ks = jax.vmap(lambda kk, ii: kk[ii])(k, idx)
        vs = jax.vmap(lambda vv, ii: vv[ii])(v, idx)
        s = jnp.einsum('bqhgd,bqkhd->bqhgk', bq.reshape(b, qb, KV_B, grp, HD_B), ks).astype(F32) * (HD_B ** -0.5)
        p = jax.nn.softmax(jnp.where(valid[:, :, None, None, :], s, -jnp.inf), axis=-1)
        o = jnp.einsum('bqhgk,bqkhd->bqhgd', p.astype(vs.dtype), vs)
        return o.reshape(b, qb, H_B, HD_B)

    out = lax.map(one, (_to_blocks(q, qb), _to_blocks(qi, qb), _to_blocks(wi, qb), q_pos.reshape(-1, qb)))
    return _from_blocks(out)

def _mixer_b(x, pos, past_k, past_v, past_ki, w_in, w_out):
    b, n, _ = x.shape
    sizes = (H_B * HD_B, KV_B * HD_B, KV_B * HD_B, H_I * D_I, D_I, H_I)
    offs = [sum(sizes[:m]) for m in range(1, len(sizes))]
    q, k, v, qi, ki, wi = jnp.split(x @ w_in, offs, axis=-1)
    q = _rope(q.reshape(b, n, H_B, HD_B), pos, HD_B // ROT_FRAC)
    k = _rope(k.reshape(b, n, KV_B, HD_B), pos, HD_B // ROT_FRAC)
    v = v.reshape(b, n, KV_B, HD_B)
    qi = _rope(qi.reshape(b, n, H_I, D_I), pos, IDX_ROT)
    ki = _rope(ki.reshape(b, n, 1, D_I), pos, IDX_ROT)[:, :, 0]
    k_all = k if past_k is None else jnp.concatenate([past_k, k], axis=1)
    v_all = v if past_v is None else jnp.concatenate([past_v, v], axis=1)
    ki_all = ki if past_ki is None else jnp.concatenate([past_ki, ki], axis=1)
    o = _dsa_attention(q, k_all, v_all, qi, ki_all, wi, pos)
    y = o.reshape(b, n, H_B * HD_B) @ w_out
    return y, k, v, ki

def _moe(x, router_w, router_b, w_gate, w_up, w_down):
    b, n, d = x.shape
    t = x.reshape(b * n, d)
    aff = jax.nn.sigmoid((t @ router_w).astype(F32))
    sel = aff + router_b.astype(F32)
    grp_score = lax.top_k(sel.reshape(-1, N_GROUPS, E_PER_GROUP), TOP_K)[0].sum(-1)
    g = jnp.argmax(grp_score, axis=-1)
    in_group = (jnp.arange(N_EXPERTS) // E_PER_GROUP)[None, :] == g[:, None]
    _, idx = lax.top_k(jnp.where(in_group, sel, -jnp.inf), TOP_K)
    gate = jnp.take_along_axis(aff, idx, axis=-1)
    gate = gate / jnp.sum(gate, axis=-1, keepdims=True)
    combine = jnp.sum(jax.nn.one_hot(idx, N_EXPERTS, dtype=F32) * gate[..., None], axis=1).astype(t.dtype)
    out = jnp.zeros_like(t)
    for e in range(N_EXPERTS):
        hdn = jax.nn.silu(t @ w_gate[e]) * (t @ w_up[e])
        out = out + combine[:, e:e + 1] * (hdn @ w_down[e])
    return out.reshape(b, n, d)

def _trunk(x, p, pos, past_a, past_b, a_w_in, a_w_out, a_lam_q1, a_lam_k1, a_lam_q2, a_lam_k2, a_subln,
           b_w_in, b_w_out, ln_g, ln_b, router_w, router_b, moe_w_gate, moe_w_up, moe_w_down,
           ple_proj, ple_gate_w, ple_gate_b):
    new_a, new_b = [], []
    for i in range(DEPTH):
        j = i // N_MIXERS
        if i % N_MIXERS == 0:
            pk, pv = (None, None) if past_a is None else past_a[j]
            lam_init = 0.8 - 0.6 * math.exp(-0.3 * i)
            h, k, v = _mixer_a(x, pos, pk, pv, a_w_in[j], a_w_out[j], a_lam_q1[j], a_lam_k1[j],
                               a_lam_q2[j], a_lam_k2[j], a_subln[j], lam_init)
            new_a.append((k, v))
        else:
            pk, pv, pki = (None, None, None) if past_b is None else past_b[j]
            h, k, v, ki = _mixer_b(x, pos, pk, pv, pki, b_w_in[j], b_w_out[j])
            new_b.append((k, v, ki))
        x = _layer_norm(ALPHA * x + h, ln_g[i, 0], ln_b[i, 0])
        x = _layer_norm(ALPHA * x + _moe(x, router_w, router_b, moe_w_gate[i], moe_w_up[i], moe_w_down[i]),
                        ln_g[i, 1], ln_b[i, 1])
        x = x + jax.nn.sigmoid(x @ ple_gate_w[i] + ple_gate_b[i]) * (p[i] @ ple_proj[i])
    return x, new_a, new_b

def setup_inputs(seed: int = 0) -> dict:
    key = jax.random.key(seed)
    ks = jax.random.split(key, 32)
    nrm = lambda kk, shape, scale: jax.random.normal(kk, shape, F32) * scale
    n_pages = PAST_LEN // PAGE_SIZE
    n_used = DEC_BATCH * n_pages
    n_pool = n_used + max(1, n_used // 4)
    page_table = jax.random.permutation(ks[0], n_pool)[:n_used].reshape(DEC_BATCH, n_pages).astype(jnp.int32)
    return {
        'x_prompt': nrm(ks[1], (BATCH, SEQ, D_MODEL), 1.0),
        'x_sample': nrm(ks[2], (DEC_BATCH, DEC_SEQ, D_MODEL), 1.0),
        'cache_a_k': nrm(ks[3], (N_LAYERS_A, n_pool, PAGE_SIZE, 2 * H_A, HD_A), 1.0),
        'cache_a_v': nrm(ks[4], (N_LAYERS_A, n_pool, PAGE_SIZE, H_A, 2 * HD_A), 1.0),
        'cache_b_k': nrm(ks[5], (N_LAYERS_B, n_pool, PAGE_SIZE, KV_B, HD_B), 1.0),
        'cache_b_v': nrm(ks[6], (N_LAYERS_B, n_pool, PAGE_SIZE, KV_B, HD_B), 1.0),
        'cache_b_kidx': nrm(ks[7], (N_LAYERS_B, n_pool, PAGE_SIZE, D_I), 1.0),
        'page_table': page_table,
        'p_prompt': nrm(ks[8], (DEPTH, BATCH, SEQ, P_DIM), 1.0),
        'p_sample': nrm(ks[9], (DEPTH, DEC_BATCH, DEC_SEQ, P_DIM), 1.0),
        'a_w_in': nrm(ks[10], (N_LAYERS_A, D_MODEL, A_IN), D_MODEL ** -0.5),
        'a_w_out': nrm(ks[11], (N_LAYERS_A, H_A * 2 * HD_A, D_MODEL), BETA * (H_A * 2 * HD_A) ** -0.5),
        'a_lam_q1': nrm(ks[12], (N_LAYERS_A, HD_A), 0.1),
        'a_lam_k1': nrm(ks[13], (N_LAYERS_A, HD_A), 0.1),
        'a_lam_q2': nrm(ks[14], (N_LAYERS_A, HD_A), 0.1),
        'a_lam_k2': nrm(ks[15], (N_LAYERS_A, HD_A), 0.1),
        'a_subln': 1.0 + nrm(ks[16], (N_LAYERS_A, 2 * HD_A), 0.02),
        'b_w_in': nrm(ks[17], (N_LAYERS_B, D_MODEL, B_IN), D_MODEL ** -0.5),
        'b_w_out': nrm(ks[18], (N_LAYERS_B, H_B * HD_B, D_MODEL), BETA * (H_B * HD_B) ** -0.5),
        'ln_g': 1.0 + nrm(ks[19], (DEPTH, 2, D_MODEL), 0.02),
        'ln_b': nrm(ks[20], (DEPTH, 2, D_MODEL), 0.02),
        'router_w': nrm(ks[21], (D_MODEL, N_EXPERTS), D_MODEL ** -0.5),
        'router_b': nrm(ks[22], (N_EXPERTS,), 0.01),
        'moe_w_gate': nrm(ks[23], (DEPTH, N_EXPERTS, D_MODEL, D_FF), D_MODEL ** -0.5),
        'moe_w_up': nrm(ks[24], (DEPTH, N_EXPERTS, D_MODEL, D_FF), D_MODEL ** -0.5),
        'moe_w_down': nrm(ks[25], (DEPTH, N_EXPERTS, D_FF, D_MODEL), BETA * D_FF ** -0.5),
        'ple_proj': nrm(ks[26], (DEPTH, P_DIM, D_MODEL), P_DIM ** -0.5),
        'ple_gate_w': nrm(ks[27], (DEPTH, D_MODEL, D_MODEL), D_MODEL ** -0.5),
        'ple_gate_b': nrm(ks[28], (DEPTH, D_MODEL), 0.02),
    }

def reference(x_prompt, x_sample, cache_a_k, cache_a_v, cache_b_k, cache_b_v, cache_b_kidx, page_table,
              p_prompt, p_sample, a_w_in, a_w_out, a_lam_q1, a_lam_k1, a_lam_q2, a_lam_k2, a_subln,
              b_w_in, b_w_out, ln_g, ln_b, router_w, router_b, moe_w_gate, moe_w_up, moe_w_down,
              ple_proj, ple_gate_w, ple_gate_b):
    past_len = page_table.shape[1] * cache_a_k.shape[2]
    pos_prompt = jnp.arange(x_prompt.shape[1])
    pos_sample = past_len + jnp.arange(x_sample.shape[1])
    weights = (a_w_in, a_w_out, a_lam_q1, a_lam_k1, a_lam_q2, a_lam_k2, a_subln, b_w_in, b_w_out, ln_g, ln_b,
               router_w, router_b, moe_w_gate, moe_w_up, moe_w_down, ple_proj, ple_gate_w, ple_gate_b)
    y_prompt, na_p, nb_p = _trunk(x_prompt, p_prompt, pos_prompt, None, None, *weights)
    past_a = [(_gather_pages(cache_a_k[j], page_table), _gather_pages(cache_a_v[j], page_table))
              for j in range(N_LAYERS_A)]
    past_b = [(_gather_pages(cache_b_k[j], page_table), _gather_pages(cache_b_v[j], page_table),
               _gather_pages(cache_b_kidx[j], page_table)) for j in range(N_LAYERS_B)]
    y_sample, na_s, nb_s = _trunk(x_sample, p_sample, pos_sample, past_a, past_b, *weights)
    a_k_p = jnp.stack([e[0] for e in na_p])
    a_v_p = jnp.stack([e[1] for e in na_p])
    b_k_p = jnp.stack([e[0] for e in nb_p])
    b_v_p = jnp.stack([e[1] for e in nb_p])
    b_ki_p = jnp.stack([e[2] for e in nb_p])
    a_k_s = jnp.stack([e[0] for e in na_s])
    a_v_s = jnp.stack([e[1] for e in na_s])
    b_k_s = jnp.stack([e[0] for e in nb_s])
    b_v_s = jnp.stack([e[1] for e in nb_s])
    b_ki_s = jnp.stack([e[2] for e in nb_s])
    return (y_prompt, y_sample, a_k_p, a_v_p, b_k_p, b_v_p, b_ki_p, a_k_s, a_v_s, b_k_s, b_v_s, b_ki_s)


_drawn_inputs = setup_inputs


def setup_inputs(seed=0):
    import zlib

    import numpy as np

    out = dict(_drawn_inputs(seed))
    spreads = {}
    factors = {'a_lam_q2': 3.507, 'a_subln': 2.916, 'ple_gate_b': 2.845}
    for name, (base, spread) in spreads.items():
        noise = np.random.default_rng([zlib.crc32(name.encode()), seed]).standard_normal(out[name].shape)
        drawn = base * np.exp(spread * noise) if base else spread * noise
        out[name] = __import__('jax').numpy.asarray(drawn.astype(out[name].dtype))
    for name, factor in factors.items():
        out[name] = (out[name] * factor).astype(out[name].dtype)
    return out
```

```python
from contextlib import ExitStack

import numpy as np
import concourse.bass as bass
from concourse import mybir

F32 = mybir.dt.float32
I32 = mybir.dt.int32
U32 = mybir.dt.uint32
ALU = mybir.AluOpType
ACT = mybir.ActivationFunctionType
AX = mybir.AxisListType

D = 1024
P = 128
KD = D // P
SEQ = 256
DB, DQ = 8, 8
NS = DB * DQ
TOK = SEQ + NS
TILES = ((0, 128), (128, 128), (256, NS))
PAGE = 128
NPAGE = 8
PAST = PAGE * NPAGE
NK = PAST + NS
HA, HB, KVB, HI, HD = 8, 16, 4, 8, 64
NE, NG, EG, FF, PD = 16, 4, 4, 512, 256
FK = FF // P
A_IN = 3 * D
B_IN = HB * HD + 2 * KVB * HD + HI * HD + HD + HI
OFF_K, OFF_V, OFF_QI, OFF_KI, OFF_WI = 1024, 1280, 1536, 2048, 2112
SEL_PROMPT, SEL_SAMPLE = 64, 256
ALPHA = 4.0 ** 0.25
EPS = 1e-5
SCALE = HD ** -0.5
IDX_SCALE = (HI ** -0.5) * (HD ** -0.5)
LAM_INIT = 0.2
OUT_GAIN = 1.0 - LAM_INIT
BIG = 1e30
NEG, PICKED = -2e38, -3e38
AT_BANK = (7, 0, 1)
SLOTS = 6


def const_layout():
    at, out = 0, {}
    for name, n in (("ident", 128), ("causal", 2 * 256), ("newmask", DB * NS), ("fold", 128), ("c0", 1), ("c1", 1),
                    ("eps", 1), ("cosA", 3 * 8), ("sinA", 3 * 8), ("cosI", 3 * 16), ("sinI", 3 * 16),
                    ("selnew", NS), ("expcode", 3 * NE), ("grpcode", 3 * NG), ("before", 128), ("ones", 128),
                    ("slotbase", 3 * NE)):
        out[name] = (at, n)
        at += n
    return out, at


CONST, CONST_COLS = const_layout()


def constants():
    c = np.zeros((P, CONST_COLS), np.float32)

    def put(name, v):
        a, n = CONST[name]
        v = np.asarray(v, np.float32).reshape(v.shape[0], n)
        c[:v.shape[0], a:a + n] = v

    r = np.arange(P)
    put("ident", np.eye(P))
    key = np.arange(256)
    put("causal", np.stack([np.where(key[None] <= (r + 128 * t)[:, None], 0.0, -BIG) for t in range(2)], 1))
    tok = np.arange(NS)
    ok = (tok[None, None] // DQ == np.arange(DB)[None, :, None]) & (tok[None, None] % DQ <= (r % DQ)[:, None, None])
    put("newmask", np.where(ok, 0.0, -BIG))
    fold = np.zeros((P, P))
    for row in range(P):
        h, q = row // 16, row % 8
        fold[row, 32 * (h // 2) + 8 * (h % 2) + q] = 1
    put("fold", fold)
    put("c0", ((r // 8) % 2 == 0)[:, None])
    put("c1", ((r // 8) % 2 == 1)[:, None])
    put("eps", np.full((P, 1), EPS))
    pos = np.zeros((P, 3), np.float32)
    pos[:, 0], pos[:, 1] = r, r + 128
    pos[:NS, 2] = PAST + tok % DQ
    for name, half in (("A", 8), ("I", 16)):
        inv = (np.float32(500000.0) ** (-np.arange(half, dtype=np.float32) / np.float32(half))).astype(np.float32)
        ang = (pos[:, :, None] * inv).astype(np.float32)
        put("cos" + name, np.cos(ang))
        put("sin" + name, np.sin(ang))
    ok = (tok[:, None] // DQ == tok[None] // DQ) & (tok[None] % DQ <= tok[:, None] % DQ)
    put("selnew", np.where(ok, 0.0, NEG))
    put("expcode", np.broadcast_to(NE - np.arange(NE), (P, 3, NE)))
    put("grpcode", np.broadcast_to(NG - np.arange(NG), (P, 3, NG)))
    put("before", r[:, None] < r[None])
    put("ones", np.ones((P, P)))
    put("slotbase", np.broadcast_to(np.arange(NE) * 128, (P, 3, NE)))
    spread = (tok[:, None, None, None] == np.arange(DB)[None, :, None, None] * DQ + np.arange(DQ)[None, None, None]) \
        * np.ones((1, 1, 8, 1))
    sp = np.zeros((P, DB * 64), np.float32)
    sp[:NS] = spread.reshape(NS, -1)
    return c, sp


PER_LAYER = {
    "qkv_mm#": 18, "qkv_evac#": 18, "xt#_mm": 6, "xt#_evac": 6, "rotated#": 3, "out_mm#": 6, "out_evac#": 6,
    "ple_mm#": 6, "experts_used#": 3 * NE, "pq#_mm": 8, "pq#_evac": 8, "pq#_zero": 1, "ps#_mm": 16, "pmask#": 16,
    "pmax#": 16, "pexp#": 16, "pw#": 16, "pat#_mm": 16, "pat#_evac": 16, "po#_mm": 16, "po#": 16,
    "po_t#_mm": 4, "po_t#_evac": 4, "so_t#_mm": 4, "so_t#_evac": 8, "xtr#_mm": 6, "xtr#_evac": 6,
    "router_landed#": 16, "logit_mm#": 2, "logit_evac#": 1, "aff_ones#": 1, "aff#": 1, "acc_zero#": 1,
    "mask_ready#": 1, "pos_mm#": 1, "dispatch_ready#": 1, "scattered#": 16 * 6, "rows_a_landed#": 8 * NE, "rows_b_landed#": 8 * NE,
    "xe_mm#": 2 * NE, "xe_evac#": 2 * NE, "sp_gate_up_mm#": NE, "sp_sig#": NE, "sp_hidden#": NE, "sp_ht_mm#": NE,
    "sp_ht_evac#": NE, "sp_y_mm#": NE, "sp_y_act#": NE + 1, "sp_y_dve#": NE + 1, "sp_y_a_stored#": 8 * NE + 16, "sp_y_b_stored#": 8 * NE + 16,
    "gathered#": 16 * 6, "chain_sparse#": NE + 9, "chain_dense#": 12 * NE // 2 + 3,
    "h_ready#": 3 * NE + 2, "gate_up_mm#": 3 * NE, "ht_mm#": 3 * NE, "ht_evac#": 3 * NE + 2, "y_mm#": 3 * NE,
    "y_used#": 3 * NE + 1, "sig#": 3 * NE, "p_landed#": 48, "pt_mm#": 1, "pt_evac#": 1, "xtg#_mm": 6, "xtg#_evac": 6,
    "gated#": 6, "gate_b_landed#": 16, "gate_biased#": 6, "gate_sig#": 6, "norm_landed#0": 32, "norm_landed#1": 32,
    "normed#0": 3, "normed#1": 3, "var#0": 1, "var#1": 1, "std#0": 1, "std#1": 1,
}


def stage_of(name):
    for n, ch in enumerate(name):
        if ch in "01" and name[:n] + "#" + name[n + 1:] in PER_LAYER:
            return name[:n] + "#" + name[n + 1:], int(ch)
    return name, 0


class Stream:

    def __init__(self):
        self.items, self.landed, self.used, self.total = {}, [], [], [0] * SLOTS

    def add(self, name, used, dmas=1):
        n = len(self.landed)
        self.items[name] = n
        self.total[n % SLOTS] += 16 * dmas
        self.landed.append(self.total[n % SLOTS])
        self.used.append(used)


def plan():
    s = Stream()
    for j in range(6):
        s.add(("a_in", j), ("qkv_mm0", 3 * j + 3))
    for j in range(2):
        s.add(("a_out", j), ("out_mm0", 3 * j + 3))
    for layer in range(2):
        for e in range(NE):
            for j in range(3):
                s.add(("moe", layer, e, j), (f"experts_used{layer}", 3 * e + j + 1))
        s.add(("ple_g", layer, 0), (f"ple_mm{layer}", 3))
        s.add(("ple_p", layer), (f"ple_mm{layer}", 6))
        s.add(("ple_g", layer, 1), (f"ple_mm{layer}", 6))
        if layer == 0:
            for j in range(5):
                s.add(("b_in", j), ("qkv_mm1", 3 * j + 3))
            s.add("kidx", ("kidx_mm", 8), DB * NPAGE)
            for pr in range(4):
                s.add(("kb", pr), ("kbt_mm", 8 * pr + 8), 2 * NPAGE)
                s.add(("vb", pr), ("pvb_mm", 2 * pr + 2), 2 * NPAGE)
            for j in range(2):
                s.add(("b_out", j), ("out_mm1", 3 * j + 3))
    return s


def pieces(t, w):
    if t < 2:
        return [(0, 128, 0, w)]
    return [(0, NS, 0, w // 2), (NS, 2 * NS, w // 2, w)]


def build(nc, x_prompt, x_sample, cache_a_k, cache_a_v, cache_b_k, cache_b_v, cache_b_kidx, page_table,
          p_prompt, p_sample, a_w_in, a_w_out, a_lam_q1, a_lam_k1, a_lam_q2, a_lam_k2, a_subln,
          b_w_in, b_w_out, ln_g, ln_b, router_w, router_b, moe_w_gate, moe_w_up, moe_w_down,
          ple_proj, ple_gate_w, ple_gate_b, consts, spread_c, outs):
    stream = plan()
    pool_pages = cache_a_k.shape[1]
    with ExitStack() as ctx:
        def sb(name, shape, dt=F32):
            return ctx.enter_context(nc.sbuf_tensor(name, shape, dt))

        sems = {}

        def S(name):
            base = stage_of(name)[0]
            if base not in sems:
                sems[base] = ctx.enter_context(nc.semaphore(base))
            return sems[base]

        def at(name, value):
            base, layer = stage_of(name)
            return S(name), value + (PER_LAYER[base] if layer else 0)

        ring = sb("ring", [P, SLOTS, 4096])
        X = sb("X", [P, 3, D])
        XT = sb("XT", [P, KD, TOK])
        QKV = sb("QKV", [P, 3, A_IN])
        KT = sb("KT", [P, KD, TOK])
        QB = sb("QB", [P, 2048])
        PR = sb("PR", [P, NK])
        KP = sb("KP", [P, 2048])
        OR = sb("OR", [P, 2048])
        SM = sb("SM", [P, 2, 512])
        C = sb("C", [P, CONST_COLS])
        IDX = sb("IDX", [P, 8], U32)
        COUNT = sb("COUNT", [1, NE + 1], I32)
        G = sb("G", [P, 14, 48])
        small = sb("small", [P, 160])
        pt_sb = sb("pt_sb", [1, DB * NPAGE], page_table.dtype)
        PS = ctx.enter_context(nc.psum_tensor("PS", [P, 8, 512], F32))
        PSF = PS[:, :, :].rearrange("p b n -> p (b n)")

        def cst(name, rows=P):
            a, n = CONST[name]
            return C[0:rows, a:a + n]

        ident = cst("ident")
        causal = cst("causal").rearrange("p (t k) -> p t k", t=2)
        newmask = cst("newmask").rearrange("p (b k) -> p b k", b=DB)
        spread = cst("newmask").rearrange("p (b r) -> p b r", b=DB)

        AT = XT[:, :, :].rearrange("p k n -> p (k n)")[:, 0:9 * 128].rearrange("p (j r) -> p j r", j=9)
        QZ = KP[:, 0:1024].rearrange("p (u c q) -> p u c q", u=2, c=2)
        ATP = KP[:, 1024:2048].rearrange("p (u c n) -> p u c n", u=2, c=2)
        KPG = KP[:, :].rearrange("p (u k n) -> p u k n", u=2, k=KD)
        KBT = KP[:, :].rearrange("p (c n) -> p c n", c=2)
        KIT = KP[:, :].rearrange("p (u n) -> p u n", u=2)
        GAIN, SHIFT = KP[:, 0:D], KP[:, D:2 * D]
        QBA = QB[:, :].rearrange("p (b h r) -> p b h r", b=DB, h=HA)
        QBB = QB[:, 0:1024].rearrange("p (b c r) -> p b c r", b=DB, c=2)
        QIB = QB[:, 1024:1536].rearrange("p (u r) -> p u r", u=4)
        WS = QB[:, 1536:1792].rearrange("p (u r) -> p u r", u=4)
        QCUR = SM[:, :, 0:256].rearrange("p u (h r) -> p u h r", h=HA)
        FOLD = SM[:, :, 256:384]
        SMF = SM[:, :, :].rearrange("p u n -> p (u n)")
        OB = SMF.rearrange("p (b u d) -> p b u d", b=DB, u=2)
        SELB = OR[:, 0:NK]
        PB = OR[:, NK:NK + 512].rearrange("p (t k) -> p t k", t=2)
        lamt = OR[:, 0:256].rearrange("p (m d) -> p m d", m=4)
        NMAX, SUMS, RC = small[:, 8:16], small[:, 16:24], small[:, 24:32]
        SUBLN, SGN, NLAM = small[:, 0:1], small[:, 1:2], small[:, 2:3]
        RMS = small[:, 32:64]
        STATS = small[:, 64:100].rearrange("p (t n) -> p t n", t=3)
        MV = small[:, 100:106].rearrange("p (t n) -> p t n", t=3)
        RSTD = small[:, 106:109]
        WI = small[:, 110:134].rearrange("p (t h) -> p t h", t=3)
        TOP8 = small[:, 134:142]

        DUP_K, DUP_I = B_IN, B_IN + 512
        QF = QKV[:, :, :].rearrange("p t n -> p (t n)")
        ACC = QF[:, 0:3072].rearrange("p (t n) -> p t n", t=3)
        MSG = QF[:, 4096:5120].rearrange("p (u n) -> p u n", u=2)
        MH = QF[:, 5120:6144].rearrange("p (u n) -> p u n", u=2)
        MHT = QF[:, 7168:8192].rearrange("p (u k n) -> p u k n", u=2, k=FK)
        XR = QF[:, 0:2048].rearrange("p (u n) -> p u n", u=2)
        XE = QF[:, 2048:3072].rearrange("p (k n) -> p k n", k=KD)
        YS = (QF[:, 6144:7168], QF[:, 8192:9216])
        YG = QF[:, 0:6144].rearrange("p (r t n) -> p r t n", r=2, t=3)
        GATES = small[:, 142:148].rearrange("p (r t) -> p r t", r=2)
        places = nc.dram_tensor("places", [NE * 128, D], F32).ap()
        PT = KT[:, 0:2, :]

        landed = [S(f"ring_landed{s}") for s in range(SLOTS)]
        k_landed = [S(f"kpage_landed{s}") for s in range(NPAGE)]
        v_landed = [S(f"vpages_landed{s}") for s in range(2)]
        kpage = ring[:, 0:2, :].rearrange("p s (j n) -> p (s j) n", j=4)
        vpage = ring[:, 2:6, :].rearrange("p s (j n) -> p (s j) n", j=4)

        y_p, y_s, nak_p, nav_p, nbk_p, nbv_p, nbi_p, nak_s, nav_s, nbk_s, nbv_s, nbi_s = outs

        def item(name):
            n = stream.items[name]
            return n, n % SLOTS

        def token_rows(prompt, sample, t):
            t0, n = TILES[t]
            return prompt[t0:t0 + n, :] if t < 2 else sample

        block = ctx.enter_context(nc.Block())

        @block.sync
        def _(sp):
            sp.wait_ge(*at("page_table_landed", 16))

            def place(name):
                n, s = item(name)
                if n >= SLOTS:
                    sp.wait_ge(*at(stream.used[n - SLOTS][0], stream.used[n - SLOTS][1]))
                return s

            def columns(name, w, c0, c1, rows_together):
                view = w.rearrange("(p k) n -> p k n", k=KD) if rows_together else \
                    w.rearrange("(k p) n -> p k n", p=P)
                s = place(name)
                sp.dma_start(ring[:, s, 0:KD * (c1 - c0)].rearrange("p (k n) -> p k n", k=KD),
                             view[:, :, c0:c1]).then_inc(landed[s], 16)

            def page_id(b, j):
                return sp.value_load(pt_sb[0:1, bass.ds(b * NPAGE + j, 1)], min_val=0, max_val=pool_pages - 1)

            for j in range(6):
                columns(("a_in", j), a_w_in[0], 512 * j, 512 * j + 512, True)

            def pages(b, par, first):
                for j in range(NPAGE):
                    pg = page_id(b, j)
                    if first and par == 0:
                        sp.wait_ge(*at("qkv_mm0", 3 * (j // 4 + 1)))
                    else:
                        sp.wait_ge(*at("kt_page_mm", b * 16 + (2 * j + 2 - 16)))
                    sp.dma_start(kpage[:, j, :], cache_a_k[0, bass.ds(pg, 1)].rearrange("a p h d -> (a p) (h d)"))\
                      .then_inc(k_landed[j], 16)
                    if first:
                        sp.wait_ge(*at("qkv_mm0", 3 * (2 + (8 * par + j) // 4 + 1)))
                    elif j == 0:
                        sp.wait_ge(*at("pv_mm", b - 1))
                    sp.dma_start(vpage[:, par * NPAGE + j, :],
                                 cache_a_v[0, bass.ds(pg, 1)].rearrange("a p h d -> (a p) (h d)"))\
                      .then_inc(v_landed[par], 16)

            pages(0, 0, True)
            pages(1, 1, True)
            with sp.Fori(1, DB // 2) as i:
                pages(i * 2, 0, False)
                pages(i * 2 + 1, 1, False)

            sp.wait_ge(*at("kt_page_mm", 16 * DB))
            for j in range(2):
                columns(("a_out", j), a_w_out[0], 512 * j, 512 * j + 512, False)
            sp.wait_ge(*at("pv_mm", DB))

            for layer in range(2):
                n0 = stream.items[("moe", layer, 0, 0)]

                def expert(e, j, wait):
                    s = (n0 + j) % SLOTS
                    wait()
                    w = (moe_w_gate, moe_w_up, moe_w_down)[j % 3]
                    sp.dma_start(ring[:, s, :], w[layer, bass.ds(e, 1)].rearrange("a (p k) n -> (a p) (k n)", p=P))\
                      .then_inc(landed[s], 16)

                for j in range(6):
                    n = n0 + j - SLOTS
                    before = layer == 0 and n < 6
                    expert(j // 3, j, (lambda: None) if before else
                           (lambda n=n: sp.wait_ge(*at(stream.used[n][0], stream.used[n][1]))))
                with sp.Fori(1, NE // 2) as i:
                    for j in range(6):
                        expert(i * 2 + j // 3, j, lambda j=j: sp.wait_ge(*at(f"experts_used{layer}", i * 6 + (j - 5))))
                columns(("ple_g", layer, 0), ple_gate_w[layer], 0, 512, True)
                s = place(("ple_p", layer))
                sp.dma_start(ring[:, s, 0:2048], ple_proj[layer].rearrange("(p k) n -> p (k n)", k=2))\
                  .then_inc(landed[s], 16)
                columns(("ple_g", layer, 1), ple_gate_w[layer], 512, 1024, True)
                if layer == 0:
                    for j in range(5):
                        columns(("b_in", j), b_w_in[0], 512 * j, min(512 * j + 512, B_IN), True)
                    s = place("kidx")
                    kx = ring[:, s, :].rearrange("p (r j b d) -> p r j b d", r=4, b=2, j=NPAGE)
                    for b in range(DB):
                        for j in range(NPAGE):
                            pg = page_id(b, j)
                            sp.dma_start(kx[:, b // 2, j, b % 2, :],
                                         cache_b_kidx[0, bass.ds(pg, 1)].rearrange("a p d -> (a p) d"))\
                              .then_inc(landed[s], 16)
                    for pr in range(4):
                        for what, cache in (("kb", cache_b_k), ("vb", cache_b_v)):
                            s = place((what, pr))
                            for bb in range(2):
                                for j in range(NPAGE):
                                    pg = page_id(2 * pr + bb, j)
                                    c0 = (bb * NPAGE + j) * KVB * HD
                                    sp.dma_start(ring[:, s, c0:c0 + KVB * HD],
                                                 cache[0, bass.ds(pg, 1)].rearrange("a p h d -> (a p) (h d)"))\
                                      .then_inc(landed[s], 16)
                    for j in range(2):
                        columns(("b_out", j), b_w_out[0], 512 * j, 512 * j + 512, False)

        @block.gpsimd
        def _(pool):
            pool.dma_start(pt_sb[:, :], page_table.rearrange("(o b) j -> o (b j)", o=1))\
                .then_inc(S("page_table_landed"), 16)
            pool.dma_start(C[:, :], consts).then_inc(S("const_landed"), 16)
            for t, (t0, n) in enumerate(TILES):
                pool.dma_start(X[0:n, t, :], token_rows(x_prompt[0], x_sample.rearrange("b q d -> (b q) d"), t))\
                    .then_inc(S(f"x_landed{t}"), 16)
            pool.dma_start(SUBLN, a_subln.rearrange("a d -> d a")).then_inc(S("subln_landed"), 16)
            for m, w in enumerate((a_lam_q1, a_lam_k1, a_lam_q2, a_lam_k2)):
                pool.dma_start(lamt[:, m, :], w[0].partition_broadcast(P)).then_inc(S("lam_landed"), 16)
            pool.dma_start(G[:, 13, 0:NE], router_b.partition_broadcast(P)).then_inc(S("router_b_landed"), 16)

            pool.wait_ge(*at("qb_zero", 1))
            for c in range(8):
                pool.dma_start(places.rearrange("(p a) n -> p (a n)", p=P)[:, 2048 * c:2048 * c + 2048], QB[:, :])\
                    .then_inc(S("places_zeroed"), 16)

            for t, (t0, n) in enumerate(TILES):
                pool.wait_ge(*at("rotated0", t + 1))
                pool.dma_start(token_rows(nak_p[0, 0].rearrange("s h d -> s (h d)"),
                                          nak_s[0].rearrange("b q h d -> (b q) (h d)"), t),
                               QKV[0:n, t, D:2 * D]).then_inc(S("stored"), 16)
                pool.wait_ge(*at("qkv_evac0", 15 + t + 1))
                pool.dma_start(token_rows(nav_p[0, 0].rearrange("s h d -> s (h d)"),
                                          nav_s[0].rearrange("b q h d -> (b q) (h d)"), t),
                               QKV[0:n, t, 2 * D:3 * D]).then_inc(S("stored"), 16)

            for layer in range(2):
                pool.wait_ge(*at(f"out_mm{layer}", 6))

                def norm_params(which):
                    for ap, w in ((GAIN, ln_g), (SHIFT, ln_b)):
                        pool.dma_start(ap, w[layer, which].partition_broadcast(P))\
                            .then_inc(S(f"norm_landed{layer}{which}"), 16)

                norm_params(0)
                pool.dma_start(SMF[:, 0:KD * NE].rearrange("p (k e) -> p k e", k=KD),
                               router_w.rearrange("(p k) e -> p k e", k=KD)).then_inc(S(f"router_landed{layer}"), 16)
                pool.wait_ge(*at(f"normed{layer}0", 3))
                norm_params(1)
                pool.wait_ge(*at(f"dispatch_ready{layer}", 1))
                pool.wait_ge(*at("stored", 96 if layer == 0 else 96 + 144))
                if layer == 0:
                    pool.wait_ge(*at("places_zeroed", 128))
                most = pool.value_load(COUNT[0:1, NE:NE + 1], min_val=0, max_val=TOK)
                with pool.If(most > 128):
                    for name in ("scattered", "rows_a_landed", "rows_b_landed", "gathered"):
                        pool.sem_inc(S(f"{name}{layer}"), PER_LAYER[name + "#"])
                with pool.Else():
                    for rank in range(2):
                        for t, (t0, n) in enumerate(TILES):
                            pool.indirect_dma_start(
                                out=places, out_offset=bass.IndirectOffsetOnAxis(ap=IDX[0:n, 3 * rank + t:3 * rank + t + 1], axis=0),
                                in_=X[0:n, t, :], in_offset=None, bounds_check=NE * 128 - 1)\
                                .then_inc(S(f"scattered{layer}"), 16)
                    pool.wait_ge(*at(f"scattered{layer}", 96))

                    def load_rows(e, par, first):
                        if not first:
                            pool.wait_ge(*at(f"xe_mm{layer}", e * 2 - 2))
                        big = pool.value_load(COUNT[0:1, bass.ds(e, 1)], min_val=0, max_val=TOK)
                        for rows, case in ((128, pool.If(big > 64)), (64, None)):
                            with case or pool.Else():
                                pool.dma_start(XR[0:rows, par, :], places[bass.ds(e * 128, rows), :])\
                                    .then_inc(S(f"rows_{'ab'[par]}_landed{layer}"), 16)
                        pool.nop()

                    load_rows(0, 0, True)
                    load_rows(1, 1, True)
                    with pool.Fori(1, NE // 2) as i:
                        load_rows(i * 2, 0, False)
                        load_rows(i * 2 + 1, 1, False)
                    for ab in "ab":
                        pool.wait_ge(*at(f"sp_y_{ab}_stored{layer}", 8 * NE + 16))
                    for rank in range(2):
                        for t, (t0, n) in enumerate(TILES):
                            pool.indirect_dma_start(
                                out=YG[0:n, rank, t, :], out_offset=None, in_=places,
                                in_offset=bass.IndirectOffsetOnAxis(ap=IDX[0:n, 3 * rank + t:3 * rank + t + 1], axis=0),
                                bounds_check=NE * 128 - 1).then_inc(S(f"gathered{layer}"), 16)
                pool.nop()
                pool.wait_ge(*at(f"normed{layer}1", 3))
                for t, (t0, n) in enumerate(TILES):
                    pool.dma_start(QKV[0:n, t, 0:PD],
                                   token_rows(p_prompt[layer, 0], p_sample[layer].rearrange("b q d -> (b q) d"), t))\
                        .then_inc(S(f"p_landed{layer}"), 16)
                pool.dma_start(GAIN, ple_gate_b[layer].partition_broadcast(P)).then_inc(S(f"gate_b_landed{layer}"), 16)
                if layer == 0:
                    a, n = CONST["newmask"]
                    pool.dma_start(C[:, a:a + n], spread_c).then_inc(S("spread_landed"), 16)
                    for t, (t0, n) in enumerate(TILES):
                        pool.wait_ge(*at("rotated1", t + 1))
                        for o_p, o_s, c0, c1 in ((nbk_p, nbk_s, OFF_K, OFF_V), (nbv_p, nbv_s, OFF_V, OFF_QI)):
                            pool.dma_start(token_rows(o_p[0, 0].rearrange("s h d -> s (h d)"),
                                                      o_s[0].rearrange("b q h d -> (b q) (h d)"), t),
                                           QKV[0:n, t, c0:c1]).then_inc(S("stored"), 16)
                        pool.dma_start(token_rows(nbi_p[0, 0], nbi_s[0].rearrange("b q d -> (b q) d"), t),
                                       QKV[0:n, t, OFF_KI:OFF_WI]).then_inc(S("stored"), 16)
            pool.wait_ge(*at("gated1", 6))
            for t, (t0, n) in enumerate(TILES):
                pool.dma_start(token_rows(y_p[0], y_s.rearrange("b q d -> (b q) d"), t), X[0:n, t, :])\
                    .then_inc(S("stored"), 16)
            pool.wait_ge(*at("stored", 16 * (6 + 9 + 3)))

        @block.tensor
        def _(pe):
            pe.wait_ge(*at("const_landed", 16))

            def transposed(tag, view, ready, tiles=(0, 1, 2)):
                for u in range(2 * len(tiles)):
                    t, half = tiles[u // 2], u % 2
                    n = TILES[t][1]
                    if half == 0:
                        ready(t)
                    if u >= 4:
                        pe.wait_ge(*at(tag + "_evac", u - 3))
                    for j in range(4):
                        ins = pe.transpose(PS[:, u % 4, j * 128:j * 128 + n], view(t, 4 * half + j)[0:n],
                                           ident[0:n, 0:n])
                    ins.then_inc(S(tag + "_mm"), 1)

            def stream_chunk(a, t, k, kd=KD):
                return a[:, t, :].rearrange("p (f k) -> p k f", k=kd)[:, k, :]

            def project(tag, items, widths, evac):
                u = 0
                for name, w in zip(items, widths):
                    n, s = item(name)
                    pe.wait_ge(landed[s], stream.landed[n])
                    wt = ring[:, s, 0:KD * w].rearrange("p (k n) -> p k n", k=KD)
                    for t, (t0, rows) in enumerate(TILES):
                        if u >= 4:
                            pe.wait_ge(*at(evac, u - 3))
                        for k in range(KD):
                            for p0, p1, c0, c1 in pieces(t, w):
                                ins = pe.matmul(PS[p0:p1, 4 + u % 4, 0:c1 - c0], XT[:, k, t0:t0 + rows],
                                                wt[:, k, c0:c1], start=(k == 0), stop=(k == KD - 1))
                        ins.then_inc(S(tag), 1)
                        u += 1

            def query_chunk(tag, m, c0):
                if m >= 2:
                    pe.wait_ge(*at(tag + "_evac", m - 1))
                for t in range(2):
                    ins = pe.transpose(PS[:, m % 2, 128 * t:128 * t + 128], QKV[:, t, c0:c0 + 128], ident)
                ins.then_inc(S(tag + "_mm"), 1)

            def prompt_scores(layer, u):
                m, qt = u // 2, u % 2
                if qt == 0:
                    pe.wait_ge(*at(f"pq{layer}_evac", m + 1))
                if u >= 2:
                    pe.wait_ge(*at(f"pmask{layer}", u - 1))
                kw = 128 * (qt + 1)
                kt = KT[:, m, :] if layer == 0 else KT[:, m // 2, :]
                for c in range(2):
                    ins = pe.matmul(PS[:, 2 + u % 2, c * 256:c * 256 + kw], QZ[:, m % 2, c, 128 * qt:128 * qt + 128],
                                    kt[:, 0:kw], start=True, stop=True)
                ins.then_inc(S(f"ps{layer}_mm"), 1)

            def prompt_turn(layer, u):
                qt = u % 2
                pe.wait_ge(*at(f"pw{layer}", u + 1))
                if u >= 2:
                    pe.wait_ge(*at(f"pat{layer}_evac", u - 1))
                for c in range(1 if layer == 0 else 2):
                    for kt in range(qt + 1):
                        ins = pe.transpose(PS[:, 4 + u % 2, (2 * c + kt) * 128:(2 * c + kt + 1) * 128],
                                           SM[:, u % 2, c * 256 + kt * 128:c * 256 + kt * 128 + 128], ident)
                ins.then_inc(S(f"pat{layer}_mm"), 1)

            def prompt_values(layer, u):
                m, qt = u // 2, u % 2
                pe.wait_ge(*at(f"pat{layer}_evac", u + 1))
                if u >= 2:
                    pe.wait_ge(*at(f"po{layer}", u - 1))
                for c in range(1 if layer == 0 else 2):
                    w = 128 if layer == 0 else 64
                    v0 = 2 * D + m * 128 if layer == 0 else OFF_V + (m // 2) * 64
                    for kt in range(qt + 1):
                        ins = pe.matmul(PS[:, 6 + u % 2, c * w:c * w + w],
                                        ATP[:, u % 2, c, kt * 128:kt * 128 + 128],
                                        QKV[:, kt, v0:v0 + w], start=(kt == 0), stop=(kt == qt))
                ins.then_inc(S(f"po{layer}_mm"), 1)

            def prompt_attention(layer):
                for m in range(2):
                    query_chunk(f"pq{layer}", m, m * 128)
                for u in range(16 + 2):
                    if u < 16:
                        prompt_scores(layer, u)
                        if u % 2 == 1 and u // 2 + 2 < 8:
                            query_chunk(f"pq{layer}", u // 2 + 2, (u // 2 + 2) * 128)
                    if 1 <= u <= 16:
                        prompt_turn(layer, u - 1)
                    if u >= 2:
                        prompt_values(layer, u - 2)

            transposed("xt0", lambda t, k: stream_chunk(X, t, k), lambda t: pe.wait_ge(*at(f"x_landed{t}", 16)))
            pe.wait_ge(*at("xt0_evac", 6))
            project("qkv_mm0", [("a_in", j) for j in range(6)], [512] * 6, "qkv_evac0")
            transposed("kt0", lambda t, k: QKV[:, t, D + 128 * k:D + 128 * k + 128],
                       lambda t: pe.wait_ge(*at("rotated0", t + 1)))
            pe.wait_ge(*at("kt0_evac", 6))
            for k in range(KD):
                ins = pe.transpose(PS[:, 0, k * NS:(k + 1) * NS], QKV[0:NS, 2, k * 128:(k + 1) * 128], ident[0:NS, 0:NS])
            ins.then_inc(S("qb0_mm"), 1)
            pe.wait_ge(*at("qb0", 4))
            pe.wait_ge(*at("qkv_evac0", 18))
            prompt_attention(0)
            pe.wait_ge(*at("po0", 16))

            def page_turn(b, j):
                pe.wait_ge(k_landed[j], b * 16 + 16)
                for half, evac in enumerate(("kt_evac_act", "kt_evac_dve")):
                    pe.wait_ge(*at(evac, b * 8 + (j + 1)))
                    for k in range(4):
                        ins = pe.transpose(PS[:, (2 * j + half) % 4, k * 128:(k + 1) * 128],
                                           kpage[:, j, (4 * half + k) * 128:(4 * half + k + 1) * 128], ident)
                    ins.then_inc(S("kt_page_mm"), 1)

            def page_scores(b, par, j):
                for evac in ("kt_evac_act", "kt_evac_dve"):
                    pe.wait_ge(*at(evac, b * 8 + (j + 3)))
                if j == 0:
                    pe.wait_ge(*at("qcur", b + 1))
                    pe.wait_ge(*at("exp_done", b + 1))
                for half in range(2):
                    for t in range(4):
                        h = 2 * t + half
                        ins = pe.matmul(PS[32 * t:32 * t + 32, 4 + j // 4, (j % 4) * 128:(j % 4) * 128 + 128],
                                        QCUR[:, par, h, :], KPG[:, j % 2, h, :], start=(half == 0), stop=(half == 1))
                ins.then_inc(S("score_mm"), 1)

            def batch_a(b, par, i):
                for j in range(NPAGE + 1):
                    if j < NPAGE:
                        page_turn(b, j)
                    if j >= 1:
                        page_scores(b, par, j - 1)
                pe.wait_ge(*at("o_evac", b + 1))
                for half in range(2):
                    for t in range(4):
                        h = 2 * t + half
                        ins = pe.matmul(PS[32 * t:32 * t + 32, 6, 0:NS], QCUR[:, par, h, :], KT[:, h, SEQ:TOK],
                                        start=(half == 0), stop=(half == 1))
                ins.then_inc(S("score_mm"), 1)
                pe.wait_ge(*at("fold_ready", b + 1))
                for u in range(3):
                    for j in range(4 * u, min(4 * u + 4, 9)):
                        keys = min(128, NK - 128 * j)
                        c0 = (j % 4) * 128
                        ins = pe.matmul(PS[0:keys, AT_BANK[u], c0:c0 + 128], PR[:, 128 * j:128 * j + keys],
                                        FOLD[:, par, :], start=True, stop=True)
                    ins.then_inc(S("at_mm"), 1)
                pe.wait_ge(v_landed[par], i * 128 + 128)
                for j in range(NPAGE + 1):
                    keys = min(128, NK - 128 * j)
                    if j in (0, 4):
                        pe.wait_ge(*at("at_evac", b * 3 + (1 if j == 0 else 3)))
                    for t in range(4):
                        v = vpage[:, par * NPAGE + j, 256 * t:256 * t + 256] if j < NPAGE else \
                            QKV[0:NS, 2, 2 * D + 256 * t:2 * D + 256 * t + 256]
                        ins = pe.matmul(PS[32 * t:32 * t + 32, 6, 256:512], AT[0:keys, j, 32 * t:32 * t + 32], v,
                                        start=(j == 0), stop=(j == NPAGE))
                ins.then_inc(S("pv_mm"), 1)

            pe.sem_inc(S("score_mm"), 1)
            with pe.Fori(0, DB // 2) as i:
                batch_a(i * 2, 0, i)
                batch_a(i * 2 + 1, 1, i)

            pe.wait_ge(*at("kt_evac_act", 8 * DB + 2))
            pe.wait_ge(*at("kt_evac_dve", 8 * DB + 2))
            pe.wait_ge(*at("or_normed", 1))
            transposed("po_t0", lambda t, k: QKV[:, t, 128 * k:128 * k + 128], lambda t: None, (0, 1))
            for u in range(4):
                for j in range(4):
                    ins = pe.transpose(PS[:, 4 + u, j * 128:j * 128 + 128],
                                       OR[:, (4 * u + j) * 128:(4 * u + j + 1) * 128], ident)
                ins.then_inc(S("so_t0_mm"), 1)
            pe.wait_ge(*at("po_t0_evac", 4))
            pe.wait_ge(*at("so_t0_evac", 8))
            project("out_mm0", [("a_out", j) for j in range(2)], [512] * 2, "out_evac0")

            def router(layer):
                pe.wait_ge(*at(f"out_evac{layer}", 6))
                transposed(f"xtr{layer}", lambda t, k: stream_chunk(X, t, k),
                           lambda t: pe.wait_ge(*at(f"normed{layer}0", t + 1)))
                pe.wait_ge(*at(f"xtr{layer}_evac", 6))
                pe.wait_ge(*at(f"router_landed{layer}", 16))
                for k in range(KD):
                    ins = pe.matmul(PS[0:NE, 4, 0:TOK], SMF[:, k * NE:(k + 1) * NE], XT[:, k, :],
                                    start=(k == 0), stop=(k == KD - 1))
                ins.then_inc(S(f"logit_mm{layer}"), 1)
                pe.wait_ge(*at(f"logit_evac{layer}", 1))
                for t, (t0, n) in enumerate(TILES):
                    ins = pe.transpose(PS[0:n, 5, t * NE:(t + 1) * NE], SMF[0:NE, 512 + t0:512 + t0 + n],
                                       ident[0:NE, 0:NE])
                ins.then_inc(S(f"logit_mm{layer}"), 1)

            def positions(layer):
                pe.wait_ge(*at(f"mask_ready{layer}", 1))
                for t in range(3):
                    for t2 in range(t + 1):
                        pe.matmul(PS[:, 3, t * NE:(t + 1) * NE], cst("before" if t2 == t else "ones"),
                                  G[:, 8, t2 * NE:(t2 + 1) * NE], start=(t2 == 0), stop=(t2 == t))
                for t in range(3):
                    ins = pe.matmul(PS[:, 3, 48:48 + NE], cst("ones"), G[:, 8, t * NE:(t + 1) * NE],
                                    start=(t == 0), stop=(t == 2))
                ins.then_inc(S(f"pos_mm{layer}"), 1)
                pe.wait_ge(*at(f"dispatch_ready{layer}", 1))

            def experts(layer):
                most = pe.value_load(COUNT[0:1, NE:NE + 1], min_val=0, max_val=TOK)
                with pe.If(most > 128):
                    for name in ("xe_mm", "sp_gate_up_mm", "sp_ht_mm", "sp_y_mm"):
                        pe.sem_inc(S(f"{name}{layer}"), PER_LAYER[name + "#"])
                    experts_dense(layer)
                with pe.Else():
                    for name in ("gate_up_mm", "ht_mm", "y_mm"):
                        pe.sem_inc(S(f"{name}{layer}"), PER_LAYER[name + "#"])
                    experts_sparse(layer)
                pe.nop()

            def experts_sparse(layer):
                n0 = stream.items[("moe", layer, 0, 0)]

                def slot_of(i, j):
                    s = (n0 + j) % SLOTS
                    pe.wait_ge(landed[s], i * 16 + stream.landed[n0 + j])
                    return ring[:, s, :]

                def expert(i, par, e, m):
                    pe.wait_ge(*at(f"rows_{'ab'[par]}_landed{layer}", i * 16 + 16))
                    for half in range(2):
                        for k in range(4):
                            ins = pe.transpose(PS[:, 4 + half, k * 128:k * 128 + 128],
                                               XR[:, par, :].rearrange("p (f k) -> p k f", k=KD)[:, 4 * half + k, :],
                                               ident)
                        ins.then_inc(S(f"xe_mm{layer}"), 1)
                    wg = slot_of(i, 3 * par).rearrange("p (k n) -> p k n", k=KD)
                    wu = slot_of(i, 3 * par + 1).rearrange("p (k n) -> p k n", k=KD)
                    p1 = 0 if m == 128 else 64
                    for k in range(KD):
                        if k % 4 == 0:
                            pe.wait_ge(*at(f"xe_evac{layer}", e * 2 + (k // 4 + 1)))
                        pe.matmul(PS[0:m, 0, :], XE[:, k, 0:m], wg[:, k, :], start=(k == 0), stop=(k == KD - 1))
                        ins = pe.matmul(PS[p1:p1 + m, 1, :], XE[:, k, 0:m], wu[:, k, :],
                                        start=(k == 0), stop=(k == KD - 1))
                    ins.then_inc(S(f"sp_gate_up_mm{layer}"), 1)
                    pe.wait_ge(*at(f"sp_hidden{layer}", e + 1))
                    for k in range(FK):
                        ins = pe.transpose(PS[:, 2, k * 128:k * 128 + 128],
                                           MH[:, 0, :].rearrange("p (f k) -> p k f", k=FK)[:, k, :], ident)
                    ins.then_inc(S(f"sp_ht_mm{layer}"), 1)
                    pe.sem_inc(S(f"experts_used{layer}"), 2)
                    wd = slot_of(i, 3 * par + 2).rearrange("p (k n) -> p k n", k=FK)
                    for name in ("sp_y_act", "sp_y_dve"):
                        pe.wait_ge(*at(f"{name}{layer}", e + 1))
                    pe.wait_ge(*at(f"sp_ht_evac{layer}", e + 1))
                    for k in range(FK):
                        for half in range(2):
                            ins = pe.matmul(PS[p1 * half:p1 * half + m, 6 + half, :], MHT[:, 0, k, 0:m],
                                            wd[:, k, 512 * half:512 * half + 512], start=(k == 0), stop=(k == FK - 1))
                    ins.then_inc(S(f"sp_y_mm{layer}"), 1)
                    pe.wait_ge(*at(f"sp_y_mm{layer}", e + 1))
                    pe.sem_inc(S(f"experts_used{layer}"), 1)

                with pe.Fori(0, NE // 2) as i:
                    for par in range(2):
                        e = i * 2 + par
                        big = pe.value_load(COUNT[0:1, bass.ds(e, 1)], min_val=0, max_val=TOK)
                        with pe.If(big > 64):
                            expert(i, par, e, 128)
                        with pe.Else():
                            expert(i, par, e, 64)
                        pe.nop()

            def experts_dense(layer):
                n0 = stream.items[("moe", layer, 0, 0)]

                def slot_of(i, j):
                    s = (n0 + j) % SLOTS
                    pe.wait_ge(landed[s], i * 16 + stream.landed[n0 + j])
                    return ring[:, s, :]

                def gate_up(i, u):
                    t, b0 = u % 3, 2 * (u % 2)
                    t0, n = TILES[t]
                    wg = slot_of(i, u // 3 * 3).rearrange("p (k n) -> p k n", k=KD)
                    wu = slot_of(i, u // 3 * 3 + 1).rearrange("p (k n) -> p k n", k=KD)
                    pe.wait_ge(*at(f"h_ready{layer}", i * 6 + (u + 1)))
                    for k in range(KD):
                        pe.matmul(PS[0:n, b0, :], XT[:, k, t0:t0 + n], wg[:, k, :], start=(k == 0), stop=(k == KD - 1))
                        p0 = 0 if t < 2 else NS
                        ins = pe.matmul(PS[p0:p0 + n, b0 + 1, :], XT[:, k, t0:t0 + n], wu[:, k, :],
                                        start=(k == 0), stop=(k == KD - 1))
                    ins.then_inc(S(f"gate_up_mm{layer}"), 1)

                def down(i, u):
                    t = u % 3
                    n = TILES[t][1]
                    pe.wait_ge(*at(f"h_ready{layer}", i * 6 + (u + 3)))
                    if t == 2:
                        pe.sem_inc(S(f"experts_used{layer}"), 2)
                    pe.wait_ge(*at(f"ht_evac{layer}", i * 6 + (u + 1)))
                    for k in range(FK):
                        ins = pe.transpose(PS[:, 4 + u % 2, k * 128:k * 128 + 128],
                                           MH[:, u % 2, :].rearrange("p (f k) -> p k f", k=FK)[:, k, :], ident)
                    ins.then_inc(S(f"ht_mm{layer}"), 1)
                    wd = slot_of(i, u // 3 * 3 + 2).rearrange("p (k n) -> p k n", k=FK)
                    pe.wait_ge(*at(f"ht_evac{layer}", i * 6 + (u + 3)))
                    pe.wait_ge(*at(f"y_used{layer}", i * 6 + (u + 1)))
                    for k in range(FK):
                        for half in range(2):
                            p0 = 0 if t < 2 or half == 0 else NS
                            ins = pe.matmul(PS[p0:p0 + n, 6 + half, :], MHT[:, u % 2, k, 0:n],
                                            wd[:, k, 512 * half:512 * half + 512], start=(k == 0), stop=(k == FK - 1))
                    ins.then_inc(S(f"y_mm{layer}"), 1)
                    if t == 2:
                        pe.wait_ge(*at(f"y_mm{layer}", i * 6 + (u + 1)))
                        pe.sem_inc(S(f"experts_used{layer}"), 1)

                with pe.Fori(0, NE // 2) as i:
                    for u in range(7):
                        if u < 6:
                            gate_up(i, u)
                        if u >= 1:
                            down(i, u - 1)

            def gated_input(layer):
                pe.wait_ge(*at(f"p_landed{layer}", 48))
                for t, (t0, n) in enumerate(TILES):
                    for k in range(2):
                        ins = pe.transpose(PS[:, 4 + k, t0:t0 + n], stream_chunk(QKV[:, :, 0:PD], t, k, 2)[0:n],
                                           ident[0:n, 0:n])
                ins.then_inc(S(f"pt_mm{layer}"), 1)
                transposed(f"xtg{layer}", lambda t, k: stream_chunk(X, t, k),
                           lambda t: pe.wait_ge(*at(f"normed{layer}1", t + 1)))
                pe.wait_ge(*at(f"xtg{layer}_evac", 6))
                pe.wait_ge(*at(f"pt_evac{layer}", 1))
                n, s = item(("ple_p", layer))
                wp = ring[:, s, 0:2048].rearrange("p (k n) -> p k n", k=2)
                for u in range(6):
                    j, t = u // 3, u % 3
                    t0, rows = TILES[t]
                    if t == 0:
                        ng, sg = item(("ple_g", layer, j))
                        pe.wait_ge(landed[sg], stream.landed[ng])
                        wg = ring[:, sg, :].rearrange("p (k n) -> p k n", k=KD)
                    if u >= 2:
                        pe.wait_ge(*at(f"gated{layer}", u - 1))
                    for k in range(KD):
                        for p0, p1, c0, c1 in pieces(t, 512):
                            pe.matmul(PS[p0:p1, 2 * (u % 2), 0:c1 - c0], XT[:, k, t0:t0 + rows], wg[:, k, c0:c1],
                                      start=(k == 0), stop=(k == KD - 1))
                    pe.wait_ge(landed[s], stream.landed[n])
                    for k in range(2):
                        for p0, p1, c0, c1 in pieces(t, 512):
                            ins = pe.matmul(PS[p0:p1, 2 * (u % 2) + 1, 0:c1 - c0], PT[:, k, t0:t0 + rows],
                                            wp[:, k, 512 * j + c0:512 * j + c1], start=(k == 0), stop=(k == 1))
                    ins.then_inc(S(f"ple_mm{layer}"), 1)

            router(0)
            positions(0)
            experts(0)
            gated_input(0)

            transposed("xt1", lambda t, k: stream_chunk(X, t, k), lambda t: pe.wait_ge(*at("gated0", 6)))
            pe.wait_ge(*at("xt1_evac", 6))
            project("qkv_mm1", [("b_in", j) for j in range(5)], [512] * 4 + [B_IN - 2048], "qkv_evac1")
            pe.wait_ge(*at("qkv_evac1", 15))
            for t, (t0, n) in enumerate(TILES):
                pe.wait_ge(*at("doubled", t + 1))
                for g in range(KVB):
                    ins = pe.transpose(PS[:, t, g * 128:g * 128 + n],
                                       QKV[0:n, t, DUP_K + g * 128:DUP_K + g * 128 + 128], ident[0:n, 0:n])
                ins.then_inc(S("bt_mm"), 1)
            for t, (t0, n) in enumerate(TILES):
                ins = pe.transpose(PS[:, 3, t0:t0 + n], QKV[0:n, t, DUP_I:DUP_I + 128], ident[0:n, 0:n])
            ins.then_inc(S("bt_mm"), 1)
            for bank, c0, n in ((4, OFF_K, 2), (5, 0, 8), (6, OFF_QI, 4)):
                for k in range(n):
                    ins = pe.transpose(PS[:, bank, k * NS:(k + 1) * NS],
                                       QKV[0:NS, 2, c0 + 128 * k:c0 + 128 * k + 128], ident[0:NS, 0:NS])
                ins.then_inc(S("bt_mm"), 1)
            pe.wait_ge(*at("ws_rows", 4))
            for u in range(4):
                ins = pe.transpose(PS[:, 7, u * NS:(u + 1) * NS], AT[0:NS, u, :], ident[0:NS, 0:NS])
            ins.then_inc(S("bt_mm"), 1)
            pe.wait_ge(*at("bt_evac_act", 6))
            pe.wait_ge(*at("bt_evac_dve", 12))

            for m in range(2):
                query_chunk("pi", m, OFF_QI + m * 128)
            for u in range(8):
                m, qt = u // 2, u % 2
                if qt == 0:
                    pe.wait_ge(*at("pi_evac", m + 1))
                if u >= 2:
                    pe.wait_ge(*at("pi_relu", u - 1))
                for c in range(2):
                    ins = pe.matmul(PS[:, 2 + u % 2, c * 256:c * 256 + 256],
                                    QZ[:, m % 2, c, 128 * qt:128 * qt + 128], KT[:, 4, 0:256], start=True, stop=True)
                ins.then_inc(S("pis_mm"), 1)
                if qt == 1 and m + 2 < 4:
                    query_chunk("pi", m + 2, OFF_QI + (m + 2) * 128)
            pe.wait_ge(*at("pi_relu", 8))

            n, s = item("kidx")
            pe.wait_ge(landed[s], stream.landed[n])
            kx = ring[:, s, :].rearrange("p (r j e) -> p r j e", r=4, j=NPAGE)

            def kidx_turn(r):
                for half in range(2):
                    v = 2 * r + half
                    if v >= 2:
                        pe.wait_ge(*at("kidx_evac", v - 1))
                    for j in range(4):
                        ins = pe.transpose(PS[:, half, j * 128:j * 128 + 128], kx[:, r, 4 * half + j, :], ident)
                    ins.then_inc(S("kidx_mm"), 1)

            def kidx_scores(r):
                pe.wait_ge(*at("kidx_evac", 2 * r + 2))
                if r >= 1:
                    pe.wait_ge(*at("si_relu", r))
                for half in range(2):
                    pe.matmul(PS[:, 2 + half, :], QIB[:, r, :], KIT[:, r % 2, 512 * half:512 * half + 512],
                              start=True, stop=True)
                pe.matmul(PS[:, 4, 0:NS], QIB[:, r, :], KT[:, 4, SEQ:TOK], start=True, stop=True)\
                    .then_inc(S("sis_mm"), 1)

            def kidx_sum(r):
                pe.wait_ge(*at("si_relu", r + 1))
                for p0, bank, w, c0 in ((0, 5, 512, 0), (NS, 5, 512, 512), (0, 6, NS, PAST)):
                    ins = pe.matmul(PS[p0:p0 + NS, bank, 0:w], WS[:, r, :], PR[:, c0:c0 + w],
                                    start=(r == 0), stop=(r == 3))
                ins.then_inc(S("si_sum_mm"), 1)

            kidx_turn(0)
            for r in range(4):
                kidx_scores(r)
                if r < 3:
                    kidx_turn(r + 1)
                kidx_sum(r)

            pe.wait_ge(*at("kidx_evac", 8))
            pe.wait_ge(*at("si_taken", 3))
            prompt_attention(1)
            pe.wait_ge(*at("po1", 16))

            def batch_b(b):
                r, bb = b // 2, b % 2
                n, s = item(("kb", r))
                nv, sv = item(("vb", r))
                if bb == 0:
                    pe.wait_ge(landed[s], stream.landed[n])
                kb = ring[:, s, :].rearrange("p (b j n) -> p b j n", b=2, j=NPAGE)
                vb = ring[:, sv, :].rearrange("p (b j n) -> p b j n", b=2, j=NPAGE)
                for v in range(4):
                    if b >= 1:
                        pe.wait_ge(*at("kbt_evac", 4 * (b - 1) + v + 1))
                    for c in range(2):
                        for j in range(2):
                            ins = pe.transpose(PS[:, v, c * 256 + j * 128:c * 256 + j * 128 + 128],
                                               kb[:, bb, 2 * v + j, c * 128:c * 128 + 128], ident)
                    ins.then_inc(S("kbt_mm"), 1)
                if b == 0:
                    pe.wait_ge(*at("selection", 1))
                if b >= 1:
                    pe.wait_ge(*at("expb_done", b))
                for half in range(2):
                    pe.wait_ge(*at("kbt_evac", 4 * b + 2 * half + 2))
                    for c in range(2):
                        pe.matmul(PS[64 * c:64 * c + 64, 4 + half, :], QBB[:, b, c, :],
                                  KBT[:, c, 512 * half:512 * half + 512], start=True, stop=False)
                    for c in range(2):
                        pe.matmul(PS[64 * c:64 * c + 64, 4 + half, :], spread[:, b, :],
                                  SELB[:, 512 * half:512 * half + 512], start=False, stop=True)
                if b >= 1:
                    pe.wait_ge(*at("ob", 4 * b))
                for c in range(2):
                    pe.matmul(PS[64 * c:64 * c + 64, 6, 0:NS], QBB[:, b, c, :], KT[:, 5 + c, 0:NS], start=True, stop=False)
                for c in range(2):
                    ins = pe.matmul(PS[64 * c:64 * c + 64, 6, 0:NS], spread[:, b, :], SELB[:, PAST:NK],
                                    start=False, stop=True)
                ins.then_inc(S("sb_mm"), 1)
                pe.wait_ge(*at("expb_done", b + 1))
                for u in range(3):
                    for j in range(4 * u, min(4 * u + 4, 9)):
                        keys = min(128, NK - 128 * j)
                        c0 = (j % 4) * 128
                        ins = pe.transpose(PS[0:keys, AT_BANK[u], c0:c0 + 128], PR[:, 128 * j:128 * j + keys], ident)
                    ins.then_inc(S("bat_mm"), 1)
                if bb == 0:
                    pe.wait_ge(landed[sv], stream.landed[nv])
                for j in range(NPAGE + 1):
                    keys = min(128, NK - 128 * j)
                    if j % 4 == 0:
                        pe.wait_ge(*at("bat_evac", b * 3 + (j // 4 + 1)))
                    for c in range(2):
                        v = vb[:, bb, j, c * 128:c * 128 + 128] if j < NPAGE else \
                            QKV[0:NS, 2, OFF_V + c * 128:OFF_V + c * 128 + 128]
                        ins = pe.matmul(PS[64 * c:64 * c + 64, 6, 256:384], AT[0:keys, j, 64 * c:64 * c + 64], v,
                                        start=(j == 0), stop=(j == NPAGE))
                ins.then_inc(S("pvb_mm"), 1)

            for b in range(DB):
                batch_b(b)

            pe.wait_ge(*at("kbt_evac", 4 * DB))
            transposed("po_t1", lambda t, k: QKV[:, t, 128 * k:128 * k + 128], lambda t: None, (0, 1))
            pe.wait_ge(*at("ob", 4 * DB))
            for u in range(2):
                for j in range(4):
                    ins = pe.transpose(PS[:, 4 + u, j * 128:j * 128 + 128],
                                       SMF[:, (4 * u + j) * 128:(4 * u + j + 1) * 128], ident)
                ins.then_inc(S("so_t1_mm"), 1)
            pe.wait_ge(*at("po_t1_evac", 4))
            pe.wait_ge(*at("so_t1_evac", 4))
            project("out_mm1", [("b_out", j) for j in range(2)], [512] * 2, "out_evac1")
            router(1)
            positions(1)
            experts(1)
            gated_input(1)

        @block.scalar
        def _(act):
            def copy(dst, src, sem=None, scale=None):
                ins = act.activation(dst, src, ACT.Copy) if scale is None else \
                    act.activation(dst, src, ACT.Copy, scale=scale)
                if sem is not None:
                    ins.then_inc(S(sem), 1)

            def copy_transposed(tag, dst, tiles=(0, 1, 2), scale=None):
                for u in range(2 * len(tiles)):
                    t, half = tiles[u // 2], u % 2
                    t0, n = TILES[t]
                    act.wait_ge(*at(tag + "_mm", u + 1))
                    copy(dst[:, 4 * half:4 * half + 4, t0:t0 + n],
                         PS[:, u % 4, :].rearrange("p (j c) -> p j c", j=4)[:, :, 0:n], tag + "_evac", scale)

            def copy_projection(tag, evac, widths):
                u = 0
                for j, w in enumerate(widths):
                    for t in range(3):
                        act.wait_ge(*at(tag, u + 1))
                        for n, (p0, p1, c0, c1) in enumerate(pieces(t, w)):
                            last = n == len(pieces(t, w)) - 1
                            copy(QKV[0:p1 - p0, t, 512 * j + c0:512 * j + c1], PS[p0:p1, 4 + u % 4, 0:c1 - c0],
                                 evac if last else None)
                        u += 1

            def copy_query_chunk(tag, m):
                act.wait_ge(*at(tag + "_mm", m + 1))
                if m == 0:
                    act.wait_ge(*at(tag + "_zero", 1))
                for c in range(2):
                    copy(QZ[64 * c:64 * c + 64, m % 2, c, :], PS[64 * c:64 * c + 64, m % 2, 0:256],
                         tag + "_evac" if c else None)

            def prompt_attention(layer):
                for m in range(2):
                    copy_query_chunk(f"pq{layer}", m)
                for u in range(17):
                    if u < 16:
                        kw = 128 * (u % 2 + 1)
                        act.wait_ge(*at(f"pmax{layer}", u + 1))
                        for c in range(2):
                            ins = act.activation(SM[:, u % 2, c * 256:c * 256 + kw], SM[:, u % 2, c * 256:c * 256 + kw],
                                                 ACT.Exp, bias=NMAX[:, 2 * (u % 2) + c:2 * (u % 2) + c + 1],
                                                 accum_out=SUMS[:, 2 * (u % 2) + c:2 * (u % 2) + c + 1])
                        ins.then_inc(S(f"pexp{layer}"), 1)
                        if u % 2 == 1 and u // 2 + 2 < 8:
                            copy_query_chunk(f"pq{layer}", u // 2 + 2)
                    if u >= 1:
                        v = u - 1
                        act.wait_ge(*at(f"pat{layer}_mm", v + 1))
                        kw = 128 * (v % 2 + 1)
                        if layer == 0:
                            copy(ATP[:, v % 2, 0, 0:kw], PS[:, 4 + v % 2, 0:kw], "pat0_evac")
                        else:
                            copy(ATP[:, v % 2, :, 0:kw],
                                 PS[:, 4 + v % 2, :].rearrange("p (c k) -> p c k", c=2)[:, :, 0:kw], "pat1_evac")

            copy_transposed("xt0", XT)
            copy_projection("qkv_mm0", "qkv_evac0", [512] * 6)
            copy_transposed("kt0", KT)
            act.wait_ge(*at("lam_sums", 1))
            act.activation(small[:, 4:6], small[:, 3:5] if False else small[:, 6:8], ACT.Exp).then_inc(S("lam_exp"), 1)
            prompt_attention(0)

            def batch_a(b, par):
                for j in range(NPAGE):
                    act.wait_ge(*at("kt_page_mm", b * 16 + (2 * j + 1)))
                    act.wait_ge(*at("score_mm", b * 9 + (max(j - 1, 0) + 1)))
                    copy(KPG[:, j % 2, 0:4, :], PS[:, (2 * j) % 4, :].rearrange("p (k n) -> p k n", k=4), "kt_evac_act")
                act.wait_ge(*at("row_max", b + 1))
                act.activation(PR[:, :], PSF[:, 2048:2048 + NK], ACT.Exp, bias=NMAX[:, par:par + 1], scale=SCALE,
                               accum_out=SUMS[:, par:par + 1]).then_inc(S("exp_done"), 1)
                for u in range(3):
                    act.wait_ge(*at("at_mm", b * 3 + (u + 1)))
                    keys, m = (128, 4) if u < 2 else (NS, 1)
                    copy(AT[0:keys, 4 * u:4 * u + m, :],
                         PS[0:keys, AT_BANK[u], 0:128 * m].rearrange("p (j r) -> p j r", j=m),
                         "at_evac")

            act.wait_ge(*at("po0_mm", 16))
            act.sem_inc(S("kt_evac_act"), 2)
            act.sem_inc(S("exp_done"), 1)
            with act.Fori(0, DB // 2) as i:
                batch_a(i * 2, 0)
                batch_a(i * 2 + 1, 1)
            act.wait_ge(*at("o_squares", 2))
            act.activation(RMS[:, 0:32], RMS[:, 0:32], ACT.Sqrt, bias=cst("eps"), scale=1.0 / 128)\
               .then_inc(S("o_root"), 1)
            copy_transposed("po_t0", XT, (0, 1), small[:, 5 - 5 + 3:4])
            for u in range(4):
                act.wait_ge(*at("so_t0_mm", u + 1))
                for hp in range(2):
                    src = PS[:, 4 + u, :].rearrange("p (b c t r) -> p b c t r", b=2, c=2, t=4)[:, :, hp, :, 8 * hp:8 * hp + 8]
                    dst = XT[:, hp::2, SEQ + 16 * u:SEQ + 16 * u + 16].rearrange("p t (b q) -> p b t q", b=2)
                    copy(dst, src, "so_t0_evac", small[:, 3:4])

            def norm_root(layer, which):
                act.wait_ge(*at(f"var{layer}{which}", 1))
                act.activation(RSTD, MV[:, :, 1], ACT.Sqrt, bias=cst("eps"), scale=1.0).then_inc(S(f"std{layer}{which}"), 1)

            def experts(layer):
                copy_transposed(f"xtr{layer}", XT)
                act.wait_ge(*at(f"logit_mm{layer}", 1))
                copy(SMF[0:NE, 512:512 + TOK], PS[0:NE, 4, 0:TOK], f"logit_evac{layer}")
                act.wait_ge(*at(f"logit_mm{layer}", 2))
                act.wait_ge(*at(f"aff_ones{layer}", 1))
                act.activation(G[:, 0, 0:32], PS[:, 5, 0:32], ACT.Sigmoid)
                act.activation(G[0:NS, 0, 32:48], PS[0:NS, 5, 32:48], ACT.Sigmoid).then_inc(S(f"aff{layer}"), 1)
                act.wait_ge(*at(f"dispatch_ready{layer}", 1))
                most = act.value_load(COUNT[0:1, NE:NE + 1], min_val=0, max_val=TOK)
                with act.If(most > 128):
                    for name in ("xe_evac", "sp_sig", "sp_ht_evac", "sp_y_act", "sp_y_a_stored", "sp_y_b_stored"):
                        act.sem_inc(S(f"{name}{layer}"), PER_LAYER[name + "#"])
                    experts_dense(layer)
                with act.Else():
                    for name in ("ht_evac", "sig"):
                        act.sem_inc(S(f"{name}{layer}"), PER_LAYER[name + "#"])
                    experts_sparse(layer)
                act.nop()

            def experts_sparse(layer):
                def expert(i, par, e, m):
                    for half in range(2):
                        act.wait_ge(*at(f"xe_mm{layer}", e * 2 + (half + 1)))
                        if half == 0:
                            act.wait_ge(*at(f"sp_gate_up_mm{layer}", e))
                        copy(XE[:, 4 * half:4 * half + 4, 0:m],
                             PS[:, 4 + half, :].rearrange("p (k c) -> p k c", k=4)[:, :, 0:m], f"xe_evac{layer}")
                    act.wait_ge(*at(f"sp_gate_up_mm{layer}", e + 1))
                    act.activation(MSG[0:m, 0, :], PS[0:m, 0, :], ACT.Sigmoid).then_inc(S(f"sp_sig{layer}"), 1)
                    act.wait_ge(*at(f"sp_ht_mm{layer}", e + 1))
                    copy(MHT[:, 0, :, 0:m], PS[:, 2, :].rearrange("p (k c) -> p k c", k=FK)[:, :, 0:m],
                         f"sp_ht_evac{layer}")
                    act.wait_ge(*at(f"sp_y_mm{layer}", e + 1))
                    act.wait_ge(*at(f"sp_y_{'ab'[par]}_stored{layer}", i * 16 + 16))
                    copy(YS[par][0:m, 0:512], PS[0:m, 6, :], f"sp_y_act{layer}")
                    act.wait_ge(*at(f"sp_y_act{layer}", e + 2))
                    act.wait_ge(*at(f"sp_y_dve{layer}", e + 2))
                    act.dma_start(places[bass.ds(e * 128, m), :], YS[par][0:m, :])\
                       .then_inc(S(f"sp_y_{'ab'[par]}_stored{layer}"), 16)

                act.sem_inc(S(f"sp_y_act{layer}"), 1)
                for ab in "ab":
                    act.sem_inc(S(f"sp_y_{ab}_stored{layer}"), 16)
                with act.Fori(0, NE // 2) as i:
                    for par in range(2):
                        e = i * 2 + par
                        big = act.value_load(COUNT[0:1, bass.ds(e, 1)], min_val=0, max_val=TOK)
                        with act.If(big > 64):
                            expert(i, par, e, 128)
                        with act.Else():
                            expert(i, par, e, 64)
                        act.nop()

            def experts_dense(layer):
                act.wait_ge(*at(f"acc_zero{layer}", 1))
                act.sem_inc(S(f"ht_evac{layer}"), 2)
                with act.Fori(0, NE // 2) as i:
                    for u in range(7):
                        if u < 6:
                            n = TILES[u % 3][1]
                            act.wait_ge(*at(f"gate_up_mm{layer}", i * 6 + (u + 1)))
                            act.activation(MSG[0:n, u % 2, :], PS[0:n, 2 * (u % 2), :], ACT.Sigmoid)\
                               .then_inc(S(f"sig{layer}"), 1)
                        if u >= 1:
                            v = u - 1
                            n = TILES[v % 3][1]
                            act.wait_ge(*at(f"ht_mm{layer}", i * 6 + (v + 1)))
                            copy(MHT[:, v % 2, :, 0:n], PS[:, 4 + v % 2, :].rearrange("p (k c) -> p k c", k=FK)[:, :, 0:n],
                                 f"ht_evac{layer}")

            def gated_input(layer):
                act.wait_ge(*at(f"pt_mm{layer}", 1))
                copy(PT, PS[:, 4:6, 0:TOK], f"pt_evac{layer}")
                copy_transposed(f"xtg{layer}", XT)
                for u in range(6):
                    n = TILES[u % 3][1]
                    act.wait_ge(*at(f"gate_biased{layer}", u + 1))
                    act.activation(MSG[0:n, u % 2, :], MSG[0:n, u % 2, :], ACT.Sigmoid).then_inc(S(f"gate_sig{layer}"), 1)

            norm_root(0, 0)
            experts(0)
            norm_root(0, 1)
            gated_input(0)

            copy_transposed("xt1", XT)
            copy_projection("qkv_mm1", "qkv_evac1", [512] * 4 + [B_IN - 2048])
            for t, (t0, n) in enumerate(TILES):
                act.wait_ge(*at("bt_mm", t + 1))
                copy(KT[:, 0:4, t0:t0 + n], PS[:, t, :].rearrange("p (g c) -> p g c", g=4)[:, :, 0:n], "bt_evac_act")
            act.wait_ge(*at("bt_mm", 4))
            copy(KT[:, 4, :], PS[:, 3, 0:TOK], "bt_evac_act")
            act.wait_ge(*at("bt_mm", 5))
            copy(KT[:, 5:7, 0:NS], PS[:, 4, 0:2 * NS].rearrange("p (c n) -> p c n", c=2), "bt_evac_act")
            act.wait_ge(*at("bt_mm", 8))
            act.wait_ge(*at("bt_evac_dve", 12))
            copy(WS, PS[:, 7, 0:4 * NS].rearrange("p (u n) -> p u n", u=4), "bt_evac_act")
            for m in range(2):
                copy_query_chunk("pi", m)
            for u in range(8):
                act.wait_ge(*at("pis_mm", u + 1))
                if u >= 2:
                    act.wait_ge(*at("pi_added", u - 1))
                act.activation(SM[:, u % 2, :], PS[:, 2 + u % 2, :], ACT.Relu).then_inc(S("pi_relu"), 1)
                if u % 2 == 1 and u // 2 + 2 < 4:
                    copy_query_chunk("pi", u // 2 + 2)
            for r in range(4):
                for half in range(2):
                    act.wait_ge(*at("kidx_mm", 2 * r + half + 1))
                    if r >= 2 and half == 0:
                        act.wait_ge(*at("sis_mm", r - 1))
                    copy(KIT[:, r % 2, 512 * half:512 * half + 512], PS[:, half, :], "kidx_evac")
                act.wait_ge(*at("sis_mm", r + 1))
                if r >= 1:
                    act.wait_ge(*at("si_sum_mm", r))
                act.activation(PR[:, :], PSF[:, 1024:1024 + NK], ACT.Relu).then_inc(S("si_relu"), 1)
            prompt_attention(1)
            for b in range(DB):
                for v in range(4):
                    act.wait_ge(*at("kbt_mm", 4 * b + v + 1))
                    if b >= 1 and v == 0:
                        act.wait_ge(*at("sb_mm", b))
                    copy(KBT[:, :, 256 * v:256 * v + 256], PS[:, v, :].rearrange("p (c n) -> p c n", c=2), "kbt_evac")
                act.wait_ge(*at("row_maxb", b + 1))
                act.activation(PR[:, :], PSF[:, 2048:2048 + NK], ACT.Exp, bias=NMAX[:, b % 2:b % 2 + 1], scale=SCALE,
                               accum_out=SUMS[:, b % 2:b % 2 + 1]).then_inc(S("expb_done"), 1)
                for u in range(3):
                    act.wait_ge(*at("bat_mm", b * 3 + u + 1))
                    keys, m = (128, 4) if u < 2 else (NS, 1)
                    copy(AT[0:keys, 4 * u:4 * u + m, :],
                         PS[0:keys, AT_BANK[u], 0:128 * m].rearrange("p (j r) -> p j r", j=m),
                         "bat_evac")
            copy_transposed("po_t1", XT, (0, 1))
            for u in range(2):
                act.wait_ge(*at("so_t1_mm", u + 1))
                for hp in range(2):
                    src = PS[64 * hp:64 * hp + 64, 4 + u, :].rearrange("p (b h c q) -> p b h c q", b=4, h=8, c=2)[:, :, :, hp, :]
                    for bb in range(4):
                        b = 4 * u + bb
                        copy(XT[64 * hp:64 * hp + 64, :, SEQ + 8 * b:SEQ + 8 * b + 8], src[:, bb],
                             "so_t1_evac" if bb == 3 else None)
            norm_root(1, 0)
            experts(1)
            norm_root(1, 1)
            gated_input(1)

        @block.vector
        def _(ve):
            chain = {"name": "vector_chain", "n": 0, "i": None, "per": 0}

            def link(ins):
                chain["n"] += 1
                ins.then_inc(S(chain["name"]), 1)
                ve.wait_ge(*at(chain["name"], chain["n"] if chain["i"] is None else
                               chain["i"] * chain["per"] + chain["n"]))

            def loop(i, per):
                chain.update(i=i, per=per, start=chain["n"])

            def loop_end(count):
                assert chain["n"] - chain["start"] == chain["per"], chain
                chain["n"] = chain["start"] + count * chain["per"]
                chain["i"] = None

            def rotate(t, c0, heads, half, cos, sin, tag):
                n = TILES[t][1]
                rot = 2 * half
                x = QKV[0:n, t, c0:c0 + heads * HD].rearrange("p (h d) -> p h d", h=heads)
                x4 = x[:, :, 0:rot].rearrange("p h (u f) -> p h u f", u=2)
                cs = cst(cos)[0:n, t * half:(t + 1) * half].unsqueeze(1).unsqueeze(1).to_broadcast([n, heads, 2, half])
                sn = cst(sin)[0:n, t * half:(t + 1) * half].unsqueeze(1).to_broadcast([n, heads, half])
                t1 = PR[0:n, 0:heads * rot].rearrange("p (h u f) -> p h u f", h=heads, u=2)
                t2 = PR[0:n, 512:512 + heads * rot].rearrange("p (h u f) -> p h u f", h=heads, u=2)
                ve.tensor_tensor(t2[:, :, 0, :], x4[:, :, 1, :], sn, ALU.mult)
                ve.tensor_tensor(t2[:, :, 1, :], x4[:, :, 0, :], sn, ALU.mult)
                link(ve.tensor_tensor(t1, x4, cs, ALU.mult))
                ve.tensor_tensor(x4[:, :, 0, :], t1[:, :, 0, :], t2[:, :, 0, :], ALU.subtract)
                ins = ve.tensor_tensor(x4[:, :, 1, :], t1[:, :, 1, :], t2[:, :, 1, :], ALU.add)
                if tag:
                    ins.then_inc(S(tag), 1)
                else:
                    link(ins)

            def prompt_attention(layer):
                po_w = 128 if layer == 0 else 64

                def scores(u):
                    qt = u % 2
                    kw = 128 * (qt + 1)
                    ve.wait_ge(*at(f"ps{layer}_mm", u + 1))
                    if u >= 2:
                        ve.wait_ge(*at(f"pat{layer}_mm", u - 1))
                    s3 = PS[:, 2 + u % 2, :].rearrange("p (c k) -> p c k", c=2)[:, :, 0:kw]
                    m3 = SM[:, u % 2, :].rearrange("p (c k) -> p c k", c=2)[:, :, 0:kw]
                    bias = (causal if layer == 0 else PB)[:, qt, 0:kw].unsqueeze(1).to_broadcast([P, 2, kw])
                    ve.scalar_tensor_tensor(m3, s3, SCALE, bias, ALU.mult, ALU.add).then_inc(S(f"pmask{layer}"), 1)
                    ve.wait_ge(*at(f"pmask{layer}", u + 1))
                    ve.tensor_reduce(NMAX[:, 2 * (u % 2):2 * (u % 2) + 2], m3, AX.X, ALU.max, negate=True)\
                      .then_inc(S(f"pmax{layer}"), 1)

                def weights(u):
                    kw = 128 * (u % 2 + 1)
                    ve.wait_ge(*at(f"pexp{layer}", u + 1))
                    rc = RC[:, 2 * (u % 2):2 * (u % 2) + 2]
                    link(ve.reciprocal(rc, SUMS[:, 2 * (u % 2):2 * (u % 2) + 2]))
                    p0, p1 = SM[:, u % 2, 0:kw], SM[:, u % 2, 256:256 + kw]
                    if layer == 0:
                        link(ve.tensor_tensor(rc[:, 1:2], rc[:, 1:2], NLAM, ALU.mult))
                        link(ve.tensor_scalar(p0, p0, rc[:, 0:1], None, ALU.mult))
                        ve.scalar_tensor_tensor(p0, p1, rc[:, 1:2], p0, ALU.mult, ALU.add).then_inc(S("pw0"), 1)
                    else:
                        ve.tensor_scalar(p0, p0, rc[:, 0:1], None, ALU.mult)
                        ve.tensor_scalar(p1, p1, rc[:, 1:2], None, ALU.mult).then_inc(S("pw1"), 1)

                def outputs(u):
                    m, qt = u // 2, u % 2
                    ve.wait_ge(*at(f"po{layer}_mm", u + 1))
                    ve.tensor_copy(QKV[:, qt, 128 * m:128 * m + 128], PS[:, 6 + u % 2, 0:128]).then_inc(S(f"po{layer}"), 1)

                for u in range(18):
                    if u < 16:
                        scores(u)
                        weights(u)
                    if u >= 2:
                        outputs(u - 2)

            ve.memset(small[:, 8:160], 1.0).then_inc(S("small_set"), 1)
            ve.memset(QB[:, :], 0.0).then_inc(S("qb_zero"), 1)
            ve.memset(KP[:, 0:1024], 0.0).then_inc(S("pq0_zero"), 1)
            ve.wait_ge(*at("const_landed", 16))
            ve.wait_ge(*at("lam_landed", 64))
            ve.wait_ge(*at("subln_landed", 16))
            ve.wait_ge(*at("small_set", 1))
            link(ve.tensor_scalar(small[:, 3:4], SUBLN, OUT_GAIN, None, ALU.mult))
            l2 = OR[:, 256:384].rearrange("p (m d) -> p m d", m=2)
            link(ve.tensor_tensor(l2, lamt[:, 0::2, :], lamt[:, 1::2, :], ALU.mult))
            ve.tensor_reduce(small[:, 6:8], l2, AX.X, ALU.add).then_inc(S("lam_sums"), 1)
            for t in range(3):
                ve.wait_ge(*at("qkv_evac0", 9 + t + 1))
                if t:
                    ve.wait_ge(*at("rotated0", t))
                rotate(t, 0, 32, 8, "cosA", "sinA", "rotated0")
            ve.wait_ge(*at("lam_exp", 1))
            link(ve.tensor_tensor(NLAM, small[:, 5:6], small[:, 4:5], ALU.subtract))
            link(ve.tensor_scalar(NLAM, NLAM, -LAM_INIT, None, ALU.add))
            link(ve.scalar_tensor_tensor(SGN, cst("c1"), NLAM, cst("c0"), ALU.mult, ALU.add))
            ve.wait_ge(*at("places_zeroed", 128))
            ve.wait_ge(*at("qb0_mm", 1))
            ve.wait_ge(*at("qb_zero", 1))
            for c in range(2):
                for hp in range(2):
                    src = PS[64 * c:64 * c + 64, 0, :].rearrange("p (t h b q) -> p t h b q", t=4, h=2, b=DB)[:, :, hp]
                    dst = QBA[64 * c:64 * c + 64, :, hp::2, hp * 16 + c * 8:hp * 16 + c * 8 + 8]\
                        .rearrange("p b t q -> p t b q")
                    ve.tensor_copy(dst, src).then_inc(S("qb0"), 1)
            prompt_attention(0)

            def batch_a(b, par):
                ve.tensor_copy(QCUR[:, par].rearrange("p h r -> p (h r)"), QB[:, bass.ds(b * 256, 256)])\
                  .then_inc(S("qcur"), 1)
                for j in range(NPAGE):
                    ve.wait_ge(*at("kt_page_mm", b * 16 + (2 * j + 2)))
                    ve.wait_ge(*at("score_mm", b * 9 + (max(j - 1, 0) + 1)))
                    ve.tensor_copy(KPG[:, j % 2, 4:8, :], PS[:, (2 * j + 1) % 4, :].rearrange("p (k n) -> p k n", k=4))\
                      .then_inc(S("kt_evac_dve"), 1)
                ve.wait_ge(*at("score_mm", b * 9 + 10))
                a0 = CONST["newmask"][0]
                link(ve.tensor_tensor(PS[:, 6, 0:NS], PS[:, 6, 0:NS], C[:, bass.ds(b * NS + a0, NS)], ALU.add))
                link(ve.tensor_reduce(small[:, 4:5], PSF[:, 2048:2048 + NK], AX.X, ALU.max))
                ve.tensor_scalar(NMAX[:, par:par + 1], small[:, 4:5], -SCALE, None, ALU.mult).then_inc(S("row_max"), 1)
                ve.wait_ge(*at("exp_done", b + 2))
                link(ve.reciprocal(RC[:, par:par + 1], SUMS[:, par:par + 1]))
                link(ve.tensor_tensor(RC[:, par:par + 1], RC[:, par:par + 1], SGN, ALU.mult))
                ve.tensor_scalar(FOLD[:, par, :], cst("fold"), RC[:, par:par + 1], None, ALU.mult)\
                  .then_inc(S("fold_ready"), 1)
                ve.wait_ge(*at("pv_mm", b + 1))
                ve.tensor_copy(OR[:, bass.ds(b * 256, 256)], PS[:, 6, 256:512]).then_inc(S("o_evac"), 1)

            ve.wait_ge(*at("po0_mm", 16))
            ve.sem_inc(S("kt_evac_dve"), 2)
            ve.sem_inc(S("o_evac"), 1)
            with ve.Fori(0, DB // 2) as i:
                loop(i, 8)
                batch_a(i * 2, 0)
                batch_a(i * 2 + 1, 1)
            loop_end(DB // 2)

            for t in range(2):
                o = QKV[:, t, 0:D]
                ve.wait_ge(*at("pv_mm", DB)) if t == 0 else None
                link(ve.tensor_tensor(SMF, o, o, ALU.mult))
                link(ve.tensor_reduce(RMS[:, 8 * t:8 * t + 8], SMF.rearrange("p (h d) -> p h d", h=8), AX.X, ALU.add))
            ve.wait_ge(*at("o_evac", DB + 1))
            for t in range(2):
                o = OR[:, D * t:D * t + D]
                link(ve.tensor_tensor(SMF, o, o, ALU.mult))
                ve.tensor_reduce(RMS[:, 16 + 8 * t:24 + 8 * t], SMF.rearrange("p (h d) -> p h d", h=8), AX.X, ALU.add)\
                  .then_inc(S("o_squares"), 1)
                ve.wait_ge(*at("o_squares", t + 1))
            ve.wait_ge(*at("o_root", 1))
            link(ve.reciprocal(RMS[:, 0:32], RMS[:, 0:32]))
            for t in range(4):
                o = (QKV[:, t, 0:D] if t < 2 else OR[:, D * (t - 2):D * (t - 1)]).rearrange("p (h d) -> p h d", h=8)
                ins = ve.tensor_tensor(o, o, RMS[:, 8 * t:8 * t + 8].unsqueeze(2).to_broadcast([P, 8, 128]), ALU.mult)
                if t == 3:
                    ins.then_inc(S("or_normed"), 1)
                else:
                    link(ins)

            def residual(layer):
                for u in range(6):
                    j, t = u // 3, u % 3
                    ve.wait_ge(*at(f"out_mm{layer}", u + 1))
                    for p0, p1, c0, c1 in pieces(t, 512):
                        x = X[0:p1 - p0, t, 512 * j + c0:512 * j + c1]
                        ins = ve.scalar_tensor_tensor(x, x, ALPHA, PS[p0:p1, 4 + u % 4, 0:c1 - c0], ALU.mult, ALU.add)
                    ins.then_inc(S(f"out_evac{layer}"), 1)
                ve.wait_ge(*at(f"out_evac{layer}", 6))

            def norm(layer, which):
                for t, (t0, n) in enumerate(TILES):
                    for half in range(2):
                        link(ve.bn_stats(STATS[0:n, t, 6 * half:6 * half + 6], X[0:n, t, 512 * half:512 * half + 512]))
                    ins = ve.bn_aggr(MV[0:n, t, :], STATS[0:n, t, :])
                    if t == 2:
                        ins.then_inc(S(f"var{layer}{which}"), 1)
                    else:
                        link(ins)
                ve.wait_ge(*at(f"std{layer}{which}", 1))
                link(ve.reciprocal(RSTD, RSTD))
                ve.wait_ge(*at(f"norm_landed{layer}{which}", 32))
                for t, (t0, n) in enumerate(TILES):
                    x = X[0:n, t, :]
                    link(ve.tensor_scalar(x, x, MV[0:n, t, 0:1], RSTD[0:n, t:t + 1], ALU.subtract, ALU.mult))
                    link(ve.tensor_tensor(x, x, GAIN[0:n], ALU.mult))
                    ve.tensor_tensor(x, x, SHIFT[0:n], ALU.add).then_inc(S(f"normed{layer}{which}"), 1)
                ve.wait_ge(*at(f"normed{layer}{which}", 3))

            def experts(layer):
                g3 = lambda m: G[:, m, 0:48].rearrange("p (t e) -> p t e", t=3)
                g12 = lambda m, w=12: G[:, m, 0:w]
                ve.memset(G[:, 0, :], 1.0).then_inc(S(f"aff_ones{layer}"), 1)
                ve.wait_ge(*at("stored", 96 if layer == 0 else 96 + 144))
                ve.wait_ge(*at(f"aff{layer}", 1))
                ve.wait_ge(*at("router_b_landed", 16))
                link(ve.tensor_tensor(g3(1), g3(0), G[:, 13, 0:NE].unsqueeze(1).to_broadcast([P, 3, NE]), ALU.add))
                s4 = G[:, 1, :].rearrange("p (g e) -> p g e", g=12)
                hi = G[:, 2, 0:24].rearrange("p (g e) -> p g e", g=12)
                lo = G[:, 2, 24:48].rearrange("p (g e) -> p g e", g=12)
                ve.tensor_tensor(hi, s4[:, :, 0::2], s4[:, :, 1::2], ALU.max)
                link(ve.tensor_tensor(lo, s4[:, :, 0::2], s4[:, :, 1::2], ALU.min))
                top, second, third = G[:, 3, 0:12], G[:, 3, 12:24], G[:, 3, 24:36]
                ve.tensor_tensor(top, hi[:, :, 0], hi[:, :, 1], ALU.max)
                ve.tensor_tensor(second, hi[:, :, 0], hi[:, :, 1], ALU.min)
                link(ve.tensor_tensor(third, lo[:, :, 0], lo[:, :, 1], ALU.max))
                link(ve.tensor_tensor(second, second, third, ALU.max))
                link(ve.tensor_tensor(top, top, second, ALU.add))

                def first_of_max(values, code, mx, out, w):
                    link(ve.tensor_reduce(mx, values, AX.X, ALU.max))
                    link(ve.tensor_tensor(out, values, mx.unsqueeze(2).to_broadcast([P, 3, w]), ALU.is_equal))
                    link(ve.tensor_tensor(out, out, code, ALU.mult))
                    link(ve.tensor_reduce(mx, out, AX.X, ALU.max))
                    link(ve.tensor_tensor(out, out, mx.unsqueeze(2).to_broadcast([P, 3, w]), ALU.is_equal))

                mx = G[:, 12, 0:3]
                grp = G[:, 4, 0:12]
                first_of_max(top.rearrange("p (t g) -> p t g", t=3), cst("grpcode").rearrange("p (t g) -> p t g", t=3), mx,
                             grp.rearrange("p (t g) -> p t g", t=3), NG)
                link(ve.tensor_scalar(G[:, 4, 12:24], grp, -1.0, BIG, ALU.add, ALU.mult))
                sel4 = G[:, 5, :].rearrange("p (g e) -> p g e", g=12)
                link(ve.tensor_tensor(sel4, s4, grp.unsqueeze(2).to_broadcast([P, 12, EG]), ALU.mult))
                link(ve.tensor_tensor(sel4, sel4, G[:, 4, 12:24].unsqueeze(2).to_broadcast([P, 12, EG]), ALU.add))
                code = cst("expcode").rearrange("p (t e) -> p t e", t=3)
                first_of_max(g3(5), code, mx, g3(6), NE)
                link(ve.scalar_tensor_tensor(g3(5), g3(6), -3.0 * BIG, g3(5), ALU.mult, ALU.add))
                first_of_max(g3(5), code, mx, g3(7), NE)
                link(ve.tensor_tensor(g3(8), g3(6), g3(7), ALU.add))
                link(ve.tensor_tensor(g3(9), g3(8), g3(0), ALU.mult))
                link(ve.tensor_reduce(mx, g3(9), AX.X, ALU.add))
                link(ve.reciprocal(mx, mx))
                link(ve.tensor_tensor(g3(10), g3(9), mx.unsqueeze(2).to_broadcast([P, 3, NE]), ALU.mult))
                ve.memset(G[NS:P, 8, 32:48], 0.0).then_inc(S(f"mask_ready{layer}"), 1)
                link(ve.memset(MH[:, 0, :], 0.0))
                link(ve.memset(XR, 0.0))
                t0, t1 = g3(1), g3(2)
                for rank in range(2):
                    link(ve.tensor_tensor(t0, g3(6 + rank), g3(10), ALU.mult))
                    link(ve.tensor_reduce(GATES[:, rank, :], t0, AX.X, ALU.add))
                ve.wait_ge(*at(f"pos_mm{layer}", 1))
                link(ve.tensor_tensor(t0, PS[:, 3, 0:48].rearrange("p (t e) -> p t e", t=3),
                                      cst("slotbase").rearrange("p (t e) -> p t e", t=3), ALU.add))
                for rank in range(2):
                    link(ve.tensor_tensor(t1, t0, g3(6 + rank), ALU.mult))
                    link(ve.tensor_reduce(mx, t1, AX.X, ALU.add))
                    link(ve.tensor_copy(IDX[:, 3 * rank:3 * rank + 3], mx))
                link(ve.tensor_reduce(G[0:1, 11, 0:1], PS[0:1, 3, 48:48 + NE], AX.X, ALU.max))
                link(ve.tensor_copy(COUNT[0:1, 0:NE], PS[0:1, 3, 48:48 + NE]))
                ve.tensor_copy(COUNT[0:1, NE:NE + 1], G[0:1, 11, 0:1]).then_inc(S(f"dispatch_ready{layer}"), 1)
                ve.wait_ge(*at(f"dispatch_ready{layer}", 1))
                most = ve.value_load(COUNT[0:1, NE:NE + 1], min_val=0, max_val=TOK)
                outer = dict(chain)
                with ve.If(most > 128):
                    for name in ("sp_hidden", "sp_y_dve", "chain_sparse"):
                        ve.sem_inc(S(f"{name}{layer}"), PER_LAYER[name + "#"])
                    chain.update(name=f"chain_dense{layer}", n=0)
                    experts_dense(layer)
                    assert chain["n"] == PER_LAYER["chain_dense#"], chain
                with ve.Else():
                    for name in ("h_ready", "y_used", "chain_dense", "acc_zero"):
                        ve.sem_inc(S(f"{name}{layer}"), PER_LAYER[name + "#"])
                    chain.update(name=f"chain_sparse{layer}", n=0)
                    experts_sparse(layer)
                    assert chain["n"] == PER_LAYER["chain_sparse#"], chain
                chain.update(outer)
                ve.nop()

            def experts_sparse(layer):
                def expert(i, par, e, m):
                    p1 = 0 if m == 128 else 64
                    ve.wait_ge(*at(f"sp_sig{layer}", e + 1))
                    link(ve.tensor_tensor(MSG[0:m, 0, :], MSG[0:m, 0, :], PS[0:m, 0, :], ALU.mult))
                    ve.tensor_tensor(MH[0:m, 0, :], MSG[0:m, 0, :], PS[p1:p1 + m, 1, :], ALU.mult)\
                      .then_inc(S(f"sp_hidden{layer}"), 1)
                    ve.wait_ge(*at(f"sp_y_mm{layer}", e + 1))
                    ve.wait_ge(*at(f"sp_y_{'ab'[par]}_stored{layer}", i * 16 + 16))
                    ve.tensor_copy(YS[par][0:m, 512:1024], PS[p1:p1 + m, 7, :]).then_inc(S(f"sp_y_dve{layer}"), 1)

                ve.sem_inc(S(f"sp_y_dve{layer}"), 1)
                with ve.Fori(0, NE // 2) as i:
                    loop(i, 2)
                    for par in range(2):
                        e = i * 2 + par
                        big = ve.value_load(COUNT[0:1, bass.ds(e, 1)], min_val=0, max_val=TOK)
                        n = chain["n"]
                        with ve.If(big > 64):
                            expert(i, par, e, 128)
                        chain["n"] = n
                        with ve.Else():
                            expert(i, par, e, 64)
                        ve.nop()
                loop_end(NE // 2)
                ve.wait_ge(*at(f"gathered{layer}", 96))
                for t, (t0, n) in enumerate(TILES):
                    x, y0, y1 = X[0:n, t, :], YG[0:n, 0, t, :], YG[0:n, 1, t, :]
                    link(ve.tensor_scalar(y1, y1, GATES[0:n, 1, t:t + 1], None, ALU.mult))
                    link(ve.scalar_tensor_tensor(y1, y0, GATES[0:n, 0, t:t + 1], y1, ALU.mult, ALU.add))
                    link(ve.scalar_tensor_tensor(x, x, ALPHA, y1, ALU.mult, ALU.add))

            def experts_dense(layer):
                ve.memset(ACC, 0.0).then_inc(S(f"acc_zero{layer}"), 1)
                ve.wait_ge(*at(f"acc_zero{layer}", 1))
                ve.sem_inc(S(f"h_ready{layer}"), 2)
                ve.sem_inc(S(f"y_used{layer}"), 1)
                with ve.Fori(0, NE // 2) as i:
                    loop(i, 6 + 4 + 2)
                    for u in range(7):
                        if u < 6:
                            t = u % 3
                            n = TILES[t][1]
                            p0 = 0 if t < 2 else NS
                            ve.wait_ge(*at(f"sig{layer}", i * 6 + (u + 1)))
                            sg, b0 = MSG[0:n, u % 2, :], 2 * (u % 2)
                            link(ve.tensor_tensor(sg, sg, PS[0:n, b0, :], ALU.mult))
                            ve.tensor_tensor(MH[0:n, u % 2, :], sg, PS[p0:p0 + n, b0 + 1, :], ALU.mult)\
                              .then_inc(S(f"h_ready{layer}"), 1)
                        if u >= 1:
                            v = u - 1
                            t = v % 3
                            n = TILES[t][1]
                            ve.wait_ge(*at(f"y_mm{layer}", i * 6 + (v + 1)))
                            comb = G[0:n, 10, bass.ds(i * 2 + (t * NE + v // 3), 1)]
                            for half in range(2):
                                p0 = 0 if t < 2 or half == 0 else NS
                                acc = ACC[0:n, t, 512 * half:512 * half + 512]
                                ins = ve.scalar_tensor_tensor(acc, PS[p0:p0 + n, 6 + half, :], comb, acc,
                                                              ALU.mult, ALU.add)
                                if half:
                                    ins.then_inc(S(f"y_used{layer}"), 1)
                                else:
                                    link(ins)
                loop_end(NE // 2)
                ve.wait_ge(*at(f"y_used{layer}", 3 * NE + 1))
                for t, (t0, n) in enumerate(TILES):
                    x = X[0:n, t, :]
                    link(ve.scalar_tensor_tensor(x, x, ALPHA, ACC[0:n, t, :], ALU.mult, ALU.add))

            def gated_input(layer):
                ve.wait_ge(*at(f"gate_b_landed{layer}", 16))
                for u in range(7):
                    if u < 6:
                        j, t = u // 3, u % 3
                        ve.wait_ge(*at(f"ple_mm{layer}", u + 1))
                        for n, (p0, p1, c0, c1) in enumerate(pieces(t, 512)):
                            ins = ve.tensor_tensor(MSG[0:p1 - p0, u % 2, c0:c1], PS[p0:p1, 2 * (u % 2), 0:c1 - c0],
                                                   GAIN[0:p1 - p0, 512 * j + c0:512 * j + c1], ALU.add)
                        ins.then_inc(S(f"gate_biased{layer}"), 1)
                    if u >= 1:
                        v = u - 1
                        j, t = v // 3, v % 3
                        ve.wait_ge(*at(f"gate_sig{layer}", v + 1))
                        for p0, p1, c0, c1 in pieces(t, 512):
                            sg = MSG[0:p1 - p0, v % 2, c0:c1]
                            link(ve.tensor_tensor(sg, sg, PS[p0:p1, 2 * (v % 2) + 1, 0:c1 - c0], ALU.mult))
                        for n, (p0, p1, c0, c1) in enumerate(pieces(t, 512)):
                            sg = MSG[0:p1 - p0, v % 2, c0:c1]
                            x = X[0:p1 - p0, t, 512 * j + c0:512 * j + c1]
                            ins = ve.tensor_tensor(x, x, sg, ALU.add)
                        ins.then_inc(S(f"gated{layer}"), 1)
                ve.wait_ge(*at(f"gated{layer}", 6))

            residual(0)
            norm(0, 0)
            experts(0)
            norm(0, 1)
            gated_input(0)

            ve.memset(QB[:, 0:1792], 0.0).then_inc(S("qb_zero"), 1)
            ve.memset(OR[:, 0:NK], 0.0).then_inc(S("or_zero"), 1)
            for t, (t0, n) in enumerate(TILES):
                ve.wait_ge(*at("qkv_evac1", 12 + t + 1))
                rotate(t, 0, HB + KVB, 8, "cosA", "sinA", None)
                rotate(t, OFF_QI, HI + 1, 16, "cosI", "sinI", "rotated1")
                ve.wait_ge(*at("rotated1", t + 1))
                k = QKV[0:n, t, OFF_K:OFF_V].rearrange("p (g d) -> p g d", g=KVB)
                dk = QKV[0:n, t, DUP_K:DUP_K + 512].rearrange("p (g u d) -> p g u d", g=KVB, u=2)
                for u in range(2):
                    ve.tensor_copy(dk[:, :, u, :], k)
                ve.tensor_scalar(WI[0:n, t, :], QKV[0:n, t, OFF_WI:B_IN], IDX_SCALE, None, ALU.mult)
                ki = QKV[0:n, t, OFF_KI:OFF_WI].unsqueeze(1).to_broadcast([n, 2, HD])
                ve.tensor_copy(QKV[0:n, t, DUP_I:DUP_I + 128].rearrange("p (u d) -> p u d", u=2), ki)\
                  .then_inc(S("doubled"), 1)
            ve.wait_ge(*at("doubled", 3))
            ve.wait_ge(*at("spread_landed", 16))
            for u in range(4):
                for bb in range(2):
                    w = WI[0:NS, 2, :].unsqueeze(2).to_broadcast([NS, HI, DQ])
                    sp = spread[0:NS, 2 * u + bb, :].rearrange("p (h q) -> p h q", h=HI)
                    ins = ve.tensor_tensor(AT[0:NS, u, 64 * bb:64 * bb + 64].rearrange("p (h q) -> p h q", h=HI),
                                           w, sp, ALU.mult)
                ins.then_inc(S("ws_rows"), 1)
            ve.wait_ge(*at("bt_mm", 6))
            ve.wait_ge(*at("qb_zero", 2))
            for c in range(2):
                for h2 in range(2):
                    for g2 in range(2):
                        src = PS[64 * h2:64 * h2 + 64, 5, :].rearrange("p (c g k b q) -> p c g k b q", c=2, g=2, k=2, b=DB)
                        dst = QBB[64 * g2:64 * g2 + 64, :, c, :]\
                            .rearrange("p b (g k h q) -> p b g k h q", g=2, k=2, h=2)[:, :, g2, :, h2, :]
                        ve.tensor_copy(dst, src[:, c, g2].rearrange("p k b q -> p b k q")).then_inc(S("bt_evac_dve"), 1)
            ve.wait_ge(*at("bt_mm", 7))
            for h2 in range(2):
                for b2 in range(2):
                    src = PS[64 * h2:64 * h2 + 64, 6, 0:256].rearrange("p (c r b q) -> p c r b q", c=4, r=4, b=2)[:, :, :, b2]
                    dst = QIB[64 * b2:64 * b2 + 64, :, 64 * b2:64 * b2 + 64]\
                        .rearrange("p r (c h q) -> p r c h q", c=4, h=2)[:, :, :, h2, :]
                    ve.tensor_copy(dst, src.rearrange("p c r q -> p r c q")).then_inc(S("bt_evac_dve"), 1)
            ve.wait_ge(*at("gated0", 6))
            ve.memset(KP[:, 0:1024], 0.0).then_inc(S("pi_zero"), 1)

            def pick(values, rounds):
                for _ in range(rounds):
                    link(ve.max(TOP8[0:values.shape[0]], values))
                    link(ve.match_replace(values, TOP8[0:values.shape[0]], values, PICKED))

            for u in range(8):
                m, t = u // 2, u % 2
                ve.wait_ge(*at("pi_relu", u + 1))
                for c in range(2):
                    s, w, acc = SM[:, u % 2, 256 * c:256 * c + 256], WI[:, t, 2 * m + c:2 * m + c + 1], PB[:, t, :]
                    ins = ve.tensor_scalar(acc, s, w, None, ALU.mult) if m == 0 and c == 0 else \
                        ve.scalar_tensor_tensor(acc, s, w, acc, ALU.mult, ALU.add)
                    if c:
                        ins.then_inc(S("pi_added"), 1)
                        ve.wait_ge(*at("pi_added", u + 1))
                    else:
                        link(ins)
            for t in range(2):
                link(ve.tensor_scalar(SMF[:, 0:256], causal[:, t, :], -1.0, NEG, ALU.is_lt, ALU.mult))
                link(ve.tensor_scalar(SMF[:, 256:512], causal[:, t, :], -1.0, None, ALU.is_gt))
                link(ve.tensor_tensor(PB[:, t, :], PB[:, t, :], SMF[:, 256:512], ALU.mult))
                link(ve.tensor_tensor(PB[:, t, :], PB[:, t, :], SMF[:, 0:256], ALU.add))
                pick(PB[:, t, :], SEL_PROMPT // 8)
                link(ve.tensor_scalar(PB[:, t, :], PB[:, t, :], -2.5e38, -BIG, ALU.is_gt, ALU.mult))
                link(ve.tensor_tensor(PB[:, t, :], PB[:, t, :], causal[:, t, :], ALU.add))
            ve.wait_ge(*at("si_sum_mm", 4))
            ve.wait_ge(*at("or_zero", 1))
            ve.tensor_copy(SELB[0:NS, 0:512], PS[0:NS, 5, :]).then_inc(S("si_taken"), 1)
            ve.tensor_copy(SELB[0:NS, 512:1024], PS[NS:2 * NS, 5, :]).then_inc(S("si_taken"), 1)
            ve.tensor_tensor(SELB[0:NS, PAST:NK], PS[0:NS, 6, 0:NS], cst("selnew", NS), ALU.add).then_inc(S("si_taken"), 1)
            ve.wait_ge(*at("kidx_evac", 8))
            ve.wait_ge(*at("sis_mm", 4))
            ve.memset(KP[:, 0:1024], 0.0).then_inc(S("pq1_zero"), 1)
            prompt_attention(1)
            ve.wait_ge(*at("si_taken", 3))
            pick(SELB[0:NS, :], SEL_SAMPLE // 8)
            ve.tensor_scalar(SELB[0:NS, :], SELB[0:NS, :], -2.5e38, -BIG, ALU.is_gt, ALU.mult).then_inc(S("selection"), 1)

            for b in range(DB):
                ve.wait_ge(*at("sb_mm", b + 1))
                link(ve.tensor_reduce(small[:, 4:5], PSF[:, 2048:2048 + NK], AX.X, ALU.max))
                ve.tensor_scalar(NMAX[:, b % 2:b % 2 + 1], small[:, 4:5], -SCALE, None, ALU.mult)\
                  .then_inc(S("row_maxb"), 1)
                ve.wait_ge(*at("expb_done", b + 1))
                link(ve.reciprocal(RC[:, 0:1], SUMS[:, b % 2:b % 2 + 1]))
                ve.wait_ge(*at("pvb_mm", b + 1))
                for j in range(4):
                    c0 = 256 + (j % 2) * 64
                    src = PS[32 * j:32 * j + 32, 6, c0:c0 + 64].unsqueeze(1).to_broadcast([32, 2, 64])
                    ve.tensor_scalar(OB[32 * j:32 * j + 32, b, :, :], src, RC[32 * j:32 * j + 32, 0:1], None, ALU.mult)\
                      .then_inc(S("ob"), 1)

            residual(1)
            norm(1, 0)
            experts(1)
            norm(1, 1)
            gated_input(1)


_INS = ["x_prompt", "x_sample", "cache_a_k", "cache_a_v", "cache_b_k", "cache_b_v", "cache_b_kidx", "page_table",
        "p_prompt", "p_sample", "a_w_in", "a_w_out", "a_lam_q1", "a_lam_k1", "a_lam_q2", "a_lam_k2", "a_subln",
        "b_w_in", "b_w_out", "ln_g", "ln_b", "router_w", "router_b", "moe_w_gate", "moe_w_up", "moe_w_down",
        "ple_proj", "ple_gate_w", "ple_gate_b"]
_OUTS = [(1, SEQ, D), (DB, DQ, D), (1, 1, SEQ, 2 * HA, HD), (1, 1, SEQ, HA, 2 * HD), (1, 1, SEQ, KVB, HD),
         (1, 1, SEQ, KVB, HD), (1, 1, SEQ, HD), (1, DB, DQ, 2 * HA, HD), (1, DB, DQ, HA, 2 * HD),
         (1, DB, DQ, KVB, HD), (1, DB, DQ, KVB, HD), (1, DB, DQ, HD)]


def program(nc, shapes):
    args = [nc.dram_tensor(f"in_{n}", shapes[n][0], mybir.dt.from_np(shapes[n][1]), kind="ExternalInput").ap()
            for n in _INS + ["consts", "spread"]]
    outs = [nc.dram_tensor(f"out_{i}", shape, F32, kind="ExternalOutput").ap() for i, shape in enumerate(_OUTS)]
    build(nc, *args, outs)


def kernel(**inputs):
    import concourse.bacc as _bacc
    from concourse.bass_utils import run_bass_kernel_spmd as _run

    nc = _bacc.Bacc("TRN2", target_bir_lowering=False, num_devices=1)
    arrays = {n: np.ascontiguousarray(inputs[n]) for n in _INS}
    arrays["consts"], arrays["spread"] = constants()
    program(nc, {n: (a.shape, a.dtype) for n, a in arrays.items()})
    r = _run(nc, [{f"in_{n}": a for n, a in arrays.items()}], core_ids=[0])
    return tuple(r.results[0][f"out_{i}"] for i in range(len(_OUTS)))
```

```python
from contextlib import ExitStack

import numpy as np
import concourse.bass as bass
from concourse import mybir

F32 = mybir.dt.float32
I32 = mybir.dt.int32
U32 = mybir.dt.uint32
ALU = mybir.AluOpType
ACT = mybir.ActivationFunctionType
AX = mybir.AxisListType

D = 1024
P = 128
KD = D // P
SEQ = 256
DB, DQ = 8, 8
NS = DB * DQ
TOK = SEQ + NS
TILES = ((0, 128), (128, 128), (256, NS))
PAGE = 128
NPAGE = 8
PAST = PAGE * NPAGE
NK = PAST + NS
HA, HB, KVB, HI, HD = 8, 16, 4, 8, 64
NE, NG, EG, FF, PD = 16, 4, 4, 512, 256
FK = FF // P
A_IN = 3 * D
B_IN = HB * HD + 2 * KVB * HD + HI * HD + HD + HI
OFF_K, OFF_V, OFF_QI, OFF_KI, OFF_WI = 1024, 1280, 1536, 2048, 2112
SEL_PROMPT, SEL_SAMPLE = 64, 256
ALPHA = 4.0 ** 0.25
EPS = 1e-5
SCALE = HD ** -0.5
IDX_SCALE = (HI ** -0.5) * (HD ** -0.5)
LAM_INIT = 0.2
OUT_GAIN = 1.0 - LAM_INIT
BIG = 1e30
NEG, PICKED = -2e38, -3e38
AT_BANK = (7, 0, 1)
TURNED = ({"tokens": 0, "keys": 6, "outputs": 12, "router": 16, "gate": 22},
          {"tokens": 0, "outputs": 6, "router": 10, "gate": 16})
SLOTS = 6


def const_layout():
    at, out = 0, {}
    for name, n in (("ident", 128), ("causal", 2 * 256), ("newmask", DB * NS), ("fold", 128), ("c0", 1), ("c1", 1),
                    ("eps", 1), ("cosA", 3 * 8), ("sinA", 3 * 8), ("cosI", 3 * 16), ("sinI", 3 * 16),
                    ("selnew", NS), ("expcode", 3 * NE), ("grpcode", 3 * NG), ("before", 128), ("ones", 128),
                    ("slotbase", 3 * NE), ("place", 128)):
        out[name] = (at, n)
        at += n
    return out, at


CONST, CONST_COLS = const_layout()


def constants():
    c = np.zeros((P, CONST_COLS), np.float32)

    def put(name, v):
        a, n = CONST[name]
        v = np.asarray(v, np.float32).reshape(v.shape[0], n)
        c[:v.shape[0], a:a + n] = v

    r = np.arange(P)
    put("ident", np.eye(P))
    key = np.arange(256)
    put("causal", np.stack([np.where(key[None] <= (r + 128 * t)[:, None], 0.0, -BIG) for t in range(2)], 1))
    tok = np.arange(NS)
    ok = (tok[None, None] // DQ == np.arange(DB)[None, :, None]) & (tok[None, None] % DQ <= (r % DQ)[:, None, None])
    put("newmask", np.where(ok, 0.0, -BIG))
    fold = np.zeros((P, P))
    for row in range(P):
        h, q = row // 16, row % 8
        fold[row, 32 * (h // 2) + 8 * (h % 2) + q] = 1
    put("fold", fold)
    put("c0", ((r // 8) % 2 == 0)[:, None])
    put("c1", ((r // 8) % 2 == 1)[:, None])
    put("eps", np.full((P, 1), EPS))
    pos = np.zeros((P, 3), np.float32)
    pos[:, 0], pos[:, 1] = r, r + 128
    pos[:NS, 2] = PAST + tok % DQ
    for name, half in (("A", 8), ("I", 16)):
        inv = (np.float32(500000.0) ** (-np.arange(half, dtype=np.float32) / np.float32(half))).astype(np.float32)
        ang = (pos[:, :, None] * inv).astype(np.float32)
        put("cos" + name, np.cos(ang))
        put("sin" + name, np.sin(ang))
    ok = (tok[:, None] // DQ == tok[None] // DQ) & (tok[None] % DQ <= tok[:, None] % DQ)
    put("selnew", np.where(ok, 0.0, NEG))
    put("expcode", np.broadcast_to(NE - np.arange(NE), (P, 3, NE)))
    put("grpcode", np.broadcast_to(NG - np.arange(NG), (P, 3, NG)))
    put("before", r[:, None] < r[None])
    put("ones", np.ones((P, P)))
    put("slotbase", np.broadcast_to(np.arange(NE) * 128, (P, 3, NE)))
    put("place", np.broadcast_to(np.arange(128), (P, 128)))
    spread = (tok[:, None, None, None] == np.arange(DB)[None, :, None, None] * DQ + np.arange(DQ)[None, None, None]) \
        * np.ones((1, 1, 8, 1))
    sp = np.zeros((P, DB * 64), np.float32)
    sp[:NS] = spread.reshape(NS, -1)
    return c, sp


PER_LAYER = {
    "qkv_mm#": 18, "qkv_evac#": 18, "turn#_mm": 28, "turn#_evac": 28, "rotated#": 3, "out_mm#": 6, "out_evac#": 6,
    "ple_mm#": 6, "experts_used#": 3 * NE, "pq#_mm": 8, "pq#_evac": 8, "pq#_zero": 1, "ps#_mm": 16, "pmask#": 16,
    "pmax#": 16, "pexp#": 16, "pw#": 16, "pat#_mm": 16, "pat#_evac": 16, "po#_mm": 16, "po#": 16,
    "so_t#_mm": 4, "so_t#_evac": 8,
    "router_landed#": 16, "logit_mm#": 1, "aff_ones#": 1, "aff#": 1, "acc_zero#": 1,
    "mask_ready#": 1, "pos_mm#": 1, "dispatch_ready#": 1, "sel_ready#": NE + 1, "rows_mm#": NE + 1,
    "rows_evac#": NE + 1, "second_mm#": 2 * NE, "second_evac#": 2 * NE, 
    "xe_mm#": NE + 1, "xe_evac#": NE + 1, "sp_gate_up_mm#": NE, "sp_sig#": NE, "sp_hidden#": NE, "sp_ht_mm#": NE,
    "sp_ht_evac#": NE, "sp_y_mm#": NE, "sp_y_act#": NE + 1, "sp_y_dve#": NE + 1, "sp_y_a_stored#": 8 * NE + 16, "sp_y_b_stored#": 8 * NE + 16,
    "chain_sparse#": NE + 9, "chain_dense#": 12 * NE // 2 + 3,
    "h_ready#": 3 * NE + 2, "gate_up_mm#": 3 * NE, "ht_mm#": 3 * NE, "ht_evac#": 3 * NE + 2, "y_mm#": 3 * NE,
    "y_used#": 3 * NE + 1, "sig#": 3 * NE, "p_landed#": 48, "pt_mm#": 1, "pt_evac#": 1, "pp_mm#": 1,
    "gated#": 6, "gate_b_landed#": 16, "gate_biased#": 6, "gate_sig#": 6, "norm_landed#0": 32, "norm_landed#1": 32,
    "normed#0": 3, "normed#1": 3, "var#0": 3, "var#1": 3, "std#0": 3, "std#1": 3,
}


def stage_of(name):
    for n, ch in enumerate(name):
        if ch in "01" and name[:n] + "#" + name[n + 1:] in PER_LAYER:
            return name[:n] + "#" + name[n + 1:], int(ch)
    return name, 0


class Stream:

    def __init__(self):
        self.items, self.landed, self.used, self.total = {}, [], [], [0] * SLOTS

    def add(self, name, used, dmas=1):
        n = len(self.landed)
        self.items[name] = n
        self.total[n % SLOTS] += 16 * dmas
        self.landed.append(self.total[n % SLOTS])
        self.used.append(used)


def plan():
    s = Stream()
    for j in range(6):
        s.add(("a_in", j), ("qkv_mm0", 3 * j + 3))
    for j in range(2):
        s.add(("a_out", j), ("out_mm0", 3 * j + 3))
    for layer in range(2):
        for e in range(NE):
            for j in range(3):
                s.add(("moe", layer, e, j), (f"experts_used{layer}", 3 * e + j + 1))
        s.add(("ple_g", layer, 0), (f"ple_mm{layer}", 3))
        s.add(("ple_p", layer), (f"ple_mm{layer}", 6))
        s.add(("ple_g", layer, 1), (f"ple_mm{layer}", 6))
        if layer == 0:
            for j in range(5):
                s.add(("b_in", j), ("qkv_mm1", 3 * j + 3))
            s.add("kidx", ("kidx_mm", 8), DB * NPAGE)
            for pr in range(4):
                s.add(("kb", pr), ("kbt_mm", 8 * pr + 8), 2 * NPAGE)
                s.add(("vb", pr), ("pvb_mm", 2 * pr + 2), 2 * NPAGE)
            for j in range(2):
                s.add(("b_out", j), ("out_mm1", 3 * j + 3))
    return s


def pieces(t, w):
    if t < 2:
        return [(0, 128, 0, w)]
    return [(0, NS, 0, w // 2), (NS, 2 * NS, w // 2, w)]


def build(nc, x_prompt, x_sample, cache_a_k, cache_a_v, cache_b_k, cache_b_v, cache_b_kidx, page_table,
          p_prompt, p_sample, a_w_in, a_w_out, a_lam_q1, a_lam_k1, a_lam_q2, a_lam_k2, a_subln,
          b_w_in, b_w_out, ln_g, ln_b, router_w, router_b, moe_w_gate, moe_w_up, moe_w_down,
          ple_proj, ple_gate_w, ple_gate_b, consts, spread_c, outs):
    stream = plan()
    pool_pages = cache_a_k.shape[1]
    with ExitStack() as ctx:
        def sb(name, shape, dt=F32):
            return ctx.enter_context(nc.sbuf_tensor(name, shape, dt))

        sems = {}

        def S(name):
            base = stage_of(name)[0]
            if base not in sems:
                sems[base] = ctx.enter_context(nc.semaphore(base))
            return sems[base]

        def at(name, value):
            base, layer = stage_of(name)
            return S(name), value + (PER_LAYER[base] if layer else 0)

        ring = sb("ring", [P, SLOTS, 4096])
        X = sb("X", [P, 3, D])
        XT = sb("XT", [P, KD, TOK])
        QKV = sb("QKV", [P, 3, A_IN])
        KT = sb("KT", [P, KD, TOK])
        QB = sb("QB", [P, 2048])
        PR = sb("PR", [P, NK])
        KP = sb("KP", [P, 2048])
        OR = sb("OR", [P, 2048])
        SM = sb("SM", [P, 2, 512])
        C = sb("C", [P, CONST_COLS])
        IDX = sb("IDX", [P, 8], U32)
        COUNT = sb("COUNT", [1, NE + 1], I32)
        G = sb("G", [P, 14, 48])
        small = sb("small", [P, 160])
        pt_sb = sb("pt_sb", [1, DB * NPAGE], page_table.dtype)
        PS = ctx.enter_context(nc.psum_tensor("PS", [P, 8, 512], F32))
        PSF = PS[:, :, :].rearrange("p b n -> p (b n)")

        def cst(name, rows=P):
            a, n = CONST[name]
            return C[0:rows, a:a + n]

        ident = cst("ident")
        causal = cst("causal").rearrange("p (t k) -> p t k", t=2)
        newmask = cst("newmask").rearrange("p (b k) -> p b k", b=DB)
        spread = cst("newmask").rearrange("p (b r) -> p b r", b=DB)

        AT = XT[:, :, :].rearrange("p k n -> p (k n)")[:, 0:9 * 128].rearrange("p (j r) -> p j r", j=9)
        QZ = KP[:, 0:1024].rearrange("p (u c q) -> p u c q", u=2, c=2)
        ATP = KP[:, 1024:2048].rearrange("p (u c n) -> p u c n", u=2, c=2)
        KPG = KP[:, :].rearrange("p (u k n) -> p u k n", u=2, k=KD)
        KBT = KP[:, :].rearrange("p (c n) -> p c n", c=2)
        KIT = KP[:, :].rearrange("p (u n) -> p u n", u=2)
        GAIN, SHIFT = KP[:, 0:D], KP[:, D:2 * D]
        QBA = QB[:, :].rearrange("p (b h r) -> p b h r", b=DB, h=HA)
        QBB = QB[:, 0:1024].rearrange("p (b c r) -> p b c r", b=DB, c=2)
        QIB = QB[:, 1024:1536].rearrange("p (u r) -> p u r", u=4)
        WS = QB[:, 1536:1792].rearrange("p (u r) -> p u r", u=4)
        QCUR = SM[:, :, 0:256].rearrange("p u (h r) -> p u h r", h=HA)
        FOLD = SM[:, :, 256:384]
        SMF = SM[:, :, :].rearrange("p u n -> p (u n)")
        OB = SMF.rearrange("p (b u d) -> p b u d", b=DB, u=2)
        SELB = OR[:, 0:NK]
        PB = OR[:, NK:NK + 512].rearrange("p (t k) -> p t k", t=2)
        lamt = OR[:, 0:256].rearrange("p (m d) -> p m d", m=4)
        NMAX, SUMS, RC = small[:, 8:16], small[:, 16:24], small[:, 24:32]
        SUBLN, SGN, NLAM = small[:, 0:1], small[:, 1:2], small[:, 2:3]
        RMS = small[:, 32:64]
        STATS = small[:, 64:100].rearrange("p (t n) -> p t n", t=3)
        MV = small[:, 100:106].rearrange("p (t n) -> p t n", t=3)
        RSTD = small[:, 106:109]
        WI = small[:, 110:134].rearrange("p (t h) -> p t h", t=3)
        TOP8 = small[:, 134:142]

        DUP_K, DUP_I = B_IN, B_IN + 512
        QF = QKV[:, :, :].rearrange("p t n -> p (t n)")
        ACC = QF[:, 0:3072].rearrange("p (t n) -> p t n", t=3)
        MSG = QF[:, 4096:5120].rearrange("p (u n) -> p u n", u=2)
        MH = QF[:, 5120:6144].rearrange("p (u n) -> p u n", u=2)
        MHT = QF[:, 7168:8192].rearrange("p (u k n) -> p u k n", u=2, k=FK)
        SEL = QF[:, 0:768].rearrange("p (u t r) -> p u t r", u=2, t=3)
        XR = QF[:, 1024:1536]
        XE = QF[:, 2048:3072].rearrange("p (k n) -> p k n", k=KD)
        YS = (QF[:, 6144:7168], QF[:, 8192:9216])
        YG = QF[:, 0:6144].rearrange("p (r t n) -> p r t n", r=2, t=3)
        GATES = small[:, 142:148].rearrange("p (r t) -> p r t", r=2)
        WHERE = QF[:, 768:768 + 3 * (NE + 1)]
        places = nc.dram_tensor("places", [NE * 128, D], F32).ap()
        KTF = KT[:, :, :].rearrange("p k n -> p (k n)")
        PT = KT[:, 0:2, :]
        PROWS = KTF[:, 768:1536].rearrange("p (t n) -> p t n", t=3)
        GATE_BIAS = KTF[:, 1536:2560]

        landed = [S(f"ring_landed{s}") for s in range(SLOTS)]
        k_landed = [S(f"kpage_landed{s}") for s in range(NPAGE)]
        v_landed = [S(f"vpages_landed{s}") for s in range(2)]
        kpage = ring[:, 0:2, :].rearrange("p s (j n) -> p (s j) n", j=4)
        vpage = ring[:, 2:6, :].rearrange("p s (j n) -> p (s j) n", j=4)

        y_p, y_s, nak_p, nav_p, nbk_p, nbv_p, nbi_p, nak_s, nav_s, nbk_s, nbv_s, nbi_s = outs

        def item(name):
            n = stream.items[name]
            return n, n % SLOTS

        def token_rows(prompt, sample, t):
            t0, n = TILES[t]
            return prompt[t0:t0 + n, :] if t < 2 else sample

        block = ctx.enter_context(nc.Block())

        @block.sync
        def _(sp):
            sp.wait_ge(*at("page_table_landed", 16))

            def place(name):
                n, s = item(name)
                if n >= SLOTS:
                    sp.wait_ge(*at(stream.used[n - SLOTS][0], stream.used[n - SLOTS][1]))
                return s

            def columns(name, w, c0, c1, rows_together):
                view = w.rearrange("(p k) n -> p k n", k=KD) if rows_together else \
                    w.rearrange("(k p) n -> p k n", p=P)
                s = place(name)
                sp.dma_start(ring[:, s, 0:KD * (c1 - c0)].rearrange("p (k n) -> p k n", k=KD),
                             view[:, :, c0:c1]).then_inc(landed[s], 16)

            def page_id(b, j):
                return sp.value_load(pt_sb[0:1, bass.ds(b * NPAGE + j, 1)], min_val=0, max_val=pool_pages - 1)

            for j in range(6):
                columns(("a_in", j), a_w_in[0], 512 * j, 512 * j + 512, True)

            def pages(b, par, first):
                for j in range(NPAGE):
                    pg = page_id(b, j)
                    if first and par == 0:
                        sp.wait_ge(*at("qkv_mm0", 3 * (j // 4 + 1)))
                    else:
                        sp.wait_ge(*at("kt_page_mm", b * 16 + (2 * j + 2 - 16)))
                    sp.dma_start(kpage[:, j, :], cache_a_k[0, bass.ds(pg, 1)].rearrange("a p h d -> (a p) (h d)"))\
                      .then_inc(k_landed[j], 16)
                    if first:
                        sp.wait_ge(*at("qkv_mm0", 3 * (2 + (8 * par + j) // 4 + 1)))
                    elif j == 0:
                        sp.wait_ge(*at("pv_mm", b - 1))
                    sp.dma_start(vpage[:, par * NPAGE + j, :],
                                 cache_a_v[0, bass.ds(pg, 1)].rearrange("a p h d -> (a p) (h d)"))\
                      .then_inc(v_landed[par], 16)

            pages(0, 0, True)
            pages(1, 1, True)
            with sp.Fori(1, DB // 2) as i:
                pages(i * 2, 0, False)
                pages(i * 2 + 1, 1, False)

            sp.wait_ge(*at("kt_page_mm", 16 * DB))
            for j in range(2):
                columns(("a_out", j), a_w_out[0], 512 * j, 512 * j + 512, False)
            sp.wait_ge(*at("pv_mm", DB))

            for layer in range(2):
                n0 = stream.items[("moe", layer, 0, 0)]

                def expert(e, j, wait):
                    s = (n0 + j) % SLOTS
                    wait()
                    w = (moe_w_gate, moe_w_up, moe_w_down)[j % 3]
                    sp.dma_start(ring[:, s, :], w[layer, bass.ds(e, 1)].rearrange("a (p k) n -> (a p) (k n)", p=P))\
                      .then_inc(landed[s], 16)

                for j in range(6):
                    n = n0 + j - SLOTS
                    before = layer == 0 and n < 6
                    expert(j // 3, j, (lambda: None) if before else
                           (lambda n=n: sp.wait_ge(*at(stream.used[n][0], stream.used[n][1]))))
                with sp.Fori(1, NE // 2) as i:
                    for j in range(6):
                        expert(i * 2 + j // 3, j, lambda j=j: sp.wait_ge(*at(f"experts_used{layer}", i * 6 + (j - 5))))
                columns(("ple_g", layer, 0), ple_gate_w[layer], 0, 512, True)
                s = place(("ple_p", layer))
                sp.dma_start(ring[:, s, 0:2048], ple_proj[layer].rearrange("(p k) n -> p (k n)", k=2))\
                  .then_inc(landed[s], 16)
                sp.wait_ge(*at(f"normed{layer}1", 1))
                columns(("ple_g", layer, 1), ple_gate_w[layer], 512, 1024, True)
                if layer == 0:
                    for j in range(5):
                        columns(("b_in", j), b_w_in[0], 512 * j, min(512 * j + 512, B_IN), True)
                    s = place("kidx")
                    kx = ring[:, s, :].rearrange("p (r j b d) -> p r j b d", r=4, b=2, j=NPAGE)
                    for b in range(DB):
                        for j in range(NPAGE):
                            pg = page_id(b, j)
                            sp.dma_start(kx[:, b // 2, j, b % 2, :],
                                         cache_b_kidx[0, bass.ds(pg, 1)].rearrange("a p d -> (a p) d"))\
                              .then_inc(landed[s], 16)
                    for pr in range(4):
                        for what, cache in (("kb", cache_b_k), ("vb", cache_b_v)):
                            s = place((what, pr))
                            for bb in range(2):
                                for j in range(NPAGE):
                                    pg = page_id(2 * pr + bb, j)
                                    c0 = (bb * NPAGE + j) * KVB * HD
                                    sp.dma_start(ring[:, s, c0:c0 + KVB * HD],
                                                 cache[0, bass.ds(pg, 1)].rearrange("a p h d -> (a p) (h d)"))\
                                      .then_inc(landed[s], 16)
                    for j in range(2):
                        columns(("b_out", j), b_w_out[0], 512 * j, 512 * j + 512, False)

        @block.gpsimd
        def _(pool):
            pool.dma_start(pt_sb[:, :], page_table.rearrange("(o b) j -> o (b j)", o=1))\
                .then_inc(S("page_table_landed"), 16)
            pool.dma_start(C[:, :], consts).then_inc(S("const_landed"), 16)
            for t, (t0, n) in enumerate(TILES):
                pool.dma_start(X[0:n, t, :], token_rows(x_prompt[0], x_sample.rearrange("b q d -> (b q) d"), t))\
                    .then_inc(S(f"x_landed{t}"), 16)
            pool.dma_start(SUBLN, a_subln.rearrange("a d -> d a")).then_inc(S("lam_landed"), 16)
            for m, w in enumerate((a_lam_q1, a_lam_k1, a_lam_q2, a_lam_k2)):
                pool.dma_start(lamt[:, m, :], w[0].partition_broadcast(P)).then_inc(S("lam_landed"), 16)
            pool.dma_start(G[:, 13, 0:NE], router_b.partition_broadcast(P)).then_inc(S("router_b_landed"), 16)

            for t, (t0, n) in enumerate(TILES):
                pool.wait_ge(*at("rotated0", t + 1))
                pool.dma_start(token_rows(nak_p[0, 0].rearrange("s h d -> s (h d)"),
                                          nak_s[0].rearrange("b q h d -> (b q) (h d)"), t),
                               QKV[0:n, t, D:2 * D]).then_inc(S("stored"), 16)
                pool.wait_ge(*at("qkv_evac0", 15 + t + 1))
                pool.dma_start(token_rows(nav_p[0, 0].rearrange("s h d -> s (h d)"),
                                          nav_s[0].rearrange("b q h d -> (b q) (h d)"), t),
                               QKV[0:n, t, 2 * D:3 * D]).then_inc(S("stored"), 16)

            pool.wait_ge(*at("or_cleared", 1))
            for c in range(8):
                pool.dma_start(places.rearrange("(p a) n -> p (a n)", p=P)[:, 2048 * c:2048 * c + 2048], OR[:, :])\
                    .then_inc(S("places_zeroed"), 16)

            for layer in range(2):
                pool.wait_ge(*at(f"out_mm{layer}", 1))

                def norm_params(which):
                    for ap, w in ((GAIN, ln_g), (SHIFT, ln_b)):
                        pool.dma_start(ap, w[layer, which].partition_broadcast(P))\
                            .then_inc(S(f"norm_landed{layer}{which}"), 16)

                norm_params(0)
                pool.dma_start(SMF[:, 0:KD * NE].rearrange("p (k e) -> p k e", k=KD),
                               router_w.rearrange("(p k) e -> p k e", k=KD)).then_inc(S(f"router_landed{layer}"), 16)
                for t, (t0, n) in enumerate(TILES):
                    pool.dma_start(PROWS[0:n, t, :],
                                   token_rows(p_prompt[layer, 0], p_sample[layer].rearrange("b q d -> (b q) d"), t))\
                        .then_inc(S(f"p_landed{layer}"), 16)
                pool.dma_start(GATE_BIAS, ple_gate_b[layer].partition_broadcast(P)).then_inc(S(f"gate_b_landed{layer}"), 16)
                pool.wait_ge(*at(f"normed{layer}0", 3))
                norm_params(1)
                pool.wait_ge(*at(f"dispatch_ready{layer}", 1))
                most = pool.value_load(COUNT[0:1, NE:NE + 1], min_val=0, max_val=TOK)
                with pool.If(most > 128):
                    pool.nop()
                with pool.Else():
                    for ab in "ab":
                        pool.wait_ge(*at(f"sp_y_{ab}_stored{layer}", 8 * NE + 16))
                    for t, (t0, n) in enumerate(TILES):
                        for rank in range(2):
                            pool.indirect_dma_start(
                                out=YG[0:n, rank, t, :], out_offset=None, in_=places,
                                in_offset=bass.IndirectOffsetOnAxis(ap=IDX[0:n, 3 * rank + t:3 * rank + t + 1], axis=0),
                                bounds_check=NE * 128 - 1).then_inc(S(f"tile{t}_moved{layer}"), 16)
                pool.nop()
                if layer == 0:
                    a, n = CONST["newmask"]
                    pool.dma_start(C[:, a:a + n], spread_c).then_inc(S("spread_landed"), 16)
                    for t, (t0, n) in enumerate(TILES):
                        pool.wait_ge(*at("rotated1", t + 1))
                        for o_p, o_s, c0, c1 in ((nbk_p, nbk_s, OFF_K, OFF_V), (nbv_p, nbv_s, OFF_V, OFF_QI)):
                            pool.dma_start(token_rows(o_p[0, 0].rearrange("s h d -> s (h d)"),
                                                      o_s[0].rearrange("b q h d -> (b q) (h d)"), t),
                                           QKV[0:n, t, c0:c1]).then_inc(S("stored"), 16)
                        pool.dma_start(token_rows(nbi_p[0, 0], nbi_s[0].rearrange("b q d -> (b q) d"), t),
                                       QKV[0:n, t, OFF_KI:OFF_WI]).then_inc(S("stored"), 16)
            pool.wait_ge(*at("gated1", 6))
            for t, (t0, n) in enumerate(TILES):
                pool.dma_start(token_rows(y_p[0], y_s.rearrange("b q d -> (b q) d"), t), X[0:n, t, :])\
                    .then_inc(S("stored"), 16)
            pool.wait_ge(*at("stored", 16 * (6 + 9 + 3)))

        @block.tensor
        def _(pe):
            pe.wait_ge(*at("const_landed", 16))

            def transposed(layer, stage, view, ready, tiles=(0, 1, 2), banks=(0, 1, 2, 3)):
                first = TURNED[layer][stage]
                for u in range(2 * len(tiles)):
                    t, half = tiles[u // 2], u % 2
                    n = TILES[t][1]
                    if half == 0:
                        ready(t)
                    if u >= len(banks):
                        pe.wait_ge(*at(f"turn{layer}_evac", first + u - len(banks) + 1))
                    for j in range(4):
                        ins = pe.transpose(PS[:, banks[u % len(banks)], j * 128:j * 128 + n], view(t, 4 * half + j)[0:n],
                                           ident[0:n, 0:n])
                    ins.then_inc(S(f"turn{layer}_mm"), 1)

            def stream_chunk(a, t, k, kd=KD):
                return a[:, t, :].rearrange("p (f k) -> p k f", k=kd)[:, k, :]

            def project(tag, items, widths, evac):
                u = 0
                for name, w in zip(items, widths):
                    n, s = item(name)
                    pe.wait_ge(landed[s], stream.landed[n])
                    wt = ring[:, s, 0:KD * w].rearrange("p (k n) -> p k n", k=KD)
                    for t, (t0, rows) in enumerate(TILES):
                        if u >= 4:
                            pe.wait_ge(*at(evac, u - 3))
                        for k in range(KD):
                            for p0, p1, c0, c1 in pieces(t, w):
                                ins = pe.matmul(PS[p0:p1, 4 + u % 4, 0:c1 - c0], XT[:, k, t0:t0 + rows],
                                                wt[:, k, c0:c1], start=(k == 0), stop=(k == KD - 1))
                        ins.then_inc(S(tag), 1)
                        u += 1

            def query_chunk(tag, m, c0):
                if m >= 2:
                    pe.wait_ge(*at(tag + "_evac", m - 1))
                for t in range(2):
                    ins = pe.transpose(PS[:, m % 2, 128 * t:128 * t + 128], QKV[:, t, c0:c0 + 128], ident)
                ins.then_inc(S(tag + "_mm"), 1)

            def prompt_scores(layer, u):
                m, qt = u // 2, u % 2
                if qt == 0:
                    pe.wait_ge(*at(f"pq{layer}_evac", m + 1))
                if u >= 2:
                    pe.wait_ge(*at(f"pmask{layer}", u - 1))
                kw = 128 * (qt + 1)
                kt = KT[:, m, :] if layer == 0 else KT[:, m // 2, :]
                for c in range(2):
                    ins = pe.matmul(PS[:, 2 + u % 2, c * 256:c * 256 + kw], QZ[:, m % 2, c, 128 * qt:128 * qt + 128],
                                    kt[:, 0:kw], start=True, stop=True)
                ins.then_inc(S(f"ps{layer}_mm"), 1)

            def prompt_turn(layer, u):
                qt = u % 2
                pe.wait_ge(*at(f"pw{layer}", u + 1))
                if u >= 2:
                    pe.wait_ge(*at(f"pat{layer}_evac", u - 1))
                for c in range(1 if layer == 0 else 2):
                    for kt in range(qt + 1):
                        ins = pe.transpose(PS[:, 4 + u % 2, (2 * c + kt) * 128:(2 * c + kt + 1) * 128],
                                           SM[:, u % 2, c * 256 + kt * 128:c * 256 + kt * 128 + 128], ident)
                ins.then_inc(S(f"pat{layer}_mm"), 1)

            def prompt_values(layer, u):
                m, qt = u // 2, u % 2
                pe.wait_ge(*at(f"pat{layer}_evac", u + 1))
                if u >= 2:
                    pe.wait_ge(*at(f"po{layer}", u - 1))
                for c in range(1 if layer == 0 else 2):
                    w = 128 if layer == 0 else 64
                    v0 = 2 * D + m * 128 if layer == 0 else OFF_V + (m // 2) * 64
                    for kt in range(qt + 1):
                        ins = pe.matmul(PS[:, 6 + u % 2, c * w:c * w + w],
                                        ATP[:, u % 2, c, kt * 128:kt * 128 + 128],
                                        QKV[:, kt, v0:v0 + w], start=(kt == 0), stop=(kt == qt))
                ins.then_inc(S(f"po{layer}_mm"), 1)

            def prompt_attention(layer):
                for m in range(2):
                    query_chunk(f"pq{layer}", m, m * 128)
                for u in range(16 + 2):
                    if u < 16:
                        prompt_scores(layer, u)
                        if u % 2 == 1 and u // 2 + 2 < 8:
                            query_chunk(f"pq{layer}", u // 2 + 2, (u // 2 + 2) * 128)
                    if 1 <= u <= 16:
                        prompt_turn(layer, u - 1)
                    if u >= 2:
                        prompt_values(layer, u - 2)

            transposed(0, "tokens", lambda t, k: stream_chunk(X, t, k), lambda t: pe.wait_ge(*at(f"x_landed{t}", 16)))
            pe.wait_ge(*at("turn0_evac", 6))
            project("qkv_mm0", [("a_in", j) for j in range(6)], [512] * 6, "qkv_evac0")
            transposed(0, "keys", lambda t, k: QKV[:, t, D + 128 * k:D + 128 * k + 128],
                       lambda t: pe.wait_ge(*at("rotated0", t + 1)))
            pe.wait_ge(*at("turn0_evac", TURNED[0]["keys"] + 6))
            for k in range(KD):
                ins = pe.transpose(PS[:, 0, k * NS:(k + 1) * NS], QKV[0:NS, 2, k * 128:(k + 1) * 128], ident[0:NS, 0:NS])
            ins.then_inc(S("qb0_mm"), 1)
            pe.wait_ge(*at("qb0", 4))
            pe.wait_ge(*at("qkv_evac0", 18))
            prompt_attention(0)
            pe.wait_ge(*at("po0", 16))

            def page_turn(b, j):
                pe.wait_ge(k_landed[j], b * 16 + 16)
                for half, evac in enumerate(("kt_evac_act", "kt_evac_dve")):
                    pe.wait_ge(*at(evac, b * 8 + (j + 1)))
                    for k in range(4):
                        ins = pe.transpose(PS[:, (2 * j + half) % 4, k * 128:(k + 1) * 128],
                                           kpage[:, j, (4 * half + k) * 128:(4 * half + k + 1) * 128], ident)
                    ins.then_inc(S("kt_page_mm"), 1)

            def page_scores(b, par, j):
                for evac in ("kt_evac_act", "kt_evac_dve"):
                    pe.wait_ge(*at(evac, b * 8 + (j + 3)))
                if j == 0:
                    pe.wait_ge(*at("qcur", b + 1))
                    pe.wait_ge(*at("exp_done", b + 1))
                for half in range(2):
                    for t in range(4):
                        h = 2 * t + half
                        ins = pe.matmul(PS[32 * t:32 * t + 32, 4 + j // 4, (j % 4) * 128:(j % 4) * 128 + 128],
                                        QCUR[:, par, h, :], KPG[:, j % 2, h, :], start=(half == 0), stop=(half == 1))
                ins.then_inc(S("score_mm"), 1)

            def batch_a(b, par, i):
                for j in range(NPAGE + 1):
                    if j < NPAGE:
                        page_turn(b, j)
                    if j >= 1:
                        page_scores(b, par, j - 1)
                pe.wait_ge(*at("o_evac", b + 1))
                for half in range(2):
                    for t in range(4):
                        h = 2 * t + half
                        ins = pe.matmul(PS[32 * t:32 * t + 32, 6, 0:NS], QCUR[:, par, h, :], KT[:, h, SEQ:TOK],
                                        start=(half == 0), stop=(half == 1))
                ins.then_inc(S("score_mm"), 1)
                pe.wait_ge(*at("fold_ready", b + 1))
                for u in range(3):
                    for j in range(4 * u, min(4 * u + 4, 9)):
                        keys = min(128, NK - 128 * j)
                        c0 = (j % 4) * 128
                        ins = pe.matmul(PS[0:keys, AT_BANK[u], c0:c0 + 128], PR[:, 128 * j:128 * j + keys],
                                        FOLD[:, par, :], start=True, stop=True)
                    ins.then_inc(S("at_mm"), 1)
                pe.wait_ge(v_landed[par], i * 128 + 128)
                for j in range(NPAGE + 1):
                    keys = min(128, NK - 128 * j)
                    if j in (0, 4):
                        pe.wait_ge(*at("at_evac", b * 3 + (1 if j == 0 else 3)))
                    for t in range(4):
                        v = vpage[:, par * NPAGE + j, 256 * t:256 * t + 256] if j < NPAGE else \
                            QKV[0:NS, 2, 2 * D + 256 * t:2 * D + 256 * t + 256]
                        ins = pe.matmul(PS[32 * t:32 * t + 32, 6, 256:512], AT[0:keys, j, 32 * t:32 * t + 32], v,
                                        start=(j == 0), stop=(j == NPAGE))
                ins.then_inc(S("pv_mm"), 1)

            pe.sem_inc(S("score_mm"), 1)
            with pe.Fori(0, DB // 2) as i:
                batch_a(i * 2, 0, i)
                batch_a(i * 2 + 1, 1, i)

            pe.wait_ge(*at("kt_evac_act", 8 * DB + 2))
            pe.wait_ge(*at("kt_evac_dve", 8 * DB + 2))
            pe.wait_ge(*at("or_normed", 1))
            transposed(0, "outputs", lambda t, k: QKV[:, t, 128 * k:128 * k + 128], lambda t: None, (0, 1))
            for u in range(4):
                for j in range(4):
                    ins = pe.transpose(PS[:, 4 + u, j * 128:j * 128 + 128],
                                       OR[:, (4 * u + j) * 128:(4 * u + j + 1) * 128], ident)
                ins.then_inc(S("so_t0_mm"), 1)
            pe.wait_ge(*at("turn0_evac", TURNED[0]["outputs"] + 4))
            pe.wait_ge(*at("so_t0_evac", 8))
            project("out_mm0", [("a_out", j) for j in range(2)], [512] * 2, "out_evac0")

            def router(layer):
                pe.wait_ge(*at(f"out_evac{layer}", 6))
                transposed(layer, "router", lambda t, k: stream_chunk(X, t, k),
                           lambda t: pe.wait_ge(*at(f"normed{layer}0", t + 1)))
                pe.wait_ge(*at(f"router_landed{layer}", 16))
                for t, (t0, n) in enumerate(TILES):
                    pe.wait_ge(*at(f"turn{layer}_evac", TURNED[layer]["router"] + 2 * t + 2))
                    for k in range(KD):
                        ins = pe.matmul(PS[0:n, 4, t * NE:(t + 1) * NE], XT[:, k, t0:t0 + n], SMF[:, k * NE:(k + 1) * NE],
                                        start=(k == 0), stop=(k == KD - 1))
                ins.then_inc(S(f"logit_mm{layer}"), 1)

            def positions(layer):
                pe.wait_ge(*at(f"p_landed{layer}", 48))
                for t, (t0, n) in enumerate(TILES):
                    for k in range(2):
                        ins = pe.transpose(PS[:, 5 + k, t0:t0 + n], stream_chunk(PROWS, t, k, 2)[0:n], ident[0:n, 0:n])
                ins.then_inc(S(f"pt_mm{layer}"), 1)
                pe.wait_ge(*at(f"mask_ready{layer}", 1))
                mask = G[:, 8, :]
                pe.matmul(PS[:, 3, 0:48], cst("before"), mask, start=True, stop=False)
                pe.matmul(PS[:, 3, NE:48], cst("ones"), mask[:, 0:2 * NE], start=False, stop=False)
                pe.matmul(PS[:, 3, 2 * NE:48], cst("ones"), mask[:, 0:NE], start=False, stop=True)
                for t in range(3):
                    ins = pe.matmul(PS[:, 3, 48:48 + NE], cst("ones"), mask[:, t * NE:(t + 1) * NE],
                                    start=(t == 0), stop=(t == 2))
                ins.then_inc(S(f"pos_mm{layer}"), 1)
                pe.wait_ge(*at(f"pt_evac{layer}", 1))
                pe.wait_ge(*at(f"dispatch_ready{layer}", 1))

            def experts(layer):
                most = pe.value_load(COUNT[0:1, NE:NE + 1], min_val=0, max_val=TOK)
                with pe.If(most > 128):
                    for name in ("rows_mm", "second_mm", "xe_mm", "sp_gate_up_mm", "sp_ht_mm", "sp_y_mm"):
                        pe.sem_inc(S(f"{name}{layer}"), PER_LAYER[name + "#"])
                    experts_dense(layer)
                with pe.Else():
                    for name in ("gate_up_mm", "ht_mm", "y_mm"):
                        pe.sem_inc(S(f"{name}{layer}"), PER_LAYER[name + "#"])
                    experts_sparse(layer)
                pe.nop()

            def experts_sparse(layer):
                n0 = stream.items[("moe", layer, 0, 0)]

                def slot_of(i, j):
                    s = (n0 + j) % SLOTS
                    pe.wait_ge(landed[s], i * 16 + stream.landed[n0 + j])
                    return ring[:, s, :]

                def rows(par, places, bank):
                    for t in range(3):
                        for half in range(2):
                            ins = pe.matmul(PS[64 * half:64 * half + 64, bank, :], SEL[:, par, t, places:places + 64],
                                            X[:, t, :].rearrange("p (f k) -> p k f", k=KD)[:, 4 * half:4 * half + 4, :],
                                            start=(t == 0), stop=(t == 2))
                    return ins

                def turn(bank):
                    for k in range(4):
                        ins = pe.transpose(PS[:, bank, k * 128:k * 128 + 128], XR[:, k * 128:k * 128 + 128], ident)
                    return ins

                def expert(i, par, e, m):
                    p1 = 0 if m == 128 else 64
                    pe.wait_ge(*at(f"xe_evac{layer}", e + 1))
                    if m == 128:
                        rows(par, 64, 4).then_inc(S(f"second_mm{layer}"), 1)
                        pe.wait_ge(*at(f"second_evac{layer}", e * 2 + 1))
                        turn(5).then_inc(S(f"second_mm{layer}"), 1)
                        pe.wait_ge(*at(f"second_evac{layer}", e * 2 + 2))
                    else:
                        pe.sem_inc(S(f"second_mm{layer}"), 2)
                    wg = slot_of(i, 3 * par).rearrange("p (k n) -> p k n", k=KD)
                    wu = slot_of(i, 3 * par + 1).rearrange("p (k n) -> p k n", k=KD)
                    for k in range(KD):
                        pe.matmul(PS[0:m, 0, :], XE[:, k, 0:m], wg[:, k, :], start=(k == 0), stop=(k == KD - 1))
                        ins = pe.matmul(PS[p1:p1 + m, 1, :], XE[:, k, 0:m], wu[:, k, :],
                                        start=(k == 0), stop=(k == KD - 1))
                    ins.then_inc(S(f"sp_gate_up_mm{layer}"), 1)
                    pe.wait_ge(*at(f"sel_ready{layer}", e + 2))
                    rows(1 - par, 0, 4).then_inc(S(f"rows_mm{layer}"), 1)
                    pe.wait_ge(*at(f"sp_hidden{layer}", e + 1))
                    pe.sem_inc(S(f"experts_used{layer}"), 2)
                    for k in range(FK):
                        ins = pe.transpose(PS[:, 2, k * 128:k * 128 + 128],
                                           MH[:, 0, :].rearrange("p (f k) -> p k f", k=FK)[:, k, :], ident)
                    ins.then_inc(S(f"sp_ht_mm{layer}"), 1)
                    pe.wait_ge(*at(f"rows_evac{layer}", e + 2))
                    turn(5).then_inc(S(f"xe_mm{layer}"), 1)
                    wd = slot_of(i, 3 * par + 2).rearrange("p (k n) -> p k n", k=FK)
                    for name in ("sp_y_act", "sp_y_dve"):
                        pe.wait_ge(*at(f"{name}{layer}", e + 1))
                    pe.wait_ge(*at(f"sp_ht_evac{layer}", e + 1))
                    for k in range(FK):
                        for half in range(2):
                            ins = pe.matmul(PS[p1 * half:p1 * half + m, 6 + half, :], MHT[:, 0, k, 0:m],
                                            wd[:, k, 512 * half:512 * half + 512], start=(k == 0), stop=(k == FK - 1))
                    ins.then_inc(S(f"sp_y_mm{layer}"), 1)
                    pe.wait_ge(*at(f"sp_y_mm{layer}", e + 1))
                    pe.sem_inc(S(f"experts_used{layer}"), 1)

                pe.wait_ge(*at(f"sel_ready{layer}", 1))
                rows(0, 0, 4).then_inc(S(f"rows_mm{layer}"), 1)
                pe.wait_ge(*at(f"rows_evac{layer}", 1))
                turn(5).then_inc(S(f"xe_mm{layer}"), 1)
                with pe.Fori(0, NE // 2) as i:
                    for par in range(2):
                        e = i * 2 + par
                        big = pe.value_load(COUNT[0:1, bass.ds(e, 1)], min_val=0, max_val=TOK)
                        with pe.If(big > 64):
                            expert(i, par, e, 128)
                        with pe.Else():
                            expert(i, par, e, 64)
                        pe.nop()

            def experts_dense(layer):
                n0 = stream.items[("moe", layer, 0, 0)]

                def slot_of(i, j):
                    s = (n0 + j) % SLOTS
                    pe.wait_ge(landed[s], i * 16 + stream.landed[n0 + j])
                    return ring[:, s, :]

                def gate_up(i, u):
                    t, b0 = u % 3, 2 * (u % 2)
                    t0, n = TILES[t]
                    wg = slot_of(i, u // 3 * 3).rearrange("p (k n) -> p k n", k=KD)
                    wu = slot_of(i, u // 3 * 3 + 1).rearrange("p (k n) -> p k n", k=KD)
                    pe.wait_ge(*at(f"h_ready{layer}", i * 6 + (u + 1)))
                    for k in range(KD):
                        pe.matmul(PS[0:n, b0, :], XT[:, k, t0:t0 + n], wg[:, k, :], start=(k == 0), stop=(k == KD - 1))
                        p0 = 0 if t < 2 else NS
                        ins = pe.matmul(PS[p0:p0 + n, b0 + 1, :], XT[:, k, t0:t0 + n], wu[:, k, :],
                                        start=(k == 0), stop=(k == KD - 1))
                    ins.then_inc(S(f"gate_up_mm{layer}"), 1)

                def down(i, u):
                    t = u % 3
                    n = TILES[t][1]
                    pe.wait_ge(*at(f"h_ready{layer}", i * 6 + (u + 3)))
                    if t == 2:
                        pe.sem_inc(S(f"experts_used{layer}"), 2)
                    pe.wait_ge(*at(f"ht_evac{layer}", i * 6 + (u + 1)))
                    for k in range(FK):
                        ins = pe.transpose(PS[:, 4 + u % 2, k * 128:k * 128 + 128],
                                           MH[:, u % 2, :].rearrange("p (f k) -> p k f", k=FK)[:, k, :], ident)
                    ins.then_inc(S(f"ht_mm{layer}"), 1)
                    wd = slot_of(i, u // 3 * 3 + 2).rearrange("p (k n) -> p k n", k=FK)
                    pe.wait_ge(*at(f"ht_evac{layer}", i * 6 + (u + 3)))
                    pe.wait_ge(*at(f"y_used{layer}", i * 6 + (u + 1)))
                    for k in range(FK):
                        for half in range(2):
                            p0 = 0 if t < 2 or half == 0 else NS
                            ins = pe.matmul(PS[p0:p0 + n, 6 + half, :], MHT[:, u % 2, k, 0:n],
                                            wd[:, k, 512 * half:512 * half + 512], start=(k == 0), stop=(k == FK - 1))
                    ins.then_inc(S(f"y_mm{layer}"), 1)
                    if t == 2:
                        pe.wait_ge(*at(f"y_mm{layer}", i * 6 + (u + 1)))
                        pe.sem_inc(S(f"experts_used{layer}"), 1)

                with pe.Fori(0, NE // 2) as i:
                    for u in range(7):
                        if u < 6:
                            gate_up(i, u)
                        if u >= 1:
                            down(i, u - 1)

            def gated_input(layer):
                n, s = item(("ple_p", layer))
                wp = ring[:, s, 0:2048].rearrange("p (k n) -> p k n", k=2)
                pe.wait_ge(landed[s], stream.landed[n])
                for t, (t0, rows) in enumerate(TILES):
                    for j in range(2):
                        out = PS[0:rows, 2 * t + j, :] if t < 2 else PS[NS * j:NS * j + NS, 4, :]
                        for k in range(2):
                            ins = pe.matmul(out, PT[:, k, t0:t0 + rows], wp[:, k, 512 * j:512 * j + 512],
                                            start=(k == 0), stop=(k == 1))
                ins.then_inc(S(f"pp_mm{layer}"), 1)
                transposed(layer, "gate", lambda t, k: stream_chunk(X, t, k),
                           lambda t: pe.wait_ge(*at(f"normed{layer}1", t + 1)), banks=(5, 6, 7))
                pe.wait_ge(*at(f"turn{layer}_evac", TURNED[layer]["gate"] + 6))
                for u in range(6):
                    j, t = u // 3, u % 3
                    t0, rows = TILES[t]
                    if t == 0:
                        ng, sg = item(("ple_g", layer, j))
                        pe.wait_ge(landed[sg], stream.landed[ng])
                        wg = ring[:, sg, :].rearrange("p (k n) -> p k n", k=KD)
                    if u >= 3:
                        pe.wait_ge(*at(f"gated{layer}", u - 2))
                    for k in range(KD):
                        for p0, p1, c0, c1 in pieces(t, 512):
                            ins = pe.matmul(PS[p0:p1, 5 + u % 3, 0:c1 - c0], XT[:, k, t0:t0 + rows], wg[:, k, c0:c1],
                                            start=(k == 0), stop=(k == KD - 1))
                    ins.then_inc(S(f"ple_mm{layer}"), 1)

            router(0)
            positions(0)
            experts(0)
            gated_input(0)

            transposed(1, "tokens", lambda t, k: stream_chunk(X, t, k), lambda t: pe.wait_ge(*at("gated0", 4 + t)))
            pe.wait_ge(*at("turn1_evac", 6))
            project("qkv_mm1", [("b_in", j) for j in range(5)], [512] * 4 + [B_IN - 2048], "qkv_evac1")
            pe.wait_ge(*at("qkv_evac1", 15))
            for t, (t0, n) in enumerate(TILES):
                pe.wait_ge(*at("doubled", t + 1))
                for g in range(KVB):
                    ins = pe.transpose(PS[:, t, g * 128:g * 128 + n],
                                       QKV[0:n, t, DUP_K + g * 128:DUP_K + g * 128 + 128], ident[0:n, 0:n])
                ins.then_inc(S("bt_mm"), 1)
            for t, (t0, n) in enumerate(TILES):
                ins = pe.transpose(PS[:, 3, t0:t0 + n], QKV[0:n, t, DUP_I:DUP_I + 128], ident[0:n, 0:n])
            ins.then_inc(S("bt_mm"), 1)
            for bank, c0, n in ((4, OFF_K, 2), (5, 0, 8), (6, OFF_QI, 4)):
                for k in range(n):
                    ins = pe.transpose(PS[:, bank, k * NS:(k + 1) * NS],
                                       QKV[0:NS, 2, c0 + 128 * k:c0 + 128 * k + 128], ident[0:NS, 0:NS])
                ins.then_inc(S("bt_mm"), 1)
            pe.wait_ge(*at("ws_rows", 4))
            for u in range(4):
                ins = pe.transpose(PS[:, 7, u * NS:(u + 1) * NS], AT[0:NS, u, :], ident[0:NS, 0:NS])
            ins.then_inc(S("bt_mm"), 1)
            pe.wait_ge(*at("bt_evac_act", 6))
            pe.wait_ge(*at("bt_evac_dve", 12))

            for m in range(2):
                query_chunk("pi", m, OFF_QI + m * 128)
            for u in range(8):
                m, qt = u // 2, u % 2
                if qt == 0:
                    pe.wait_ge(*at("pi_evac", m + 1))
                if u >= 2:
                    pe.wait_ge(*at("pi_relu", u - 1))
                for c in range(2):
                    ins = pe.matmul(PS[:, 2 + u % 2, c * 256:c * 256 + 256],
                                    QZ[:, m % 2, c, 128 * qt:128 * qt + 128], KT[:, 4, 0:256], start=True, stop=True)
                ins.then_inc(S("pis_mm"), 1)
                if qt == 1 and m + 2 < 4:
                    query_chunk("pi", m + 2, OFF_QI + (m + 2) * 128)
            pe.wait_ge(*at("pi_relu", 8))

            n, s = item("kidx")
            pe.wait_ge(landed[s], stream.landed[n])
            kx = ring[:, s, :].rearrange("p (r j e) -> p r j e", r=4, j=NPAGE)

            def kidx_turn(r):
                for half in range(2):
                    v = 2 * r + half
                    if v >= 2:
                        pe.wait_ge(*at("kidx_evac", v - 1))
                    for j in range(4):
                        ins = pe.transpose(PS[:, half, j * 128:j * 128 + 128], kx[:, r, 4 * half + j, :], ident)
                    ins.then_inc(S("kidx_mm"), 1)

            def kidx_scores(r):
                pe.wait_ge(*at("kidx_evac", 2 * r + 2))
                if r >= 1:
                    pe.wait_ge(*at("si_relu", r))
                for half in range(2):
                    pe.matmul(PS[:, 2 + half, :], QIB[:, r, :], KIT[:, r % 2, 512 * half:512 * half + 512],
                              start=True, stop=True)
                pe.matmul(PS[:, 4, 0:NS], QIB[:, r, :], KT[:, 4, SEQ:TOK], start=True, stop=True)\
                    .then_inc(S("sis_mm"), 1)

            def kidx_sum(r):
                pe.wait_ge(*at("si_relu", r + 1))
                for p0, bank, w, c0 in ((0, 5, 512, 0), (NS, 5, 512, 512), (0, 6, NS, PAST)):
                    ins = pe.matmul(PS[p0:p0 + NS, bank, 0:w], WS[:, r, :], PR[:, c0:c0 + w],
                                    start=(r == 0), stop=(r == 3))
                ins.then_inc(S("si_sum_mm"), 1)

            kidx_turn(0)
            for r in range(4):
                kidx_scores(r)
                if r < 3:
                    kidx_turn(r + 1)
                kidx_sum(r)

            pe.wait_ge(*at("kidx_evac", 8))
            pe.wait_ge(*at("si_taken", 3))
            prompt_attention(1)
            pe.wait_ge(*at("po1", 16))

            def batch_b(b):
                r, bb = b // 2, b % 2
                n, s = item(("kb", r))
                nv, sv = item(("vb", r))
                if bb == 0:
                    pe.wait_ge(landed[s], stream.landed[n])
                kb = ring[:, s, :].rearrange("p (b j n) -> p b j n", b=2, j=NPAGE)
                vb = ring[:, sv, :].rearrange("p (b j n) -> p b j n", b=2, j=NPAGE)
                for v in range(4):
                    if b >= 1:
                        pe.wait_ge(*at("kbt_evac", 4 * (b - 1) + v + 1))
                    for c in range(2):
                        for j in range(2):
                            ins = pe.transpose(PS[:, v, c * 256 + j * 128:c * 256 + j * 128 + 128],
                                               kb[:, bb, 2 * v + j, c * 128:c * 128 + 128], ident)
                    ins.then_inc(S("kbt_mm"), 1)
                if b == 0:
                    pe.wait_ge(*at("selection", 1))
                if b >= 1:
                    pe.wait_ge(*at("expb_done", b))
                for half in range(2):
                    pe.wait_ge(*at("kbt_evac", 4 * b + 2 * half + 2))
                    for c in range(2):
                        pe.matmul(PS[64 * c:64 * c + 64, 4 + half, :], QBB[:, b, c, :],
                                  KBT[:, c, 512 * half:512 * half + 512], start=True, stop=False)
                    for c in range(2):
                        pe.matmul(PS[64 * c:64 * c + 64, 4 + half, :], spread[:, b, :],
                                  SELB[:, 512 * half:512 * half + 512], start=False, stop=True)
                if b >= 1:
                    pe.wait_ge(*at("ob", 4 * b))
                for c in range(2):
                    pe.matmul(PS[64 * c:64 * c + 64, 6, 0:NS], QBB[:, b, c, :], KT[:, 5 + c, 0:NS], start=True, stop=False)
                for c in range(2):
                    ins = pe.matmul(PS[64 * c:64 * c + 64, 6, 0:NS], spread[:, b, :], SELB[:, PAST:NK],
                                    start=False, stop=True)
                ins.then_inc(S("sb_mm"), 1)
                pe.wait_ge(*at("expb_done", b + 1))
                for u in range(3):
                    for j in range(4 * u, min(4 * u + 4, 9)):
                        keys = min(128, NK - 128 * j)
                        c0 = (j % 4) * 128
                        ins = pe.transpose(PS[0:keys, AT_BANK[u], c0:c0 + 128], PR[:, 128 * j:128 * j + keys], ident)
                    ins.then_inc(S("bat_mm"), 1)
                if bb == 0:
                    pe.wait_ge(landed[sv], stream.landed[nv])
                for j in range(NPAGE + 1):
                    keys = min(128, NK - 128 * j)
                    if j % 4 == 0:
                        pe.wait_ge(*at("bat_evac", b * 3 + (j // 4 + 1)))
                    for c in range(2):
                        v = vb[:, bb, j, c * 128:c * 128 + 128] if j < NPAGE else \
                            QKV[0:NS, 2, OFF_V + c * 128:OFF_V + c * 128 + 128]
                        ins = pe.matmul(PS[64 * c:64 * c + 64, 6, 256:384], AT[0:keys, j, 64 * c:64 * c + 64], v,
                                        start=(j == 0), stop=(j == NPAGE))
                ins.then_inc(S("pvb_mm"), 1)

            for b in range(DB):
                batch_b(b)

            pe.wait_ge(*at("kbt_evac", 4 * DB))
            transposed(1, "outputs", lambda t, k: QKV[:, t, 128 * k:128 * k + 128], lambda t: None, (0, 1))
            pe.wait_ge(*at("ob", 4 * DB))
            for u in range(2):
                for j in range(4):
                    ins = pe.transpose(PS[:, 4 + u, j * 128:j * 128 + 128],
                                       SMF[:, (4 * u + j) * 128:(4 * u + j + 1) * 128], ident)
                ins.then_inc(S("so_t1_mm"), 1)
            pe.wait_ge(*at("turn1_evac", TURNED[1]["outputs"] + 4))
            pe.wait_ge(*at("so_t1_evac", 4))
            project("out_mm1", [("b_out", j) for j in range(2)], [512] * 2, "out_evac1")
            router(1)
            positions(1)
            experts(1)
            gated_input(1)

        @block.scalar
        def _(act):
            def copy(dst, src, sem=None, scale=None):
                ins = act.activation(dst, src, ACT.Copy) if scale is None else \
                    act.activation(dst, src, ACT.Copy, scale=scale)
                if sem is not None:
                    ins.then_inc(S(sem), 1)

            def copy_transposed(layer, stage, dst, tiles=(0, 1, 2), scale=None, banks=(0, 1, 2, 3)):
                first = TURNED[layer][stage]
                for u in range(2 * len(tiles)):
                    t, half = tiles[u // 2], u % 2
                    t0, n = TILES[t]
                    act.wait_ge(*at(f"turn{layer}_mm", first + u + 1))
                    copy(dst[:, 4 * half:4 * half + 4, t0:t0 + n],
                         PS[:, banks[u % len(banks)], :].rearrange("p (j c) -> p j c", j=4)[:, :, 0:n],
                         f"turn{layer}_evac", scale)

            def copy_projection(tag, evac, widths):
                u = 0
                for j, w in enumerate(widths):
                    for t in range(3):
                        act.wait_ge(*at(tag, u + 1))
                        for n, (p0, p1, c0, c1) in enumerate(pieces(t, w)):
                            last = n == len(pieces(t, w)) - 1
                            copy(QKV[0:p1 - p0, t, 512 * j + c0:512 * j + c1], PS[p0:p1, 4 + u % 4, 0:c1 - c0],
                                 evac if last else None)
                        u += 1

            def copy_query_chunk(tag, m):
                act.wait_ge(*at(tag + "_mm", m + 1))
                if m == 0:
                    act.wait_ge(*at(tag + "_zero", 1))
                for c in range(2):
                    copy(QZ[64 * c:64 * c + 64, m % 2, c, :], PS[64 * c:64 * c + 64, m % 2, 0:256],
                         tag + "_evac" if c else None)

            def prompt_attention(layer):
                for m in range(2):
                    copy_query_chunk(f"pq{layer}", m)
                for u in range(17):
                    if u < 16:
                        kw = 128 * (u % 2 + 1)
                        act.wait_ge(*at(f"pmax{layer}", u + 1))
                        for c in range(2):
                            ins = act.activation(SM[:, u % 2, c * 256:c * 256 + kw], SM[:, u % 2, c * 256:c * 256 + kw],
                                                 ACT.Exp, bias=NMAX[:, 2 * (u % 2) + c:2 * (u % 2) + c + 1],
                                                 accum_out=SUMS[:, 2 * (u % 2) + c:2 * (u % 2) + c + 1])
                        ins.then_inc(S(f"pexp{layer}"), 1)
                        if u % 2 == 1 and u // 2 + 2 < 8:
                            copy_query_chunk(f"pq{layer}", u // 2 + 2)
                    if u >= 1:
                        v = u - 1
                        act.wait_ge(*at(f"pat{layer}_mm", v + 1))
                        kw = 128 * (v % 2 + 1)
                        if layer == 0:
                            copy(ATP[:, v % 2, 0, 0:kw], PS[:, 4 + v % 2, 0:kw], "pat0_evac")
                        else:
                            copy(ATP[:, v % 2, :, 0:kw],
                                 PS[:, 4 + v % 2, :].rearrange("p (c k) -> p c k", c=2)[:, :, 0:kw], "pat1_evac")

            copy_transposed(0, "tokens", XT)
            copy_projection("qkv_mm0", "qkv_evac0", [512] * 6)
            copy_transposed(0, "keys", KT)
            act.wait_ge(*at("lam_sums", 1))
            act.activation(small[:, 4:6], small[:, 6:8], ACT.Exp).then_inc(S("lam_exp"), 1)
            prompt_attention(0)

            def batch_a(b, par):
                for j in range(NPAGE):
                    act.wait_ge(*at("kt_page_mm", b * 16 + (2 * j + 1)))
                    act.wait_ge(*at("score_mm", b * 9 + (max(j - 1, 0) + 1)))
                    copy(KPG[:, j % 2, 0:4, :], PS[:, (2 * j) % 4, :].rearrange("p (k n) -> p k n", k=4), "kt_evac_act")
                act.wait_ge(*at("row_max", b + 1))
                act.activation(PR[:, :], PSF[:, 2048:2048 + NK], ACT.Exp, bias=NMAX[:, par:par + 1], scale=SCALE,
                               accum_out=SUMS[:, par:par + 1]).then_inc(S("exp_done"), 1)
                for u in range(3):
                    act.wait_ge(*at("at_mm", b * 3 + (u + 1)))
                    keys, m = (128, 4) if u < 2 else (NS, 1)
                    copy(AT[0:keys, 4 * u:4 * u + m, :],
                         PS[0:keys, AT_BANK[u], 0:128 * m].rearrange("p (j r) -> p j r", j=m),
                         "at_evac")

            act.wait_ge(*at("po0_mm", 16))
            act.sem_inc(S("kt_evac_act"), 2)
            act.sem_inc(S("exp_done"), 1)
            with act.Fori(0, DB // 2) as i:
                batch_a(i * 2, 0)
                batch_a(i * 2 + 1, 1)
            act.wait_ge(*at("o_squares", 2))
            act.activation(RMS[:, 0:32], RMS[:, 0:32], ACT.Sqrt, bias=cst("eps"), scale=1.0 / 128)\
               .then_inc(S("o_root"), 1)
            copy_transposed(0, "outputs", XT, (0, 1), small[:, 3:4])
            for u in range(4):
                act.wait_ge(*at("so_t0_mm", u + 1))
                for hp in range(2):
                    src = PS[:, 4 + u, :].rearrange("p (b c t r) -> p b c t r", b=2, c=2, t=4)[:, :, hp, :, 8 * hp:8 * hp + 8]
                    dst = XT[:, hp::2, SEQ + 16 * u:SEQ + 16 * u + 16].rearrange("p t (b q) -> p b t q", b=2)
                    copy(dst, src, "so_t0_evac", small[:, 3:4])

            def norm_root(layer, which):
                for t in range(3):
                    act.wait_ge(*at(f"var{layer}{which}", t + 1))
                    act.activation(RSTD[:, t:t + 1], MV[:, t, 1:2], ACT.Sqrt, bias=cst("eps"), scale=1.0)\
                       .then_inc(S(f"std{layer}{which}"), 1)

            def experts(layer):
                copy_transposed(layer, "router", XT)
                act.wait_ge(*at(f"logit_mm{layer}", 1))
                act.wait_ge(*at(f"aff_ones{layer}", 1))
                act.activation(G[:, 0, 0:32], PS[:, 4, 0:32], ACT.Sigmoid)
                act.activation(G[0:NS, 0, 32:48], PS[0:NS, 4, 32:48], ACT.Sigmoid).then_inc(S(f"aff{layer}"), 1)
                act.wait_ge(*at(f"pt_mm{layer}", 1))
                copy(PT, PS[:, 5:7, 0:TOK], f"pt_evac{layer}")
                act.wait_ge(*at(f"dispatch_ready{layer}", 1))
                most = act.value_load(COUNT[0:1, NE:NE + 1], min_val=0, max_val=TOK)
                with act.If(most > 128):
                    for name in ("rows_evac", "second_evac", "xe_evac", "sp_sig", "sp_ht_evac", "sp_y_act", "sp_y_a_stored", "sp_y_b_stored"):
                        act.sem_inc(S(f"{name}{layer}"), PER_LAYER[name + "#"])
                    experts_dense(layer)
                with act.Else():
                    for name in ("ht_evac", "sig"):
                        act.sem_inc(S(f"{name}{layer}"), PER_LAYER[name + "#"])
                    experts_sparse(layer)
                act.nop()

            def experts_sparse(layer):
                def copy_turned(first, sem):
                    copy(XE[:, :, first:first + 64].rearrange("p (h k) c -> p k h c", h=2),
                         PS[:, 5, :].rearrange("p (k h c) -> p k h c", k=4, h=2), sem)

                def expert(i, par, e, m):
                    if m == 128:
                        act.wait_ge(*at(f"second_mm{layer}", e * 2 + 1))
                        copy(XR, PS[:, 4, :], f"second_evac{layer}")
                        act.wait_ge(*at(f"second_mm{layer}", e * 2 + 2))
                        copy_turned(64, f"second_evac{layer}")
                    else:
                        act.sem_inc(S(f"second_evac{layer}"), 2)
                    act.wait_ge(*at(f"sp_gate_up_mm{layer}", e + 1))
                    act.activation(MSG[0:m, 0, :], PS[0:m, 0, :], ACT.Sigmoid).then_inc(S(f"sp_sig{layer}"), 1)
                    act.wait_ge(*at(f"rows_mm{layer}", e + 2))
                    copy(XR, PS[:, 4, :], f"rows_evac{layer}")
                    act.wait_ge(*at(f"sp_ht_mm{layer}", e + 1))
                    copy(MHT[:, 0, :, 0:m], PS[:, 2, :].rearrange("p (k c) -> p k c", k=FK)[:, :, 0:m],
                         f"sp_ht_evac{layer}")
                    act.wait_ge(*at(f"xe_mm{layer}", e + 2))
                    copy_turned(0, f"xe_evac{layer}")
                    act.wait_ge(*at(f"sp_y_mm{layer}", e + 1))
                    act.wait_ge(*at(f"sp_y_{'ab'[par]}_stored{layer}", i * 16 + 16))
                    copy(YS[par][0:m, 0:512], PS[0:m, 6, :], f"sp_y_act{layer}")
                    act.wait_ge(*at(f"sp_y_act{layer}", e + 2))
                    act.wait_ge(*at(f"sp_y_dve{layer}", e + 2))
                    act.dma_start(places[bass.ds(e * 128, m), :], YS[par][0:m, :])\
                       .then_inc(S(f"sp_y_{'ab'[par]}_stored{layer}"), 16)

                act.wait_ge(*at(f"rows_mm{layer}", 1))
                copy(XR, PS[:, 4, :], f"rows_evac{layer}")
                act.wait_ge(*at(f"xe_mm{layer}", 1))
                copy_turned(0, f"xe_evac{layer}")
                act.sem_inc(S(f"sp_y_act{layer}"), 1)
                for ab in "ab":
                    act.sem_inc(S(f"sp_y_{ab}_stored{layer}"), 16)
                with act.Fori(0, NE // 2) as i:
                    for par in range(2):
                        e = i * 2 + par
                        big = act.value_load(COUNT[0:1, bass.ds(e, 1)], min_val=0, max_val=TOK)
                        with act.If(big > 64):
                            expert(i, par, e, 128)
                        with act.Else():
                            expert(i, par, e, 64)
                        act.nop()

            def experts_dense(layer):
                act.wait_ge(*at(f"acc_zero{layer}", 1))
                act.sem_inc(S(f"ht_evac{layer}"), 2)
                with act.Fori(0, NE // 2) as i:
                    for u in range(7):
                        if u < 6:
                            n = TILES[u % 3][1]
                            act.wait_ge(*at(f"gate_up_mm{layer}", i * 6 + (u + 1)))
                            act.activation(MSG[0:n, u % 2, :], PS[0:n, 2 * (u % 2), :], ACT.Sigmoid)\
                               .then_inc(S(f"sig{layer}"), 1)
                        if u >= 1:
                            v = u - 1
                            n = TILES[v % 3][1]
                            act.wait_ge(*at(f"ht_mm{layer}", i * 6 + (v + 1)))
                            copy(MHT[:, v % 2, :, 0:n], PS[:, 4 + v % 2, :].rearrange("p (k c) -> p k c", k=FK)[:, :, 0:n],
                                 f"ht_evac{layer}")

            def gated_input(layer):
                copy_transposed(layer, "gate", XT, banks=(5, 6, 7))
                for u in range(6):
                    n = TILES[u % 3][1]
                    act.wait_ge(*at(f"gate_biased{layer}", u + 1))
                    act.activation(MSG[0:n, u % 2, :], MSG[0:n, u % 2, :], ACT.Sigmoid).then_inc(S(f"gate_sig{layer}"), 1)

            norm_root(0, 0)
            experts(0)
            norm_root(0, 1)
            gated_input(0)

            copy_transposed(1, "tokens", XT)
            copy_projection("qkv_mm1", "qkv_evac1", [512] * 4 + [B_IN - 2048])
            for t, (t0, n) in enumerate(TILES):
                act.wait_ge(*at("bt_mm", t + 1))
                copy(KT[:, 0:4, t0:t0 + n], PS[:, t, :].rearrange("p (g c) -> p g c", g=4)[:, :, 0:n], "bt_evac_act")
            act.wait_ge(*at("bt_mm", 4))
            copy(KT[:, 4, :], PS[:, 3, 0:TOK], "bt_evac_act")
            act.wait_ge(*at("bt_mm", 5))
            copy(KT[:, 5:7, 0:NS], PS[:, 4, 0:2 * NS].rearrange("p (c n) -> p c n", c=2), "bt_evac_act")
            act.wait_ge(*at("bt_mm", 8))
            act.wait_ge(*at("bt_evac_dve", 12))
            copy(WS, PS[:, 7, 0:4 * NS].rearrange("p (u n) -> p u n", u=4), "bt_evac_act")
            for m in range(2):
                copy_query_chunk("pi", m)
            for u in range(8):
                act.wait_ge(*at("pis_mm", u + 1))
                if u >= 2:
                    act.wait_ge(*at("pi_added", u - 1))
                act.activation(SM[:, u % 2, :], PS[:, 2 + u % 2, :], ACT.Relu).then_inc(S("pi_relu"), 1)
                if u % 2 == 1 and u // 2 + 2 < 4:
                    copy_query_chunk("pi", u // 2 + 2)
            for r in range(4):
                for half in range(2):
                    act.wait_ge(*at("kidx_mm", 2 * r + half + 1))
                    if r >= 2 and half == 0:
                        act.wait_ge(*at("sis_mm", r - 1))
                    copy(KIT[:, r % 2, 512 * half:512 * half + 512], PS[:, half, :], "kidx_evac")
                act.wait_ge(*at("sis_mm", r + 1))
                if r >= 1:
                    act.wait_ge(*at("si_sum_mm", r))
                act.activation(PR[:, :], PSF[:, 1024:1024 + NK], ACT.Relu).then_inc(S("si_relu"), 1)
            prompt_attention(1)
            for b in range(DB):
                for v in range(4):
                    act.wait_ge(*at("kbt_mm", 4 * b + v + 1))
                    if b >= 1 and v == 0:
                        act.wait_ge(*at("sb_mm", b))
                    copy(KBT[:, :, 256 * v:256 * v + 256], PS[:, v, :].rearrange("p (c n) -> p c n", c=2), "kbt_evac")
                act.wait_ge(*at("row_maxb", b + 1))
                act.activation(PR[:, :], PSF[:, 2048:2048 + NK], ACT.Exp, bias=NMAX[:, b % 2:b % 2 + 1], scale=SCALE,
                               accum_out=SUMS[:, b % 2:b % 2 + 1]).then_inc(S("expb_done"), 1)
                for u in range(3):
                    act.wait_ge(*at("bat_mm", b * 3 + u + 1))
                    keys, m = (128, 4) if u < 2 else (NS, 1)
                    copy(AT[0:keys, 4 * u:4 * u + m, :],
                         PS[0:keys, AT_BANK[u], 0:128 * m].rearrange("p (j r) -> p j r", j=m),
                         "bat_evac")
            copy_transposed(1, "outputs", XT, (0, 1))
            for u in range(2):
                act.wait_ge(*at("so_t1_mm", u + 1))
                for hp in range(2):
                    src = PS[64 * hp:64 * hp + 64, 4 + u, :].rearrange("p (b h c q) -> p b h c q", b=4, h=8, c=2)[:, :, :, hp, :]
                    for bb in range(4):
                        b = 4 * u + bb
                        copy(XT[64 * hp:64 * hp + 64, :, SEQ + 8 * b:SEQ + 8 * b + 8], src[:, bb],
                             "so_t1_evac" if bb == 3 else None)
            norm_root(1, 0)
            experts(1)
            norm_root(1, 1)
            gated_input(1)

        @block.vector
        def _(ve):
            chain = {"name": "vector_chain", "n": 0, "i": None, "per": 0}

            def link(ins):
                chain["n"] += 1
                ins.then_inc(S(chain["name"]), 1)
                ve.wait_ge(*at(chain["name"], chain["n"] if chain["i"] is None else
                               chain["i"] * chain["per"] + chain["n"]))

            def loop(i, per):
                chain.update(i=i, per=per, start=chain["n"])

            def loop_end(count):
                assert chain["n"] - chain["start"] == chain["per"], chain
                chain["n"] = chain["start"] + count * chain["per"]
                chain["i"] = None

            def rotate(t, c0, heads, half, cos, sin, tag):
                n = TILES[t][1]
                rot = 2 * half
                x = QKV[0:n, t, c0:c0 + heads * HD].rearrange("p (h d) -> p h d", h=heads)
                x4 = x[:, :, 0:rot].rearrange("p h (u f) -> p h u f", u=2)
                cs = cst(cos)[0:n, t * half:(t + 1) * half].unsqueeze(1).unsqueeze(1).to_broadcast([n, heads, 2, half])
                sn = cst(sin)[0:n, t * half:(t + 1) * half].unsqueeze(1).to_broadcast([n, heads, half])
                t1 = PR[0:n, 0:heads * rot].rearrange("p (h u f) -> p h u f", h=heads, u=2)
                t2 = PR[0:n, 512:512 + heads * rot].rearrange("p (h u f) -> p h u f", h=heads, u=2)
                ve.tensor_tensor(t2[:, :, 0, :], x4[:, :, 1, :], sn, ALU.mult)
                ve.tensor_tensor(t2[:, :, 1, :], x4[:, :, 0, :], sn, ALU.mult)
                link(ve.tensor_tensor(t1, x4, cs, ALU.mult))
                ve.tensor_tensor(x4[:, :, 0, :], t1[:, :, 0, :], t2[:, :, 0, :], ALU.subtract)
                ins = ve.tensor_tensor(x4[:, :, 1, :], t1[:, :, 1, :], t2[:, :, 1, :], ALU.add)
                if tag:
                    ins.then_inc(S(tag), 1)
                else:
                    link(ins)

            def prompt_attention(layer, between=lambda: None):
                def scores(u):
                    qt = u % 2
                    kw = 128 * (qt + 1)
                    ve.wait_ge(*at(f"ps{layer}_mm", u + 1))
                    if u >= 2:
                        ve.wait_ge(*at(f"pat{layer}_mm", u - 1))
                    s3 = PS[:, 2 + u % 2, :].rearrange("p (c k) -> p c k", c=2)[:, :, 0:kw]
                    m3 = SM[:, u % 2, :].rearrange("p (c k) -> p c k", c=2)[:, :, 0:kw]
                    bias = (causal if layer == 0 else PB)[:, qt, 0:kw].unsqueeze(1).to_broadcast([P, 2, kw])
                    ve.scalar_tensor_tensor(m3, s3, SCALE, bias, ALU.mult, ALU.add).then_inc(S(f"pmask{layer}"), 1)
                    ve.wait_ge(*at(f"pmask{layer}", u + 1))
                    ve.tensor_reduce(NMAX[:, 2 * (u % 2):2 * (u % 2) + 2], m3, AX.X, ALU.max, negate=True)\
                      .then_inc(S(f"pmax{layer}"), 1)

                def weights(u):
                    kw = 128 * (u % 2 + 1)
                    ve.wait_ge(*at(f"pexp{layer}", u + 1))
                    rc = RC[:, 2 * (u % 2):2 * (u % 2) + 2]
                    link(ve.reciprocal(rc, SUMS[:, 2 * (u % 2):2 * (u % 2) + 2]))
                    p0, p1 = SM[:, u % 2, 0:kw], SM[:, u % 2, 256:256 + kw]
                    if layer == 0:
                        link(ve.tensor_tensor(rc[:, 1:2], rc[:, 1:2], NLAM, ALU.mult))
                        link(ve.tensor_scalar(p0, p0, rc[:, 0:1], None, ALU.mult))
                        ve.scalar_tensor_tensor(p0, p1, rc[:, 1:2], p0, ALU.mult, ALU.add).then_inc(S("pw0"), 1)
                    else:
                        ve.tensor_scalar(p0, p0, rc[:, 0:1], None, ALU.mult)
                        ve.tensor_scalar(p1, p1, rc[:, 1:2], None, ALU.mult).then_inc(S("pw1"), 1)

                def outputs(u):
                    m, qt = u // 2, u % 2
                    ve.wait_ge(*at(f"po{layer}_mm", u + 1))
                    ve.tensor_copy(QKV[:, qt, 128 * m:128 * m + 128], PS[:, 6 + u % 2, 0:128]).then_inc(S(f"po{layer}"), 1)

                for u in range(18):
                    if u < 16:
                        scores(u)
                        between()
                        weights(u)
                        between()
                    if u >= 2:
                        outputs(u - 2)

            link(ve.memset(small[:, 8:160], 1.0))
            link(ve.memset(X[NS:P, 2, :], 0.0))
            ve.memset(QB[:, :], 0.0).then_inc(S("qb_zero"), 1)
            ve.memset(KP[:, 0:1024], 0.0).then_inc(S("pq0_zero"), 1)
            ve.wait_ge(*at("const_landed", 16))
            ve.wait_ge(*at("lam_landed", 80))
            link(ve.tensor_scalar(small[:, 3:4], SUBLN, OUT_GAIN, None, ALU.mult))
            l2 = OR[:, 256:384].rearrange("p (m d) -> p m d", m=2)
            link(ve.tensor_tensor(l2, lamt[:, 0::2, :], lamt[:, 1::2, :], ALU.mult))
            ve.tensor_reduce(small[:, 6:8], l2, AX.X, ALU.add).then_inc(S("lam_sums"), 1)
            for t in range(3):
                ve.wait_ge(*at("qkv_evac0", 9 + t + 1))
                if t:
                    ve.wait_ge(*at("rotated0", t))
                rotate(t, 0, 32, 8, "cosA", "sinA", "rotated0")
            ve.wait_ge(*at("lam_exp", 1))
            link(ve.tensor_tensor(NLAM, small[:, 5:6], small[:, 4:5], ALU.subtract))
            link(ve.tensor_scalar(NLAM, NLAM, -LAM_INIT, None, ALU.add))
            link(ve.scalar_tensor_tensor(SGN, cst("c1"), NLAM, cst("c0"), ALU.mult, ALU.add))
            ve.wait_ge(*at("qb0_mm", 1))
            ve.wait_ge(*at("qb_zero", 1))
            for c in range(2):
                for hp in range(2):
                    src = PS[64 * c:64 * c + 64, 0, :].rearrange("p (t h b q) -> p t h b q", t=4, h=2, b=DB)[:, :, hp]
                    dst = QBA[64 * c:64 * c + 64, :, hp::2, hp * 16 + c * 8:hp * 16 + c * 8 + 8]\
                        .rearrange("p b t q -> p t b q")
                    ve.tensor_copy(dst, src).then_inc(S("qb0"), 1)
            ve.memset(OR[:, :], 0.0).then_inc(S("or_cleared"), 1)
            prompt_attention(0)

            def batch_a(b, par):
                ve.tensor_copy(QCUR[:, par].rearrange("p h r -> p (h r)"), QB[:, bass.ds(b * 256, 256)])\
                  .then_inc(S("qcur"), 1)
                for j in range(NPAGE):
                    ve.wait_ge(*at("kt_page_mm", b * 16 + (2 * j + 2)))
                    ve.wait_ge(*at("score_mm", b * 9 + (max(j - 1, 0) + 1)))
                    ve.tensor_copy(KPG[:, j % 2, 4:8, :], PS[:, (2 * j + 1) % 4, :].rearrange("p (k n) -> p k n", k=4))\
                      .then_inc(S("kt_evac_dve"), 1)
                ve.wait_ge(*at("score_mm", b * 9 + 10))
                a0 = CONST["newmask"][0]
                link(ve.tensor_tensor(PS[:, 6, 0:NS], PS[:, 6, 0:NS], C[:, bass.ds(b * NS + a0, NS)], ALU.add))
                link(ve.tensor_reduce(small[:, 4:5], PSF[:, 2048:2048 + NK], AX.X, ALU.max))
                ve.tensor_scalar(NMAX[:, par:par + 1], small[:, 4:5], -SCALE, None, ALU.mult).then_inc(S("row_max"), 1)
                ve.wait_ge(*at("exp_done", b + 2))
                link(ve.reciprocal(RC[:, par:par + 1], SUMS[:, par:par + 1]))
                link(ve.tensor_tensor(RC[:, par:par + 1], RC[:, par:par + 1], SGN, ALU.mult))
                ve.tensor_scalar(FOLD[:, par, :], cst("fold"), RC[:, par:par + 1], None, ALU.mult)\
                  .then_inc(S("fold_ready"), 1)
                ve.wait_ge(*at("pv_mm", b + 1))
                ve.tensor_copy(OR[:, bass.ds(b * 256, 256)], PS[:, 6, 256:512]).then_inc(S("o_evac"), 1)

            ve.wait_ge(*at("po0_mm", 16))
            ve.wait_ge(*at("places_zeroed", 128))
            ve.sem_inc(S("kt_evac_dve"), 2)
            ve.sem_inc(S("o_evac"), 1)
            with ve.Fori(0, DB // 2) as i:
                loop(i, 8)
                batch_a(i * 2, 0)
                batch_a(i * 2 + 1, 1)
            loop_end(DB // 2)

            for t in range(2):
                o = QKV[:, t, 0:D]
                ve.wait_ge(*at("pv_mm", DB)) if t == 0 else None
                link(ve.tensor_tensor(SMF, o, o, ALU.mult))
                link(ve.tensor_reduce(RMS[:, 8 * t:8 * t + 8], SMF.rearrange("p (h d) -> p h d", h=8), AX.X, ALU.add))
            ve.wait_ge(*at("o_evac", DB + 1))
            for t in range(2):
                o = OR[:, D * t:D * t + D]
                link(ve.tensor_tensor(SMF, o, o, ALU.mult))
                ve.tensor_reduce(RMS[:, 16 + 8 * t:24 + 8 * t], SMF.rearrange("p (h d) -> p h d", h=8), AX.X, ALU.add)\
                  .then_inc(S("o_squares"), 1)
                ve.wait_ge(*at("o_squares", t + 1))
            ve.wait_ge(*at("o_root", 1))
            link(ve.reciprocal(RMS[:, 0:32], RMS[:, 0:32]))
            for t in range(4):
                o = (QKV[:, t, 0:D] if t < 2 else OR[:, D * (t - 2):D * (t - 1)]).rearrange("p (h d) -> p h d", h=8)
                ins = ve.tensor_tensor(o, o, RMS[:, 8 * t:8 * t + 8].unsqueeze(2).to_broadcast([P, 8, 128]), ALU.mult)
                if t == 3:
                    ins.then_inc(S("or_normed"), 1)
                else:
                    link(ins)

            def residual(layer):
                def part(j, t):
                    u = 3 * j + t
                    ve.wait_ge(*at(f"out_mm{layer}", u + 1))
                    for p0, p1, c0, c1 in pieces(t, 512):
                        x = X[0:p1 - p0, t, 512 * j + c0:512 * j + c1]
                        ins = ve.scalar_tensor_tensor(x, x, ALPHA, PS[p0:p1, 4 + u % 4, 0:c1 - c0], ALU.mult, ALU.add)
                    ins.then_inc(S(f"out_evac{layer}"), 1)

                def tile(t):
                    part(1, t)
                    ve.wait_ge(*at(f"out_evac{layer}", t + 4))

                for t in range(3):
                    part(0, t)
                return tile

            def norm(layer, which, prepare):
                for u in range(4):
                    if u < 3:
                        t, n = u, TILES[u][1]
                        prepare(t)
                        for half in range(2):
                            ins = ve.bn_stats(STATS[0:n, t, 6 * half:6 * half + 6], X[0:n, t, 512 * half:512 * half + 512])
                        link(ins)
                        ve.bn_aggr(MV[0:n, t, :], STATS[0:n, t, :]).then_inc(S(f"var{layer}{which}"), 1)
                    if u >= 1:
                        t, n = u - 1, TILES[u - 1][1]
                        x = X[0:n, t, :]
                        ve.wait_ge(*at(f"std{layer}{which}", u))
                        link(ve.reciprocal(RSTD[:, t:t + 1], RSTD[:, t:t + 1]))
                        link(ve.tensor_scalar(x, x, MV[0:n, t, 0:1], RSTD[0:n, t:t + 1], ALU.subtract, ALU.mult))
                        ve.wait_ge(*at(f"norm_landed{layer}{which}", 32))
                        link(ve.tensor_tensor(x, x, GAIN[0:n], ALU.mult))
                        ve.tensor_tensor(x, x, SHIFT[0:n], ALU.add).then_inc(S(f"normed{layer}{which}"), 1)
                ve.wait_ge(*at(f"normed{layer}{which}", 3))

            def experts(layer):
                g3 = lambda m: G[:, m, 0:48].rearrange("p (t e) -> p t e", t=3)
                g12 = lambda m, w=12: G[:, m, 0:w]
                ve.memset(G[:, 0, :], 1.0).then_inc(S(f"aff_ones{layer}"), 1)
                ve.wait_ge(*at("stored", 96 if layer == 0 else 96 + 144))
                ve.wait_ge(*at(f"aff{layer}", 1))
                ve.wait_ge(*at("router_b_landed", 16))
                link(ve.tensor_tensor(g3(1), g3(0), G[:, 13, 0:NE].unsqueeze(1).to_broadcast([P, 3, NE]), ALU.add))
                s4 = G[:, 1, :].rearrange("p (g e) -> p g e", g=12)
                hi = G[:, 2, 0:24].rearrange("p (g e) -> p g e", g=12)
                lo = G[:, 2, 24:48].rearrange("p (g e) -> p g e", g=12)
                ve.tensor_tensor(hi, s4[:, :, 0::2], s4[:, :, 1::2], ALU.max)
                link(ve.tensor_tensor(lo, s4[:, :, 0::2], s4[:, :, 1::2], ALU.min))
                top, second, third = G[:, 3, 0:12], G[:, 3, 12:24], G[:, 3, 24:36]
                ve.tensor_tensor(top, hi[:, :, 0], hi[:, :, 1], ALU.max)
                ve.tensor_tensor(second, hi[:, :, 0], hi[:, :, 1], ALU.min)
                link(ve.tensor_tensor(third, lo[:, :, 0], lo[:, :, 1], ALU.max))
                link(ve.tensor_tensor(second, second, third, ALU.max))
                link(ve.tensor_tensor(top, top, second, ALU.add))

                def first_of_max(values, code, mx, out, w):
                    link(ve.tensor_reduce(mx, values, AX.X, ALU.max))
                    link(ve.tensor_tensor(out, values, mx.unsqueeze(2).to_broadcast([P, 3, w]), ALU.is_equal))
                    link(ve.tensor_tensor(out, out, code, ALU.mult))
                    link(ve.tensor_reduce(mx, out, AX.X, ALU.max))
                    link(ve.tensor_tensor(out, out, mx.unsqueeze(2).to_broadcast([P, 3, w]), ALU.is_equal))

                mx = G[:, 12, 0:3]
                grp = G[:, 4, 0:12]
                first_of_max(top.rearrange("p (t g) -> p t g", t=3), cst("grpcode").rearrange("p (t g) -> p t g", t=3), mx,
                             grp.rearrange("p (t g) -> p t g", t=3), NG)
                link(ve.tensor_scalar(G[:, 4, 12:24], grp, -1.0, BIG, ALU.add, ALU.mult))
                sel4 = G[:, 5, :].rearrange("p (g e) -> p g e", g=12)
                link(ve.tensor_tensor(sel4, s4, grp.unsqueeze(2).to_broadcast([P, 12, EG]), ALU.mult))
                link(ve.tensor_tensor(sel4, sel4, G[:, 4, 12:24].unsqueeze(2).to_broadcast([P, 12, EG]), ALU.add))
                code = cst("expcode").rearrange("p (t e) -> p t e", t=3)
                first_of_max(g3(5), code, mx, g3(6), NE)
                link(ve.scalar_tensor_tensor(g3(5), g3(6), -3.0 * BIG, g3(5), ALU.mult, ALU.add))
                first_of_max(g3(5), code, mx, g3(7), NE)
                link(ve.tensor_tensor(g3(8), g3(6), g3(7), ALU.add))
                link(ve.tensor_tensor(g3(9), g3(8), g3(0), ALU.mult))
                link(ve.tensor_reduce(mx, g3(9), AX.X, ALU.add))
                link(ve.reciprocal(mx, mx))
                link(ve.tensor_tensor(g3(10), g3(9), mx.unsqueeze(2).to_broadcast([P, 3, NE]), ALU.mult))
                ve.memset(G[NS:P, 8, 32:48], 0.0).then_inc(S(f"mask_ready{layer}"), 1)
                link(ve.memset(MH[:, 0, :], 0.0))
                link(ve.memset(WHERE[:, 3 * NE:], -1.0))
                t0, t1 = g3(1), g3(2)
                for rank in range(2):
                    link(ve.tensor_tensor(t0, g3(6 + rank), g3(10), ALU.mult))
                    link(ve.tensor_reduce(GATES[:, rank, :], t0, AX.X, ALU.add))
                ve.wait_ge(*at(f"pos_mm{layer}", 1))
                link(ve.scalar_tensor_tensor(t1, PS[:, 3, 0:48].rearrange("p (t e) -> p t e", t=3), 1.0, g3(8),
                                             ALU.add, ALU.mult))
                link(ve.tensor_scalar(WHERE[:, 0:3 * NE].rearrange("p (e t) -> p t e", t=3), t1, -1.0, None, ALU.add))
                link(ve.tensor_tensor(t0, PS[:, 3, 0:48].rearrange("p (t e) -> p t e", t=3),
                                      cst("slotbase").rearrange("p (t e) -> p t e", t=3), ALU.add))
                for rank in range(2):
                    link(ve.tensor_tensor(t1, t0, g3(6 + rank), ALU.mult))
                    link(ve.tensor_reduce(mx, t1, AX.X, ALU.add))
                    link(ve.tensor_copy(IDX[:, 3 * rank:3 * rank + 3], mx))
                link(ve.tensor_reduce(G[0:1, 11, 0:1], PS[0:1, 3, 48:48 + NE], AX.X, ALU.max))
                link(ve.tensor_copy(COUNT[0:1, 0:NE], PS[0:1, 3, 48:48 + NE]))
                ve.tensor_copy(COUNT[0:1, NE:NE + 1], G[0:1, 11, 0:1]).then_inc(S(f"dispatch_ready{layer}"), 1)
                ve.wait_ge(*at(f"dispatch_ready{layer}", 1))
                most = ve.value_load(COUNT[0:1, NE:NE + 1], min_val=0, max_val=TOK)
                outer = dict(chain)
                with ve.If(most > 128):
                    for name in ("sel_ready", "sp_hidden", "sp_y_dve", "chain_sparse"):
                        ve.sem_inc(S(f"{name}{layer}"), PER_LAYER[name + "#"])
                    chain.update(name=f"chain_dense{layer}", n=0)
                    experts_dense(layer)
                    assert chain["n"] == PER_LAYER["chain_dense#"], chain
                with ve.Else():
                    for name in ("h_ready", "y_used", "chain_dense", "acc_zero"):
                        ve.sem_inc(S(f"{name}{layer}"), PER_LAYER[name + "#"])
                    chain.update(name=f"chain_sparse{layer}", n=0)
                    experts_sparse(layer)
                    assert chain["n"] == PER_LAYER["chain_sparse#"], chain
                chain.update(outer)
                ve.nop()
                return lambda t: None

            def experts_sparse(layer):
                def select(e, par):
                    ve.tensor_tensor(SEL[:, par], cst("place").unsqueeze(1).to_broadcast([P, 3, 128]),
                                     WHERE[:, bass.ds(e * 3, 3)].unsqueeze(2).to_broadcast([P, 3, 128]),
                                     ALU.is_equal).then_inc(S(f"sel_ready{layer}"), 1)

                def expert(i, par, e, m):
                    p1 = 0 if m == 128 else 64
                    select(e + 1, 1 - par)
                    ve.wait_ge(*at(f"sp_sig{layer}", e + 1))
                    link(ve.tensor_tensor(MSG[0:m, 0, :], MSG[0:m, 0, :], PS[0:m, 0, :], ALU.mult))
                    ve.tensor_tensor(MH[0:m, 0, :], MSG[0:m, 0, :], PS[p1:p1 + m, 1, :], ALU.mult)\
                      .then_inc(S(f"sp_hidden{layer}"), 1)
                    ve.wait_ge(*at(f"sp_y_mm{layer}", e + 1))
                    ve.wait_ge(*at(f"sp_y_{'ab'[par]}_stored{layer}", i * 16 + 16))
                    ve.tensor_copy(YS[par][0:m, 512:1024], PS[p1:p1 + m, 7, :]).then_inc(S(f"sp_y_dve{layer}"), 1)

                select(0, 0)
                ve.sem_inc(S(f"sp_y_dve{layer}"), 1)
                with ve.Fori(0, NE // 2) as i:
                    loop(i, 2)
                    for par in range(2):
                        e = i * 2 + par
                        big = ve.value_load(COUNT[0:1, bass.ds(e, 1)], min_val=0, max_val=TOK)
                        n = chain["n"]
                        with ve.If(big > 64):
                            expert(i, par, e, 128)
                        chain["n"] = n
                        with ve.Else():
                            expert(i, par, e, 64)
                        ve.nop()
                loop_end(NE // 2)
                for t, (t0, n) in enumerate(TILES):
                    link(ve.tensor_scalar(X[0:n, t, :], X[0:n, t, :], ALPHA, None, ALU.mult))
                for t, (t0, n) in enumerate(TILES):
                    x = X[0:n, t, :]
                    ve.wait_ge(*at(f"tile{t}_moved{layer}", 32))
                    for rank in range(2):
                        link(ve.scalar_tensor_tensor(x, YG[0:n, rank, t, :], GATES[0:n, rank, t:t + 1], x,
                                                     ALU.mult, ALU.add))

            def experts_dense(layer):
                ve.memset(ACC, 0.0).then_inc(S(f"acc_zero{layer}"), 1)
                ve.wait_ge(*at(f"acc_zero{layer}", 1))
                ve.sem_inc(S(f"h_ready{layer}"), 2)
                ve.sem_inc(S(f"y_used{layer}"), 1)
                with ve.Fori(0, NE // 2) as i:
                    loop(i, 6 + 4 + 2)
                    for u in range(7):
                        if u < 6:
                            t = u % 3
                            n = TILES[t][1]
                            p0 = 0 if t < 2 else NS
                            ve.wait_ge(*at(f"sig{layer}", i * 6 + (u + 1)))
                            sg, b0 = MSG[0:n, u % 2, :], 2 * (u % 2)
                            link(ve.tensor_tensor(sg, sg, PS[0:n, b0, :], ALU.mult))
                            ve.tensor_tensor(MH[0:n, u % 2, :], sg, PS[p0:p0 + n, b0 + 1, :], ALU.mult)\
                              .then_inc(S(f"h_ready{layer}"), 1)
                        if u >= 1:
                            v = u - 1
                            t = v % 3
                            n = TILES[t][1]
                            ve.wait_ge(*at(f"y_mm{layer}", i * 6 + (v + 1)))
                            comb = G[0:n, 10, bass.ds(i * 2 + (t * NE + v // 3), 1)]
                            for half in range(2):
                                p0 = 0 if t < 2 or half == 0 else NS
                                acc = ACC[0:n, t, 512 * half:512 * half + 512]
                                ins = ve.scalar_tensor_tensor(acc, PS[p0:p0 + n, 6 + half, :], comb, acc,
                                                              ALU.mult, ALU.add)
                                if half:
                                    ins.then_inc(S(f"y_used{layer}"), 1)
                                else:
                                    link(ins)
                loop_end(NE // 2)
                ve.wait_ge(*at(f"y_used{layer}", 3 * NE + 1))
                for t, (t0, n) in enumerate(TILES):
                    x = X[0:n, t, :]
                    link(ve.scalar_tensor_tensor(x, x, ALPHA, ACC[0:n, t, :], ALU.mult, ALU.add))

            def gated_input(layer):
                ve.wait_ge(*at(f"gate_b_landed{layer}", 16))
                ve.wait_ge(*at(f"pp_mm{layer}", 1))
                for u in range(7):
                    if u < 6:
                        j, t = u // 3, u % 3
                        ve.wait_ge(*at(f"ple_mm{layer}", u + 1))
                        if u >= 2:
                            ve.wait_ge(*at(f"gated{layer}", u - 1))
                        for n, (p0, p1, c0, c1) in enumerate(pieces(t, 512)):
                            ins = ve.tensor_tensor(MSG[0:p1 - p0, u % 2, c0:c1], PS[p0:p1, 5 + u % 3, 0:c1 - c0],
                                                   GATE_BIAS[0:p1 - p0, 512 * j + c0:512 * j + c1], ALU.add)
                        ins.then_inc(S(f"gate_biased{layer}"), 1)
                    if u >= 1:
                        v = u - 1
                        j, t = v // 3, v % 3
                        ve.wait_ge(*at(f"gate_sig{layer}", v + 1))
                        n = TILES[t][1]
                        pp = PS[0:n, 2 * t + j, :] if t < 2 else PS[NS * j:NS * j + NS, 4, :]
                        link(ve.tensor_tensor(MSG[0:n, v % 2, :], MSG[0:n, v % 2, :], pp, ALU.mult))
                        x = X[0:n, t, 512 * j:512 * j + 512]
                        ins = ve.tensor_tensor(x, x, MSG[0:n, v % 2, :], ALU.add)
                        ins.then_inc(S(f"gated{layer}"), 1)
                ve.wait_ge(*at(f"gated{layer}", 6))

            norm(0, 0, residual(0))
            norm(0, 1, experts(0))
            gated_input(0)

            ve.memset(QB[:, 0:1792], 0.0).then_inc(S("qb_zero"), 1)
            ve.memset(OR[:, 0:NK], 0.0).then_inc(S("or_zero"), 1)
            for t, (t0, n) in enumerate(TILES):
                ve.wait_ge(*at("qkv_evac1", 12 + t + 1))
                rotate(t, 0, HB + KVB, 8, "cosA", "sinA", None)
                rotate(t, OFF_QI, HI + 1, 16, "cosI", "sinI", "rotated1")
                ve.wait_ge(*at("rotated1", t + 1))
                k = QKV[0:n, t, OFF_K:OFF_V].rearrange("p (g d) -> p g d", g=KVB)
                dk = QKV[0:n, t, DUP_K:DUP_K + 512].rearrange("p (g u d) -> p g u d", g=KVB, u=2)
                for u in range(2):
                    ve.tensor_copy(dk[:, :, u, :], k)
                ve.tensor_scalar(WI[0:n, t, :], QKV[0:n, t, OFF_WI:B_IN], IDX_SCALE, None, ALU.mult)
                ki = QKV[0:n, t, OFF_KI:OFF_WI].unsqueeze(1).to_broadcast([n, 2, HD])
                ve.tensor_copy(QKV[0:n, t, DUP_I:DUP_I + 128].rearrange("p (u d) -> p u d", u=2), ki)\
                  .then_inc(S("doubled"), 1)
            ve.wait_ge(*at("doubled", 3))
            ve.wait_ge(*at("spread_landed", 16))
            for u in range(4):
                for bb in range(2):
                    w = WI[0:NS, 2, :].unsqueeze(2).to_broadcast([NS, HI, DQ])
                    sp = spread[0:NS, 2 * u + bb, :].rearrange("p (h q) -> p h q", h=HI)
                    ins = ve.tensor_tensor(AT[0:NS, u, 64 * bb:64 * bb + 64].rearrange("p (h q) -> p h q", h=HI),
                                           w, sp, ALU.mult)
                ins.then_inc(S("ws_rows"), 1)
            ve.wait_ge(*at("bt_mm", 6))
            ve.wait_ge(*at("qb_zero", 2))
            for c in range(2):
                for h2 in range(2):
                    for g2 in range(2):
                        src = PS[64 * h2:64 * h2 + 64, 5, :].rearrange("p (c g k b q) -> p c g k b q", c=2, g=2, k=2, b=DB)
                        dst = QBB[64 * g2:64 * g2 + 64, :, c, :]\
                            .rearrange("p b (g k h q) -> p b g k h q", g=2, k=2, h=2)[:, :, g2, :, h2, :]
                        ve.tensor_copy(dst, src[:, c, g2].rearrange("p k b q -> p b k q")).then_inc(S("bt_evac_dve"), 1)
            ve.wait_ge(*at("bt_mm", 7))
            for h2 in range(2):
                for b2 in range(2):
                    src = PS[64 * h2:64 * h2 + 64, 6, 0:256].rearrange("p (c r b q) -> p c r b q", c=4, r=4, b=2)[:, :, :, b2]
                    dst = QIB[64 * b2:64 * b2 + 64, :, 64 * b2:64 * b2 + 64]\
                        .rearrange("p r (c h q) -> p r c h q", c=4, h=2)[:, :, :, h2, :]
                    ve.tensor_copy(dst, src.rearrange("p c r q -> p r c q")).then_inc(S("bt_evac_dve"), 1)
            ve.wait_ge(*at("gated0", 6))
            ve.memset(KP[:, 0:1024], 0.0).then_inc(S("pi_zero"), 1)

            def pick(values, rounds):
                for _ in range(rounds):
                    link(ve.max(TOP8[0:values.shape[0]], values))
                    link(ve.match_replace(values, TOP8[0:values.shape[0]], values, PICKED))

            for u in range(8):
                m, t = u // 2, u % 2
                ve.wait_ge(*at("pi_relu", u + 1))
                for c in range(2):
                    s, w, acc = SM[:, u % 2, 256 * c:256 * c + 256], WI[:, t, 2 * m + c:2 * m + c + 1], PB[:, t, :]
                    ins = ve.tensor_scalar(acc, s, w, None, ALU.mult) if m == 0 and c == 0 else \
                        ve.scalar_tensor_tensor(acc, s, w, acc, ALU.mult, ALU.add)
                    if c:
                        ins.then_inc(S("pi_added"), 1)
                        ve.wait_ge(*at("pi_added", u + 1))
                    else:
                        link(ins)
            for t in range(2):
                link(ve.tensor_scalar(SMF[:, 0:256], causal[:, t, :], -1.0, NEG, ALU.is_lt, ALU.mult))
                link(ve.tensor_scalar(SMF[:, 256:512], causal[:, t, :], -1.0, None, ALU.is_gt))
                link(ve.tensor_tensor(PB[:, t, :], PB[:, t, :], SMF[:, 256:512], ALU.mult))
                link(ve.tensor_tensor(PB[:, t, :], PB[:, t, :], SMF[:, 0:256], ALU.add))
                pick(PB[:, t, :], SEL_PROMPT // 8)
                link(ve.tensor_scalar(PB[:, t, :], PB[:, t, :], -2.5e38, -BIG, ALU.is_gt, ALU.mult))
                link(ve.tensor_tensor(PB[:, t, :], PB[:, t, :], causal[:, t, :], ALU.add))
            ve.wait_ge(*at("si_sum_mm", 4))
            ve.wait_ge(*at("or_zero", 1))
            ve.tensor_copy(SELB[0:NS, 0:512], PS[0:NS, 5, :]).then_inc(S("si_taken"), 1)
            ve.tensor_copy(SELB[0:NS, 512:1024], PS[NS:2 * NS, 5, :]).then_inc(S("si_taken"), 1)
            ve.tensor_tensor(SELB[0:NS, PAST:NK], PS[0:NS, 6, 0:NS], cst("selnew", NS), ALU.add).then_inc(S("si_taken"), 1)
            ve.wait_ge(*at("kidx_evac", 8))
            ve.wait_ge(*at("sis_mm", 4))
            ve.memset(KP[:, 0:1024], 0.0).then_inc(S("pq1_zero"), 1)
            ve.wait_ge(*at("si_taken", 3))
            assert SEL_SAMPLE // 8 == 32
            prompt_attention(1, lambda: pick(SELB[0:NS, :], 1))
            ve.tensor_scalar(SELB[0:NS, :], SELB[0:NS, :], -2.5e38, -BIG, ALU.is_gt, ALU.mult).then_inc(S("selection"), 1)

            for b in range(DB):
                ve.wait_ge(*at("sb_mm", b + 1))
                link(ve.tensor_reduce(small[:, 4:5], PSF[:, 2048:2048 + NK], AX.X, ALU.max))
                ve.tensor_scalar(NMAX[:, b % 2:b % 2 + 1], small[:, 4:5], -SCALE, None, ALU.mult)\
                  .then_inc(S("row_maxb"), 1)
                ve.wait_ge(*at("expb_done", b + 1))
                link(ve.reciprocal(RC[:, 0:1], SUMS[:, b % 2:b % 2 + 1]))
                ve.wait_ge(*at("pvb_mm", b + 1))
                for j in range(4):
                    c0 = 256 + (j % 2) * 64
                    src = PS[32 * j:32 * j + 32, 6, c0:c0 + 64].unsqueeze(1).to_broadcast([32, 2, 64])
                    ve.tensor_scalar(OB[32 * j:32 * j + 32, b, :, :], src, RC[32 * j:32 * j + 32, 0:1], None, ALU.mult)\
                      .then_inc(S("ob"), 1)

            norm(1, 0, residual(1))
            norm(1, 1, experts(1))
            gated_input(1)


_INS = ["x_prompt", "x_sample", "cache_a_k", "cache_a_v", "cache_b_k", "cache_b_v", "cache_b_kidx", "page_table",
        "p_prompt", "p_sample", "a_w_in", "a_w_out", "a_lam_q1", "a_lam_k1", "a_lam_q2", "a_lam_k2", "a_subln",
        "b_w_in", "b_w_out", "ln_g", "ln_b", "router_w", "router_b", "moe_w_gate", "moe_w_up", "moe_w_down",
        "ple_proj", "ple_gate_w", "ple_gate_b"]
_OUTS = [(1, SEQ, D), (DB, DQ, D), (1, 1, SEQ, 2 * HA, HD), (1, 1, SEQ, HA, 2 * HD), (1, 1, SEQ, KVB, HD),
         (1, 1, SEQ, KVB, HD), (1, 1, SEQ, HD), (1, DB, DQ, 2 * HA, HD), (1, DB, DQ, HA, 2 * HD),
         (1, DB, DQ, KVB, HD), (1, DB, DQ, KVB, HD), (1, DB, DQ, HD)]


def program(nc, shapes):
    args = [nc.dram_tensor(f"in_{n}", shapes[n][0], mybir.dt.from_np(shapes[n][1]), kind="ExternalInput").ap()
            for n in _INS + ["consts", "spread"]]
    outs = [nc.dram_tensor(f"out_{i}", shape, F32, kind="ExternalOutput").ap() for i, shape in enumerate(_OUTS)]
    build(nc, *args, outs)


def kernel(**inputs):
    import concourse.bacc as _bacc
    from concourse.bass_utils import run_bass_kernel_spmd as _run

    nc = _bacc.Bacc("TRN2", target_bir_lowering=False, num_devices=1)
    arrays = {n: np.ascontiguousarray(inputs[n]) for n in _INS}
    arrays["consts"], arrays["spread"] = constants()
    program(nc, {n: (a.shape, a.dtype) for n, a in arrays.items()})
    r = _run(nc, [{f"in_{n}": a for n, a in arrays.items()}], core_ids=[0])
    return tuple(r.results[0][f"out_{i}"] for i in range(len(_OUTS)))
```

```python
from contextlib import ExitStack

import numpy as np
import concourse.bass as bass
from concourse import mybir

F32 = mybir.dt.float32
I32 = mybir.dt.int32
U32 = mybir.dt.uint32
ALU = mybir.AluOpType
ACT = mybir.ActivationFunctionType
AX = mybir.AxisListType

D = 1024
P = 128
KD = D // P
SEQ = 256
DB, DQ = 8, 8
NS = DB * DQ
TOK = SEQ + NS
TILES = ((0, 128), (128, 128), (256, NS))
PAGE = 128
NPAGE = 8
PAST = PAGE * NPAGE
NK = PAST + NS
HA, HB, KVB, HI, HD = 8, 16, 4, 8, 64
NE, NG, EG, FF, PD = 16, 4, 4, 512, 256
FK = FF // P
A_IN = 3 * D
B_IN = HB * HD + 2 * KVB * HD + HI * HD + HD + HI
OFF_K, OFF_V, OFF_QI, OFF_KI, OFF_WI = 1024, 1280, 1536, 2048, 2112
SEL_PROMPT, SEL_SAMPLE = 64, 256
ALPHA = 4.0 ** 0.25
EPS = 1e-5
SCALE = HD ** -0.5
IDX_SCALE = (HI ** -0.5) * (HD ** -0.5)
LAM_INIT = 0.2
OUT_GAIN = 1.0 - LAM_INIT
BIG = 1e30
NEG, PICKED = -2e38, -3e38
EXPERT_USED = (3, 3, 4)
GATE_BANK = (7, 5, 6)
PROJECT_BANK_B = (7, 5, 6, 4)
INDEX_BANK = (2, 3, 4, 7)
AT_BANK = (7, 0, 1)
AT_BANK_B = (0, 1, 4)
TURNED = ({"tokens": 0, "keys": 6, "outputs": 12, "router": 16, "gate": 22},
          {"tokens": 0, "outputs": 6, "router": 10, "gate": 16})
SLOTS = 6


def const_layout():
    at, out = 0, {}
    for name, n in (("ident", 128), ("causal", 2 * 256), ("newmask", DB * NS), ("fold", 128), ("c0", 1), ("c1", 1),
                    ("eps", 1), ("cosA", 3 * 8), ("sinA", 3 * 8), ("cosI", 3 * 16), ("sinI", 3 * 16),
                    ("selnew", NS), ("expcode", NE), ("grpcode", NG), ("before", 128), ("ones", 128),
                    ("slotbase", NE), ("place", 128), ("reversal", 128)):
        out[name] = (at, n)
        at += n
    return out, at


CONST, CONST_COLS = const_layout()


def constants():
    c = np.zeros((P, CONST_COLS), np.float32)

    def put(name, v):
        a, n = CONST[name]
        v = np.asarray(v, np.float32).reshape(v.shape[0], n)
        c[:v.shape[0], a:a + n] = v

    r = np.arange(P)
    put("ident", np.eye(P))
    key = np.arange(256)
    put("causal", np.stack([np.where(key[None] <= (r + 128 * t)[:, None], 0.0, -BIG) for t in range(2)], 1))
    tok = np.arange(NS)
    ok = (tok[None, None] // DQ == np.arange(DB)[None, :, None]) & (tok[None, None] % DQ <= (r % DQ)[:, None, None])
    put("newmask", np.where(ok, 0.0, -BIG))
    fold = np.zeros((P, P))
    for row in range(P):
        h, q = row // 16, row % 8
        fold[row, 32 * (h // 2) + 8 * (h % 2) + q] = 1
    put("fold", fold)
    put("c0", ((r // 8) % 2 == 0)[:, None])
    put("c1", ((r // 8) % 2 == 1)[:, None])
    put("eps", np.full((P, 1), EPS))
    pos = np.zeros((P, 3), np.float32)
    pos[:, 0], pos[:, 1] = r, r + 128
    pos[:NS, 2] = PAST + tok % DQ
    for name, half in (("A", 8), ("I", 16)):
        inv = (np.float32(500000.0) ** (-np.arange(half, dtype=np.float32) / np.float32(half))).astype(np.float32)
        ang = (pos[:, :, None] * inv).astype(np.float32)
        put("cos" + name, np.cos(ang))
        put("sin" + name, np.sin(ang))
    ok = (tok[:, None] // DQ == tok[None] // DQ) & (tok[None] % DQ <= tok[:, None] % DQ)
    put("selnew", np.where(ok, 0.0, NEG))
    put("expcode", np.broadcast_to(NE - np.arange(NE), (P, NE)))
    put("grpcode", np.broadcast_to(NG - np.arange(NG), (P, NG)))
    put("before", r[:, None] < r[None])
    put("ones", np.ones((P, P)))
    put("slotbase", np.broadcast_to(np.arange(NE) * 128, (P, NE)))
    put("reversal", np.eye(P)[::-1])
    put("place", np.broadcast_to(np.arange(128), (P, 128)))
    spread = (tok[:, None, None, None] == np.arange(DB)[None, :, None, None] * DQ + np.arange(DQ)[None, None, None]) \
        * np.ones((1, 1, 8, 1))
    sp = np.zeros((P, DB * 64), np.float32)
    sp[:NS] = sp[NS:] = spread.reshape(NS, -1)
    return c, sp


PER_LAYER = {
    "qkv_mm#": 18, "qkv_evac#": 18, "turn#_mm": 28, "turn#_evac": 28, "rotated#": 3, "out_mm#": 6, "out_evac#": 6,
    "ple_mm#": 6, "experts_used#": 3 * NE + 1, "pq#_mm": 8, "pq#_evac": 8, "pq#_zero": 1, "ps#_mm": 16, "pmask#": 16,
    "pmax#": 16, "pexp#": 16, "pw#": 16, "pat#_mm": 16, "pat#_evac": 16, "po#_mm": 16, "po#": 16,
    "so_t#_mm": 4, "so_t#_evac": 8,
    "router_landed#": 16, "logit_mm#": 1, "aff_ones#": 1, "aff#": 1, "acc_zero#": 1,
    "mask_ready#": 1, "pos_mm#": 1, "dispatch_ready#": 1, "sel_ready#": NE + 1, "rows_mm#": NE + 1,
    "rows_evac#": NE + 1, "second_mm#": 2 * NE, "second_evac#": 2 * NE, 
    "xe_mm#": NE + 1, "xe_evac#": NE + 1, "sp_gate_up_mm#": NE, "sp_sig#": NE, "sp_hidden#": NE, "sp_ht_mm#": NE,
    "sp_ht_evac#": NE, "sp_y_mm#": NE, "sp_y_act#": NE + 1, "sp_y_dve#": NE + 1, "sp_y_a_stored#": 8 * NE + 16, "sp_y_b_stored#": 8 * NE + 16,
    "chain_sparse#": NE + 21, "chain_dense#": 12 * NE // 2 + 15,
    "h_ready#": 3 * NE + 2, "gate_up_mm#": 3 * NE, "ht_mm#": 3 * NE, "ht_evac#": 3 * NE + 2, "y_mm#": 3 * NE,
    "y_used#": 3 * NE + 1, "sig#": 3 * NE, "p_landed#": 48, "pt_mm#": 1, "pt_evac#": 1, "pp_mm#": 1,
    "gated#": 6, "gate_b_landed#": 16, "gate_biased#": 6, "gate_sig#": 6, "norm_landed#0": 32, "norm_landed#1": 32,
    "normed#0": 3, "normed#1": 3, "var#": 6, "std#": 6,
}


def stage_of(name):
    for n, ch in enumerate(name):
        if ch in "01" and name[:n] + "#" + name[n + 1:] in PER_LAYER:
            return name[:n] + "#" + name[n + 1:], int(ch)
    return name, 0


class Stream:

    def __init__(self):
        self.items, self.landed, self.used, self.total = {}, [], [], [0] * SLOTS

    def add(self, name, used, dmas=1):
        n = len(self.landed)
        self.items[name] = n
        self.total[n % SLOTS] += 16 * dmas
        self.landed.append(self.total[n % SLOTS])
        self.used.append(used)


def plan():
    s = Stream()
    for j in range(6):
        s.add(("a_in", j), ("qkv_mm0", 3 * j + 3))
    for j in range(2):
        s.add(("a_out", j), ("out_mm0", 3 * j + 3))
    for layer in range(2):
        for e in range(NE):
            for j in range(3):
                s.add(("moe", layer, e, j), (f"experts_used{layer}", 3 * e + EXPERT_USED[j]))
        s.add(("ple_g", layer, 0), (f"ple_mm{layer}", 3))
        s.add(("ple_p", layer), (f"ple_mm{layer}", 6))
        s.add(("ple_g", layer, 1), (f"ple_mm{layer}", 6))
        if layer == 0:
            for j in range(5):
                s.add(("b_in", j), ("qkv_mm1", 3 * j + 3))
            s.add("kidx", ("kidx_mm", 8), DB * NPAGE)
            for pr in range(4):
                s.add(("kb", pr), ("kbt_mm", 8 * pr + 8), 2 * NPAGE)
                s.add(("vb", pr), ("pvb_mm", 2 * pr + 2), 2 * NPAGE)
            for j in range(2):
                s.add(("b_out", j), ("out_mm1", 3 * j + 3))
    return s


def pieces(t, w):
    if t < 2:
        return [(0, 128, 0, w)]
    return [(0, NS, 0, w // 2), (NS, 2 * NS, w // 2, w)]


def build(nc, x_prompt, x_sample, cache_a_k, cache_a_v, cache_b_k, cache_b_v, cache_b_kidx, page_table,
          p_prompt, p_sample, a_w_in, a_w_out, a_lam_q1, a_lam_k1, a_lam_q2, a_lam_k2, a_subln,
          b_w_in, b_w_out, ln_g, ln_b, router_w, router_b, moe_w_gate, moe_w_up, moe_w_down,
          ple_proj, ple_gate_w, ple_gate_b, consts, spread_c, outs):
    stream = plan()
    pool_pages = cache_a_k.shape[1]
    with ExitStack() as ctx:
        def sb(name, shape, dt=F32):
            return ctx.enter_context(nc.sbuf_tensor(name, shape, dt))

        sems = {}

        def S(name):
            base = stage_of(name)[0]
            if base not in sems:
                sems[base] = ctx.enter_context(nc.semaphore(base))
            return sems[base]

        def at(name, value):
            base, layer = stage_of(name)
            return S(name), value + (PER_LAYER[base] if layer else 0)

        ring = sb("ring", [P, SLOTS, 4096])
        X = sb("X", [P, 3, D])
        XT = sb("XT", [P, KD, TOK])
        QKV = sb("QKV", [P, 3, A_IN])
        KT = sb("KT", [P, KD, TOK])
        QB = sb("QB", [P, 2048])
        PR = sb("PR", [P, NK])
        KP = sb("KP", [P, 2048])
        OR = sb("OR", [P, 2048])
        SM = sb("SM", [P, 2, 512])
        C = sb("C", [P, CONST_COLS])
        IDX = sb("IDX", [P, 8], U32)
        COUNT = sb("COUNT", [1, NE + 1], I32)
        G = sb("G", [P, 14, 48])
        small = sb("small", [P, 152])
        pt_sb = sb("pt_sb", [1, DB * NPAGE], page_table.dtype)
        PS = ctx.enter_context(nc.psum_tensor("PS", [P, 8, 512], F32))
        PSF = PS[:, :, :].rearrange("p b n -> p (b n)")

        def cst(name, rows=P):
            a, n = CONST[name]
            return C[0:rows, a:a + n]

        ident = cst("ident")
        causal = cst("causal").rearrange("p (t k) -> p t k", t=2)
        newmask = cst("newmask").rearrange("p (b k) -> p b k", b=DB)
        spread = cst("newmask").rearrange("p (b r) -> p b r", b=DB)

        AT = XT[:, :, :].rearrange("p k n -> p (k n)")[:, 0:9 * 128].rearrange("p (j r) -> p j r", j=9)
        XTF = XT[:, :, :].rearrange("p k n -> p (k n)")
        RELU_NEW = XTF[:, 2176:2432]
        QZ = XTF[:, 1152:1664].rearrange("p (c q) -> p c q", c=2)
        PSM = (XTF[:, 1664:1920].rearrange("p (c k) -> p c k", c=2), XTF[:, 1920:2432].rearrange("p (c k) -> p c k", c=2))
        ATP = G[:, :, :].rearrange("p m n -> p (m n)")[:, 0:512].rearrange("p (c n) -> p c n", c=2)
        QZI = KP[:, 0:1024].rearrange("p (u c q) -> p u c q", u=2, c=2)
        KPG = KP[:, :].rearrange("p (u k n) -> p u k n", u=2, k=KD)
        KBT = KP[:, :].rearrange("p (c n) -> p c n", c=2)
        KIT = KP[:, :].rearrange("p (u n) -> p u n", u=2)
        SQUARES = (KP[:, 0:D], KP[:, D:2 * D], QB[:, 0:D], QB[:, D:2 * D])
        GAIN, SHIFT = KP[:, 0:D], KP[:, D:2 * D]
        QBA = QB[:, :].rearrange("p (b h r) -> p b h r", b=DB, h=HA)
        QBB = QB[:, 0:1024].rearrange("p (b c r) -> p b c r", b=DB, c=2)
        QIB = QB[:, 1024:1536].rearrange("p (u r) -> p u r", u=4)
        WS = QB[:, 1536:1792].rearrange("p (u r) -> p u r", u=4)
        QCUR = SM[:, :, 0:256].rearrange("p u (h r) -> p u h r", h=HA)
        FOLD = SM[:, :, 256:384]
        SMF = SM[:, :, :].rearrange("p u n -> p (u n)")
        OB = SMF.rearrange("p (b u d) -> p b u d", b=DB, u=2)
        SELB = OR[:, 0:NK]
        HALF = 512 + NS
        PICK, SORTED = PR[:, 0:HALF], PR[:, HALF:HALF + SEL_SAMPLE]
        TURNED_SORTED = PR[:, HALF + SEL_SAMPLE:HALF + 2 * SEL_SAMPLE].rearrange("p (c r) -> p c r", c=2)
        SCORE, ABOVE, EQUAL = (QKV[:, t, B_IN:B_IN + HALF] for t in range(3))
        LEAST, TIES = small[:, 148:149], small[:, 149:150]
        PB = OR[:, NK:NK + 512].rearrange("p (t k) -> p t k", t=2)
        lamt = OR[:, 0:256].rearrange("p (m d) -> p m d", m=4)
        NMAX, SUMS, RC = small[:, 8:16], small[:, 16:24], small[:, 24:32]
        SUBLN, SGN, NLAM = small[:, 0:1], small[:, 1:2], small[:, 2:3]
        RMS = small[:, 32:64]
        STATS = small[:, 64:100].rearrange("p (t n) -> p t n", t=3)
        MV = small[:, 100:106].rearrange("p (t n) -> p t n", t=3)
        RSTD = small[:, 106:109]
        WI = small[:, 110:134].rearrange("p (t h) -> p t h", t=3)
        TOP8 = OR[:, NK + 512:NK + 528].rearrange("p (t n) -> p t n", t=2)

        DUP_K, DUP_I = B_IN, B_IN + 512
        QF = QKV[:, :, :].rearrange("p t n -> p (t n)")
        ACC = QF[:, 0:3072].rearrange("p (t n) -> p t n", t=3)
        MSG = QF[:, 4096:5120].rearrange("p (u n) -> p u n", u=2)
        MH = QF[:, 5120:6144].rearrange("p (u n) -> p u n", u=2)
        MHT = QF[:, 7168:8192].rearrange("p (u k n) -> p u k n", u=2, k=FK)
        SEL = QF[:, 0:768].rearrange("p (u t r) -> p u t r", u=2, t=3)
        XR = QF[:, 1024:1536]
        XE = QF[:, 2048:3072].rearrange("p (k n) -> p k n", k=KD)
        YS = (QF[:, 6144:7168], QF[:, 8192:9216])
        YG = QF[:, 0:6144].rearrange("p (r t n) -> p r t n", r=2, t=3)
        GATES = small[:, 142:148].rearrange("p (r t) -> p r t", r=2)
        WHERE = QF[:, 768:768 + 3 * (NE + 1)]
        places = nc.dram_tensor("places", [NE * 128, D], F32).ap()
        KTF = KT[:, :, :].rearrange("p k n -> p (k n)")
        PT = KT[:, 0:2, :]
        PROWS = KTF[:, 768:1536].rearrange("p (t n) -> p t n", t=3)
        GATE_BIAS = KTF[:, 1536:2560]

        landed = [S(f"ring_landed{s}") for s in range(SLOTS)]
        k_landed = [S(f"kpage_landed{s}") for s in range(NPAGE)]
        v_landed = [S(f"vpages_landed{s}") for s in range(2)]
        kpage = ring[:, 0:2, :].rearrange("p s (j n) -> p (s j) n", j=4)
        vpage = ring[:, 2:6, :].rearrange("p s (j n) -> p (s j) n", j=4)

        y_p, y_s, nak_p, nav_p, nbk_p, nbv_p, nbi_p, nak_s, nav_s, nbk_s, nbv_s, nbi_s = outs

        def item(name):
            n = stream.items[name]
            return n, n % SLOTS

        def token_rows(prompt, sample, t):
            t0, n = TILES[t]
            return prompt[t0:t0 + n, :] if t < 2 else sample

        block = ctx.enter_context(nc.Block())

        @block.sync
        def _(sp):
            def place(name):
                n, s = item(name)
                if n >= SLOTS:
                    sp.wait_ge(*at(stream.used[n - SLOTS][0], stream.used[n - SLOTS][1]))
                return s

            def columns(name, w, c0, c1, rows_together):
                view = w.rearrange("(p k) n -> p k n", k=KD) if rows_together else \
                    w.rearrange("(k p) n -> p k n", p=P)
                s = place(name)
                sp.dma_start(ring[:, s, 0:KD * (c1 - c0)].rearrange("p (k n) -> p k n", k=KD),
                             view[:, :, c0:c1]).then_inc(landed[s], 16)

            def page_id(b, j):
                return sp.value_load(pt_sb[0:1, bass.ds(b * NPAGE + j, 1)], min_val=0, max_val=pool_pages - 1)

            for t, (t0, n) in enumerate(TILES):
                sp.dma_start(X[0:n, t, :], token_rows(x_prompt[0], x_sample.rearrange("b q d -> (b q) d"), t))\
                  .then_inc(S(f"x_landed{t}"), 16)
            for j in range(6):
                columns(("a_in", j), a_w_in[0], 512 * j, 512 * j + 512, True)
            sp.wait_ge(*at("page_table_landed", 16))

            def pages(b, par, first):
                for j in range(NPAGE):
                    pg = page_id(b, j)
                    if first and par == 0:
                        sp.wait_ge(*at("qkv_mm0", 3 * (j // 4 + 1)))
                    else:
                        sp.wait_ge(*at("kt_page_mm", b * 16 + (2 * j + 2 - 16)))
                    sp.dma_start(kpage[:, j, :], cache_a_k[0, bass.ds(pg, 1)].rearrange("a p h d -> (a p) (h d)"))\
                      .then_inc(k_landed[j], 16)
                    if first:
                        sp.wait_ge(*at("qkv_mm0", 3 * (2 + (8 * par + j) // 4 + 1)))
                    elif j == 0:
                        sp.wait_ge(*at("pv_mm", b - 1))
                    sp.dma_start(vpage[:, par * NPAGE + j, :],
                                 cache_a_v[0, bass.ds(pg, 1)].rearrange("a p h d -> (a p) (h d)"))\
                      .then_inc(v_landed[par], 16)

            pages(0, 0, True)
            pages(1, 1, True)
            with sp.Fori(1, DB // 2) as i:
                pages(i * 2, 0, False)
                pages(i * 2 + 1, 1, False)

            sp.wait_ge(*at("kt_page_mm", 16 * DB))
            for j in range(2):
                columns(("a_out", j), a_w_out[0], 512 * j, 512 * j + 512, False)
            sp.wait_ge(*at("pv_mm", DB))

            for layer in range(2):
                n0 = stream.items[("moe", layer, 0, 0)]

                def expert(e, j, wait):
                    s = (n0 + j) % SLOTS
                    wait()
                    w = (moe_w_gate, moe_w_up, moe_w_down)[j % 3]
                    sp.dma_start(ring[:, s, :], w[layer, bass.ds(e, 1)].rearrange("a (p k) n -> (a p) (k n)", p=P))\
                      .then_inc(landed[s], 16)

                for j in range(6):
                    n = n0 + j - SLOTS
                    before = layer == 0 and n < 6
                    expert(j // 3, j, (lambda: None) if before else
                           (lambda n=n: sp.wait_ge(*at(stream.used[n][0], stream.used[n][1]))))
                with sp.Fori(1, NE // 2) as i:
                    for j in range(6):
                        expert(i * 2 + j // 3, j, lambda j=j: sp.wait_ge(
                            *at(f"experts_used{layer}", i * 6 + (3 * (j // 3) - 6 + EXPERT_USED[j % 3]))))
                columns(("ple_g", layer, 0), ple_gate_w[layer], 0, 512, True)
                s = place(("ple_p", layer))
                sp.dma_start(ring[:, s, 0:2048], ple_proj[layer].rearrange("(p k) n -> p (k n)", k=2))\
                  .then_inc(landed[s], 16)
                sp.wait_ge(*at(f"normed{layer}1", 1))
                columns(("ple_g", layer, 1), ple_gate_w[layer], 512, 1024, True)
                if layer == 0:
                    for j in range(5):
                        columns(("b_in", j), b_w_in[0], 512 * j, min(512 * j + 512, B_IN), True)
                    s = place("kidx")
                    kx = ring[:, s, :].rearrange("p (r j b d) -> p r j b d", r=4, b=2, j=NPAGE)
                    for b in range(DB):
                        for j in range(NPAGE):
                            pg = page_id(b, j)
                            sp.dma_start(kx[:, b // 2, j, b % 2, :],
                                         cache_b_kidx[0, bass.ds(pg, 1)].rearrange("a p d -> (a p) d"))\
                              .then_inc(landed[s], 16)
                    for pr in range(4):
                        for what, cache in (("kb", cache_b_k), ("vb", cache_b_v)):
                            s = place((what, pr))
                            for bb in range(2):
                                for j in range(NPAGE):
                                    pg = page_id(2 * pr + bb, j)
                                    c0 = (bb * NPAGE + j) * KVB * HD
                                    sp.dma_start(ring[:, s, c0:c0 + KVB * HD],
                                                 cache[0, bass.ds(pg, 1)].rearrange("a p h d -> (a p) (h d)"))\
                                      .then_inc(landed[s], 16)
                    for j in range(2):
                        columns(("b_out", j), b_w_out[0], 512 * j, 512 * j + 512, False)

        @block.gpsimd
        def _(pool):
            a, n = CONST["ident"]
            pool.dma_start(C[:, a:a + n], consts[:, a:a + n]).then_inc(S("ident_landed"), 16)
            pool.dma_start(C[:, a + n:], consts[:, a + n:]).then_inc(S("const_landed"), 16)
            pool.dma_start(pt_sb[:, :], page_table.rearrange("(o b) j -> o (b j)", o=1))\
                .then_inc(S("page_table_landed"), 16)
            pool.dma_start(SUBLN, a_subln.rearrange("a d -> d a")).then_inc(S("lam_landed"), 16)
            for m, w in enumerate((a_lam_q1, a_lam_k1, a_lam_q2, a_lam_k2)):
                pool.dma_start(lamt[:, m, :], w[0].partition_broadcast(P)).then_inc(S("lam_landed"), 16)
            pool.dma_start(G[:, 13, 0:NE], router_b.partition_broadcast(P)).then_inc(S("router_b_landed"), 16)

            pool.wait_ge(*at("or_cleared", 1))
            pool.wait_ge(*at("qkv_mm0", 3))
            for c in range(8):
                pool.dma_start(places.rearrange("(p a) n -> p (a n)", p=P)[:, 2048 * c:2048 * c + 2048], OR[:, :])\
                    .then_inc(S("places_zeroed"), 16)

            for t, (t0, n) in enumerate(TILES):
                pool.wait_ge(*at("rotated0", t + 1))
                pool.dma_start(token_rows(nak_p[0, 0].rearrange("s h d -> s (h d)"),
                                          nak_s[0].rearrange("b q h d -> (b q) (h d)"), t),
                               QKV[0:n, t, D:2 * D]).then_inc(S("stored"), 16)
                pool.wait_ge(*at("qkv_evac0", 15 + t + 1))
                pool.dma_start(token_rows(nav_p[0, 0].rearrange("s h d -> s (h d)"),
                                          nav_s[0].rearrange("b q h d -> (b q) (h d)"), t),
                               QKV[0:n, t, 2 * D:3 * D]).then_inc(S("stored"), 16)

            for layer in range(2):
                pool.wait_ge(*at(f"out_mm{layer}", 1))

                def norm_params(which):
                    for ap, w in ((GAIN, ln_g), (SHIFT, ln_b)):
                        pool.dma_start(ap, w[layer, which].partition_broadcast(P))\
                            .then_inc(S(f"norm_landed{layer}{which}"), 16)

                norm_params(0)
                pool.dma_start(SMF[:, 0:KD * NE].rearrange("p (k e) -> p k e", k=KD),
                               router_w.rearrange("(p k) e -> p k e", k=KD)).then_inc(S(f"router_landed{layer}"), 16)
                for t, (t0, n) in enumerate(TILES):
                    pool.dma_start(PROWS[0:n, t, :],
                                   token_rows(p_prompt[layer, 0], p_sample[layer].rearrange("b q d -> (b q) d"), t))\
                        .then_inc(S(f"p_landed{layer}"), 16)
                pool.dma_start(GATE_BIAS, ple_gate_b[layer].partition_broadcast(P)).then_inc(S(f"gate_b_landed{layer}"), 16)
                pool.wait_ge(*at(f"normed{layer}0", 3))
                norm_params(1)
                pool.wait_ge(*at(f"dispatch_ready{layer}", 1))
                most = pool.value_load(COUNT[0:1, NE:NE + 1], min_val=0, max_val=TOK)
                with pool.If(most > 128):
                    pool.nop()
                with pool.Else():
                    for ab in "ab":
                        pool.wait_ge(*at(f"sp_y_{ab}_stored{layer}", 8 * NE + 16))
                    for t, (t0, n) in enumerate(TILES):
                        for rank in range(2):
                            pool.indirect_dma_start(
                                out=YG[0:n, rank, t, :], out_offset=None, in_=places,
                                in_offset=bass.IndirectOffsetOnAxis(ap=IDX[0:n, 3 * rank + t:3 * rank + t + 1], axis=0),
                                bounds_check=NE * 128 - 1).then_inc(S(f"tile{t}_moved{layer}"), 16)
                pool.nop()
                if layer == 0:
                    a, n = CONST["newmask"]
                    pool.dma_start(C[:, a:a + n], spread_c).then_inc(S("spread_landed"), 16)
                    for t, (t0, n) in enumerate(TILES):
                        pool.wait_ge(*at("rotated1", t + 1))
                        for o_p, o_s, c0, c1 in ((nbk_p, nbk_s, OFF_K, OFF_V), (nbv_p, nbv_s, OFF_V, OFF_QI)):
                            pool.dma_start(token_rows(o_p[0, 0].rearrange("s h d -> s (h d)"),
                                                      o_s[0].rearrange("b q h d -> (b q) (h d)"), t),
                                           QKV[0:n, t, c0:c1]).then_inc(S("stored"), 16)
                        pool.dma_start(token_rows(nbi_p[0, 0], nbi_s[0].rearrange("b q d -> (b q) d"), t),
                                       QKV[0:n, t, OFF_KI:OFF_WI]).then_inc(S("stored"), 16)
            pool.wait_ge(*at("gated1", 6))
            for t, (t0, n) in enumerate(TILES):
                pool.dma_start(token_rows(y_p[0], y_s.rearrange("b q d -> (b q) d"), t), X[0:n, t, :])\
                    .then_inc(S("stored"), 16)
            pool.wait_ge(*at("stored", 16 * (6 + 9 + 3)))

        @block.tensor
        def _(pe):
            pe.wait_ge(*at("ident_landed", 16))

            def transposed(layer, stage, view, ready, tiles=(0, 1, 2), banks=(0, 1, 2, 3), done=0):
                first = TURNED[layer][stage]
                for u in range(done, done + 2 * len(tiles)):
                    t, half = tiles[(u - done) // 2], u % 2
                    n = TILES[t][1]
                    if half == 0:
                        ready(t)
                    if u >= len(banks):
                        pe.wait_ge(*at(f"turn{layer}_evac", first + u - len(banks) + 1))
                    for j in range(4):
                        ins = pe.transpose(PS[:, banks[u % len(banks)], j * 128:j * 128 + n], view(t, 4 * half + j)[0:n],
                                           ident[0:n, 0:n])
                    ins.then_inc(S(f"turn{layer}_mm"), 1)

            def stream_chunk(a, t, k, kd=KD):
                return a[:, t, :].rearrange("p (f k) -> p k f", k=kd)[:, k, :]

            def project(tag, items, widths, evac, before=lambda t: None, banks=(4, 5, 6, 7)):
                u = 0
                for name, w in zip(items, widths):
                    n, s = item(name)
                    pe.wait_ge(landed[s], stream.landed[n])
                    wt = ring[:, s, 0:KD * w].rearrange("p (k n) -> p k n", k=KD)
                    for t, (t0, rows) in enumerate(TILES):
                        if u < 3:
                            before(t)
                        if u >= 4:
                            pe.wait_ge(*at(evac, u - 3))
                        for k in range(KD):
                            for p0, p1, c0, c1 in pieces(t, w):
                                ins = pe.matmul(PS[p0:p1, banks[u % 4], 0:c1 - c0], XT[:, k, t0:t0 + rows],
                                                wt[:, k, c0:c1], start=(k == 0), stop=(k == KD - 1))
                        ins.then_inc(S(tag), 1)
                        u += 1

            def query_chunk(tag, m, c0):
                if m >= 2:
                    pe.wait_ge(*at(tag + "_evac", m - 1))
                for t in range(2):
                    ins = pe.transpose(PS[:, m % 2, 128 * t:128 * t + 128], QKV[:, t, c0:c0 + 128], ident)
                ins.then_inc(S(tag + "_mm"), 1)

            def prompt_stages(layer, m):
                v0 = (2 * D + m * 128 if layer == 0 else OFF_V + (m // 2) * 64)
                w, heads = (128, 1) if layer == 0 else (64, 2)

                def query():
                    if layer == 0:
                        pe.wait_ge(*at("qchunk", m + 1))
                    for t in range(2):
                        q = PSM[0][:, t, :] if layer == 0 else QKV[:, t, m * 128:m * 128 + 128]
                        ins = pe.transpose(PS[:, 7, 128 * t:128 * t + 128], q, ident)
                    ins.then_inc(S(f"pq{layer}_mm"), 1)

                def scores(qt):
                    if qt == 0:
                        pe.wait_ge(*at(f"pq{layer}_evac", m + 1))
                    else:
                        pe.wait_ge(*at(f"pmask{layer}", m * 2 + 1))
                    kw = 128 * (qt + 1)
                    for c in range(2):
                        kt = KTF[:, bass.ds(m * TOK, kw)] if layer == 0 else KT[:, m // 2, 0:kw]
                        ins = pe.matmul(PS[:, 7, c * 256:c * 256 + kw], QZ[:, c, 128 * qt:128 * qt + 128], kt,
                                        start=True, stop=True)
                    ins.then_inc(S(f"ps{layer}_mm"), 1)

                def turn(qt):
                    if qt == 0:
                        pe.wait_ge(*at(f"pmask{layer}", m * 2 + 2))
                    else:
                        pe.wait_ge(*at(f"po{layer}", m * 2 + 1))
                    pe.wait_ge(*at(f"pw{layer}", m * 2 + (qt + 1)))
                    for c in range(heads):
                        for kt in range(qt + 1):
                            ins = pe.transpose(PS[:, 7, (2 * c + kt) * 128:(2 * c + kt + 1) * 128],
                                               PSM[qt][:, c, kt * 128:kt * 128 + 128], ident)
                    ins.then_inc(S(f"pat{layer}_mm"), 1)

                def values(qt):
                    pe.wait_ge(*at(f"pat{layer}_evac", m * 2 + (qt + 1)))
                    for c in range(heads):
                        for kt in range(qt + 1):
                            ins = pe.matmul(PS[:, 7, c * w:c * w + w], ATP[:, c, kt * 128:kt * 128 + 128],
                                            QKV[:, kt, bass.ds(v0, w)], start=(kt == 0), stop=(kt == qt))
                    ins.then_inc(S(f"po{layer}_mm"), 1)

                return (query, lambda: scores(0), lambda: scores(1), lambda: turn(0), lambda: values(0),
                        lambda: turn(1), lambda: values(1))

            transposed(0, "tokens", lambda t, k: stream_chunk(X, t, k), lambda t: pe.wait_ge(*at(f"x_landed{t}", 16)))
            pe.wait_ge(*at("turn0_evac", 6))
            project("qkv_mm0", [("a_in", j) for j in range(6)], [512] * 6, "qkv_evac0")
            transposed(0, "keys", lambda t, k: QKV[:, t, D + 128 * k:D + 128 * k + 128],
                       lambda t: pe.wait_ge(*at("rotated0", t + 1)))
            pe.wait_ge(*at("turn0_evac", TURNED[0]["keys"] + 6))
            for k in range(KD):
                ins = pe.transpose(PS[:, 0, k * NS:(k + 1) * NS], QKV[0:NS, 2, k * 128:(k + 1) * 128], ident[0:NS, 0:NS])
            ins.then_inc(S("qb0_mm"), 1)
            pe.wait_ge(*at("qb0", 4))
            pe.wait_ge(*at("qkv_evac0", 18))

            def page_turn(b, j):
                pe.wait_ge(k_landed[j], b * 16 + 16)
                for half, evac in enumerate(("kt_evac_act", "kt_evac_dve")):
                    pe.wait_ge(*at(evac, b * 8 + (j + 1)))
                    for k in range(4):
                        ins = pe.transpose(PS[:, (2 * j + half) % 4, k * 128:(k + 1) * 128],
                                           kpage[:, j, (4 * half + k) * 128:(4 * half + k + 1) * 128], ident)
                    ins.then_inc(S("kt_page_mm"), 1)

            def page_scores(b, par, j):
                for evac in ("kt_evac_act", "kt_evac_dve"):
                    pe.wait_ge(*at(evac, b * 8 + (j + 3)))
                if j == 0:
                    pe.wait_ge(*at("qcur", b + 1))
                    pe.wait_ge(*at("exp_done", b + 1))
                for half in range(2):
                    for t in range(4):
                        h = 2 * t + half
                        ins = pe.matmul(PS[32 * t:32 * t + 32, 4 + j // 4, (j % 4) * 128:(j % 4) * 128 + 128],
                                        QCUR[:, par, h, :], KPG[:, j % 2, h, :], start=(half == 0), stop=(half == 1))
                ins.then_inc(S("score_mm"), 1)

            def batch_a(b, par, i):
                stages = prompt_stages(0, b)
                for j in range(NPAGE + 1):
                    if j < NPAGE:
                        page_turn(b, j)
                    if j >= 1:
                        page_scores(b, par, j - 1)
                    if j < 5:
                        stages[j]()
                pe.wait_ge(*at("o_evac", b + 1))
                for half in range(2):
                    for t in range(4):
                        h = 2 * t + half
                        ins = pe.matmul(PS[32 * t:32 * t + 32, 6, 0:NS], QCUR[:, par, h, :], KT[:, h, SEQ:TOK],
                                        start=(half == 0), stop=(half == 1))
                ins.then_inc(S("score_mm"), 1)
                stages[5]()
                stages[6]()
                pe.wait_ge(*at("po0", b * 2 + 2))
                pe.wait_ge(*at("fold_ready", b + 1))
                for u in range(3):
                    for j in range(4 * u, min(4 * u + 4, 9)):
                        keys = min(128, NK - 128 * j)
                        c0 = (j % 4) * 128
                        ins = pe.matmul(PS[0:keys, AT_BANK[u], c0:c0 + 128], PR[:, 128 * j:128 * j + keys],
                                        FOLD[:, par, :], start=True, stop=True)
                    ins.then_inc(S("at_mm"), 1)
                pe.wait_ge(v_landed[par], i * 128 + 128)
                for j in range(NPAGE + 1):
                    keys = min(128, NK - 128 * j)
                    if j in (0, 4):
                        pe.wait_ge(*at("at_evac", b * 3 + (1 if j == 0 else 3)))
                    for t in range(4):
                        v = vpage[:, par * NPAGE + j, 256 * t:256 * t + 256] if j < NPAGE else \
                            QKV[0:NS, 2, 2 * D + 256 * t:2 * D + 256 * t + 256]
                        ins = pe.matmul(PS[32 * t:32 * t + 32, 6, 256:512], AT[0:keys, j, 32 * t:32 * t + 32], v,
                                        start=(j == 0), stop=(j == NPAGE))
                ins.then_inc(S("pv_mm"), 1)

            pe.sem_inc(S("score_mm"), 1)
            with pe.Fori(0, DB // 2) as i:
                batch_a(i * 2, 0, i)
                batch_a(i * 2 + 1, 1, i)

            pe.wait_ge(*at("kt_evac_act", 8 * DB + 2))
            pe.wait_ge(*at("kt_evac_dve", 8 * DB + 2))
            transposed(0, "outputs", lambda t, k: QKV[:, t, 128 * k:128 * k + 128],
                       lambda t: pe.wait_ge(*at("or_normed", t + 1)), (0, 1))
            for u in range(4):
                pe.wait_ge(*at("or_normed", 3 + u // 2))
                for j in range(4):
                    ins = pe.transpose(PS[:, 4 + u, j * 128:j * 128 + 128],
                                       OR[:, (4 * u + j) * 128:(4 * u + j + 1) * 128], ident)
                ins.then_inc(S("so_t0_mm"), 1)
            pe.wait_ge(*at("turn0_evac", TURNED[0]["outputs"] + 4))
            pe.wait_ge(*at("so_t0_evac", 8))
            project("out_mm0", [("a_out", j) for j in range(2)], [512] * 2, "out_evac0")

            def router(layer):
                pe.wait_ge(*at(f"out_evac{layer}", 6))
                transposed(layer, "router", lambda t, k: stream_chunk(X, t, k),
                           lambda t: pe.wait_ge(*at(f"normed{layer}0", t + 1)))
                pe.wait_ge(*at(f"router_landed{layer}", 16))
                for t, (t0, n) in enumerate(TILES):
                    pe.wait_ge(*at(f"turn{layer}_evac", TURNED[layer]["router"] + 2 * t + 2))
                    for k in range(KD):
                        ins = pe.matmul(PS[0:n, 4, t * NE:(t + 1) * NE], XT[:, k, t0:t0 + n], SMF[:, k * NE:(k + 1) * NE],
                                        start=(k == 0), stop=(k == KD - 1))
                ins.then_inc(S(f"logit_mm{layer}"), 1)

            def positions(layer):
                pe.wait_ge(*at(f"p_landed{layer}", 48))
                for t, (t0, n) in enumerate(TILES):
                    for k in range(2):
                        ins = pe.transpose(PS[:, 5 + k, t0:t0 + n], stream_chunk(PROWS, t, k, 2)[0:n], ident[0:n, 0:n])
                ins.then_inc(S(f"pt_mm{layer}"), 1)
                pe.wait_ge(*at(f"mask_ready{layer}", 1))
                mask = G[:, 8, :]
                pe.matmul(PS[:, 3, 0:48], cst("before"), mask, start=True, stop=False)
                pe.matmul(PS[:, 3, NE:48], cst("ones"), mask[:, 0:2 * NE], start=False, stop=False)
                pe.matmul(PS[:, 3, 2 * NE:48], cst("ones"), mask[:, 0:NE], start=False, stop=True)
                for t in range(3):
                    ins = pe.matmul(PS[:, 3, 48:48 + NE], cst("ones"), mask[:, t * NE:(t + 1) * NE],
                                    start=(t == 0), stop=(t == 2))
                ins.then_inc(S(f"pos_mm{layer}"), 1)
                pe.wait_ge(*at(f"pt_evac{layer}", 1))
                pe.wait_ge(*at(f"dispatch_ready{layer}", 1))

            def experts(layer):
                most = pe.value_load(COUNT[0:1, NE:NE + 1], min_val=0, max_val=TOK)
                with pe.If(most > 128):
                    for name in ("rows_mm", "second_mm", "xe_mm", "sp_gate_up_mm", "sp_ht_mm", "sp_y_mm"):
                        pe.sem_inc(S(f"{name}{layer}"), PER_LAYER[name + "#"])
                    experts_dense(layer)
                with pe.Else():
                    for name in ("gate_up_mm", "ht_mm", "y_mm"):
                        pe.sem_inc(S(f"{name}{layer}"), PER_LAYER[name + "#"])
                    experts_sparse(layer)
                pe.nop()

            def experts_sparse(layer):
                n0 = stream.items[("moe", layer, 0, 0)]

                def slot_of(i, j):
                    s = (n0 + j) % SLOTS
                    pe.wait_ge(landed[s], i * 16 + stream.landed[n0 + j])
                    return ring[:, s, :]

                def rows(par, places, bank, release=False):
                    for t in range(3):
                        for half in range(2):
                            ins = pe.matmul(PS[64 * half:64 * half + 64, bank, :], SEL[:, par, t, places:places + 64],
                                            X[:, t, :].rearrange("p (f k) -> p k f", k=KD)[:, 4 * half:4 * half + 4, :],
                                            start=(t == 0), stop=(t == 2))
                            if release and t == 0 and half == 0:
                                ins.then_inc(S(f"experts_used{layer}"), 2)
                    return ins

                def turn(bank):
                    for k in range(4):
                        ins = pe.transpose(PS[:, bank, k * 128:k * 128 + 128], XR[:, k * 128:k * 128 + 128], ident)
                    return ins

                def expert(i, par, e, m):
                    p1 = 0 if m == 128 else 64
                    pe.wait_ge(*at(f"xe_evac{layer}", e + 1))
                    if m == 128:
                        rows(par, 64, 4).then_inc(S(f"second_mm{layer}"), 1)
                        pe.wait_ge(*at(f"second_evac{layer}", e * 2 + 1))
                        turn(5).then_inc(S(f"second_mm{layer}"), 1)
                        pe.wait_ge(*at(f"second_evac{layer}", e * 2 + 2))
                    else:
                        pe.sem_inc(S(f"second_mm{layer}"), 2)
                    wg = slot_of(i, 3 * par).rearrange("p (k n) -> p k n", k=KD)
                    wu = slot_of(i, 3 * par + 1).rearrange("p (k n) -> p k n", k=KD)
                    for k in range(KD):
                        ins = pe.matmul(PS[0:m, 0, :], XE[:, k, 0:m], wg[:, k, :], start=(k == 0), stop=(k == KD - 1))
                        if k == 0:
                            ins.then_inc(S(f"experts_used{layer}"), 1)
                        ins = pe.matmul(PS[p1:p1 + m, 1, :], XE[:, k, 0:m], wu[:, k, :],
                                        start=(k == 0), stop=(k == KD - 1))
                    ins.then_inc(S(f"sp_gate_up_mm{layer}"), 1)
                    pe.wait_ge(*at(f"sel_ready{layer}", e + 2))
                    rows(1 - par, 0, 4, release=True).then_inc(S(f"rows_mm{layer}"), 1)
                    pe.wait_ge(*at(f"sp_hidden{layer}", e + 1))
                    for k in range(FK):
                        ins = pe.transpose(PS[:, 2, k * 128:k * 128 + 128],
                                           MH[:, 0, :].rearrange("p (f k) -> p k f", k=FK)[:, k, :], ident)
                    ins.then_inc(S(f"sp_ht_mm{layer}"), 1)
                    pe.wait_ge(*at(f"rows_evac{layer}", e + 2))
                    turn(5).then_inc(S(f"xe_mm{layer}"), 1)
                    wd = slot_of(i, 3 * par + 2).rearrange("p (k n) -> p k n", k=FK)
                    for name in ("sp_y_act", "sp_y_dve"):
                        pe.wait_ge(*at(f"{name}{layer}", e + 1))
                    pe.wait_ge(*at(f"sp_ht_evac{layer}", e + 1))
                    for k in range(FK):
                        for half in range(2):
                            ins = pe.matmul(PS[p1 * half:p1 * half + m, 6 + half, :], MHT[:, 0, k, 0:m],
                                            wd[:, k, 512 * half:512 * half + 512], start=(k == 0), stop=(k == FK - 1))
                    ins.then_inc(S(f"sp_y_mm{layer}"), 1)

                pe.wait_ge(*at(f"sel_ready{layer}", 1))
                rows(0, 0, 4).then_inc(S(f"rows_mm{layer}"), 1)
                pe.wait_ge(*at(f"rows_evac{layer}", 1))
                turn(5).then_inc(S(f"xe_mm{layer}"), 1)
                with pe.Fori(0, NE // 2) as i:
                    for par in range(2):
                        e = i * 2 + par
                        big = pe.value_load(COUNT[0:1, bass.ds(e, 1)], min_val=0, max_val=TOK)
                        with pe.If(big > 64):
                            expert(i, par, e, 128)
                        with pe.Else():
                            expert(i, par, e, 64)
                        pe.nop()
                pe.wait_ge(*at(f"sp_y_mm{layer}", NE))
                pe.sem_inc(S(f"experts_used{layer}"), 1)

            def experts_dense(layer):
                n0 = stream.items[("moe", layer, 0, 0)]

                def slot_of(i, j):
                    s = (n0 + j) % SLOTS
                    pe.wait_ge(landed[s], i * 16 + stream.landed[n0 + j])
                    return ring[:, s, :]

                def gate_up(i, u):
                    t, b0 = u % 3, 2 * (u % 2)
                    t0, n = TILES[t]
                    wg = slot_of(i, u // 3 * 3).rearrange("p (k n) -> p k n", k=KD)
                    wu = slot_of(i, u // 3 * 3 + 1).rearrange("p (k n) -> p k n", k=KD)
                    pe.wait_ge(*at(f"h_ready{layer}", i * 6 + (u + 1)))
                    for k in range(KD):
                        pe.matmul(PS[0:n, b0, :], XT[:, k, t0:t0 + n], wg[:, k, :], start=(k == 0), stop=(k == KD - 1))
                        p0 = 0 if t < 2 else NS
                        ins = pe.matmul(PS[p0:p0 + n, b0 + 1, :], XT[:, k, t0:t0 + n], wu[:, k, :],
                                        start=(k == 0), stop=(k == KD - 1))
                    ins.then_inc(S(f"gate_up_mm{layer}"), 1)

                def down(i, u):
                    t = u % 3
                    n = TILES[t][1]
                    pe.wait_ge(*at(f"h_ready{layer}", i * 6 + (u + 3)))
                    if t == 2:
                        pe.sem_inc(S(f"experts_used{layer}"), 2)
                    pe.wait_ge(*at(f"ht_evac{layer}", i * 6 + (u + 1)))
                    for k in range(FK):
                        ins = pe.transpose(PS[:, 4 + u % 2, k * 128:k * 128 + 128],
                                           MH[:, u % 2, :].rearrange("p (f k) -> p k f", k=FK)[:, k, :], ident)
                    ins.then_inc(S(f"ht_mm{layer}"), 1)
                    wd = slot_of(i, u // 3 * 3 + 2).rearrange("p (k n) -> p k n", k=FK)
                    pe.wait_ge(*at(f"ht_evac{layer}", i * 6 + (u + 3)))
                    pe.wait_ge(*at(f"y_used{layer}", i * 6 + (u + 1)))
                    for k in range(FK):
                        for half in range(2):
                            p0 = 0 if t < 2 or half == 0 else NS
                            ins = pe.matmul(PS[p0:p0 + n, 6 + half, :], MHT[:, u % 2, k, 0:n],
                                            wd[:, k, 512 * half:512 * half + 512], start=(k == 0), stop=(k == FK - 1))
                    ins.then_inc(S(f"y_mm{layer}"), 1)
                    if t == 2:
                        pe.wait_ge(*at(f"y_mm{layer}", i * 6 + (u + 1)))
                        pe.sem_inc(S(f"experts_used{layer}"), 1)

                pe.sem_inc(S(f"experts_used{layer}"), 1)
                with pe.Fori(0, NE // 2) as i:
                    for u in range(7):
                        if u < 6:
                            gate_up(i, u)
                        if u >= 1:
                            down(i, u - 1)

            def gated_input(layer):
                n, s = item(("ple_p", layer))
                wp = ring[:, s, 0:2048].rearrange("p (k n) -> p k n", k=2)
                pe.wait_ge(landed[s], stream.landed[n])
                for t, (t0, rows) in enumerate(TILES):
                    for j in range(2):
                        out = PS[0:rows, 2 * t + j, :] if t < 2 else PS[NS * j:NS * j + NS, 4, :]
                        for k in range(2):
                            ins = pe.matmul(out, PT[:, k, t0:t0 + rows], wp[:, k, 512 * j:512 * j + 512],
                                            start=(k == 0), stop=(k == 1))
                ins.then_inc(S(f"pp_mm{layer}"), 1)

                def turn_tiles(tiles):
                    transposed(layer, "gate", lambda t, k: stream_chunk(X, t, k),
                               lambda t: pe.wait_ge(*at(f"normed{layer}1", t + 1)), tiles, (5, 6), 2 * tiles[0])
                    pe.wait_ge(*at(f"turn{layer}_evac", TURNED[layer]["gate"] + 2 * tiles[-1] + 2))

                turn_tiles((0,))
                for u in range(6):
                    j, t = u // 3, u % 3
                    t0, rows = TILES[t]
                    if t == 0:
                        ng, sg = item(("ple_g", layer, j))
                        pe.wait_ge(landed[sg], stream.landed[ng])
                        wg = ring[:, sg, :].rearrange("p (k n) -> p k n", k=KD)
                    if u == 1:
                        turn_tiles((1, 2))
                    if u >= 3:
                        pe.wait_ge(*at(f"gated{layer}", u - 2))
                    for k in range(KD):
                        for p0, p1, c0, c1 in pieces(t, 512):
                            ins = pe.matmul(PS[p0:p1, GATE_BANK[u % 3], 0:c1 - c0], XT[:, k, t0:t0 + rows], wg[:, k, c0:c1],
                                            start=(k == 0), stop=(k == KD - 1))
                    ins.then_inc(S(f"ple_mm{layer}"), 1)

            router(0)
            positions(0)
            experts(0)
            gated_input(0)

            def turn_tile(t):
                transposed(1, "tokens", lambda t, k: stream_chunk(X, t, k),
                           lambda t: pe.wait_ge(*at("gated0", 4 + t)), (t,), done=2 * t)
                pe.wait_ge(*at("turn1_evac", 2 * t + 2))

            project("qkv_mm1", [("b_in", j) for j in range(5)], [512] * 4 + [B_IN - 2048], "qkv_evac1",
                    turn_tile, PROJECT_BANK_B)
            pe.wait_ge(*at("qkv_evac1", 15))
            for t, (t0, n) in enumerate(TILES):
                pe.wait_ge(*at("doubled", t + 1))
                for g in range(KVB):
                    ins = pe.transpose(PS[:, t, g * 128:g * 128 + n],
                                       QKV[0:n, t, DUP_K + g * 128:DUP_K + g * 128 + 128], ident[0:n, 0:n])
                ins.then_inc(S("bt_mm"), 1)
            for t, (t0, n) in enumerate(TILES):
                ins = pe.transpose(PS[:, 3, t0:t0 + n], QKV[0:n, t, DUP_I:DUP_I + 128], ident[0:n, 0:n])
            ins.then_inc(S("bt_mm"), 1)
            for bank, c0, n in ((4, OFF_K, 2), (5, 0, 8), (6, OFF_QI, 4)):
                for k in range(n):
                    ins = pe.transpose(PS[:, bank, k * NS:(k + 1) * NS],
                                       QKV[0:NS, 2, c0 + 128 * k:c0 + 128 * k + 128], ident[0:NS, 0:NS])
                ins.then_inc(S("bt_mm"), 1)
            pe.wait_ge(*at("ws_rows", 4))
            for u in range(4):
                ins = pe.transpose(PS[:, 7, u * NS:(u + 1) * NS], AT[0:NS, u, :], ident[0:NS, 0:NS])
            ins.then_inc(S("bt_mm"), 1)
            pe.wait_ge(*at("bt_evac_act", 6))
            pe.wait_ge(*at("bt_evac_dve", 12))

            for m in range(2):
                query_chunk("pi", m, OFF_QI + m * 128)
            for u in range(8):
                m, qt = u // 2, u % 2
                if qt == 0:
                    pe.wait_ge(*at("pi_evac", m + 1))
                if u >= 2:
                    pe.wait_ge(*at("pi_relu", u - 1))
                kw = 128 * (qt + 1)
                for c in range(2):
                    ins = pe.matmul(PS[:, 2 + u % 2, c * 256:c * 256 + kw],
                                    QZI[:, m % 2, c, 128 * qt:128 * qt + 128], KT[:, 4, 0:kw], start=True, stop=True)
                ins.then_inc(S("pis_mm"), 1)
                if qt == 1 and m + 2 < 4:
                    query_chunk("pi", m + 2, OFF_QI + (m + 2) * 128)
            pe.wait_ge(*at("pi_relu", 8))

            n, s = item("kidx")
            pe.wait_ge(landed[s], stream.landed[n])
            kx = ring[:, s, :].rearrange("p (r j e) -> p r j e", r=4, j=NPAGE)

            def kidx_turn(r):
                for half in range(2):
                    v = 2 * r + half
                    if v >= 2:
                        pe.wait_ge(*at("kidx_evac", v - 1))
                    for j in range(4):
                        ins = pe.transpose(PS[:, half, j * 128:j * 128 + 128], kx[:, r, 4 * half + j, :], ident)
                    ins.then_inc(S("kidx_mm"), 1)

            def new_scores():
                for r in range(4):
                    ins = pe.matmul(PS[:, 7, r * NS:(r + 1) * NS], QIB[:, r, :], KT[:, 4, SEQ:TOK], start=True, stop=True)
                ins.then_inc(S("sis_mm"), 1)
                pe.wait_ge(*at("si_relu", 1))
                for r in range(4):
                    ins = pe.matmul(PS[0:NS, 6, 0:NS], WS[:, r, :], RELU_NEW[:, r * NS:(r + 1) * NS],
                                    start=(r == 0), stop=(r == 3))
                ins.then_inc(S("si_sum_mm"), 1)

            def kidx_scores(h):
                r, half = h // 2, h % 2
                pe.wait_ge(*at("kidx_evac", h + 1))
                if h >= 4:
                    pe.wait_ge(*at("si_relu", h - 4 + 2))
                pe.matmul(PS[:, INDEX_BANK[h % 4], :], QIB[:, r, :], KIT[:, r % 2, 512 * half:512 * half + 512],
                          start=True, stop=True).then_inc(S("sis_mm"), 1)

            def kidx_sum(h):
                r, half = h // 2, h % 2
                pe.wait_ge(*at("si_relu", h + 2))
                pe.matmul(PS[NS * half:NS * half + NS, 5, :], WS[:, r, :], PR[:, 512 * half:512 * half + 512],
                          start=(r == 0), stop=(r == 3)).then_inc(S("si_sum_mm"), 1)

            kidx_turn(0)
            new_scores()
            for h in range(8):
                kidx_scores(h)
                if h % 2 == 0 and h < 6:
                    kidx_turn(h // 2 + 1)
                if h >= 1:
                    kidx_sum(h - 1)
            kidx_sum(7)

            pe.wait_ge(*at("kidx_evac", 8))
            pe.wait_ge(*at("sorted", SEL_SAMPLE // 8))
            for c in range(2):
                ins = pe.transpose(PS[:, 4, 128 * c:128 * c + 128], SORTED[:, 128 * c:128 * c + 128], ident)
            ins.then_inc(S("sort_mm"), 1)
            pe.wait_ge(*at("sort_evac", 1))
            for c in range(2):
                ins = pe.matmul(PS[0:NS, 5, 128 * c:128 * c + 128], TURNED_SORTED[:, 1 - c, NS:P], cst("reversal"),
                                start=True, stop=True)
            ins.then_inc(S("sort_mm"), 1)

            def keys_turn(b, v):
                r, bb = b // 2, b % 2
                n, s = item(("kb", r))
                if bb == 0 and v == 2:
                    pe.wait_ge(landed[s], stream.landed[n])
                kb = ring[:, s, :].rearrange("p (b j n) -> p b j n", b=2, j=NPAGE)
                if b >= 1:
                    pe.wait_ge(*at("kbt_evac", 4 * (b - 1) + (v + 2) % 4 + 1))
                for c in range(2):
                    for j in range(2):
                        ins = pe.transpose(PS[:, v, c * 256 + j * 128:c * 256 + j * 128 + 128],
                                           kb[:, bb, 2 * v + j, c * 128:c * 128 + 128], ident)
                ins.then_inc(S("kbt_mm"), 1)

            def batch_b(b):
                r, bb = b // 2, b % 2
                nv, sv = item(("vb", r))
                vb = ring[:, sv, :].rearrange("p (b j n) -> p b j n", b=2, j=NPAGE)
                _, scores0, scores1, turn0, values0, turn1, values1 = prompt_stages(1, b)
                keys_turn(b, 0)
                scores0()
                keys_turn(b, 1)
                scores1()
                if b == 0:
                    pe.wait_ge(*at("selection", 1))
                if b >= 1:
                    pe.wait_ge(*at("expb_done", b))
                for half in (1, 0):
                    pe.wait_ge(*at("kbt_evac", 4 * b + (2 if half else 4)))
                    for c in range(2):
                        pe.matmul(PS[64 * c:64 * c + 64, 4 + half, :], QBB[:, b, c, :],
                                  KBT[:, c, 512 * half:512 * half + 512], start=True, stop=False)
                    for c in range(2):
                        pe.matmul(PS[64 * c:64 * c + 64, 4 + half, :], spread[:, b, :],
                                  SELB[:, 512 * half:512 * half + 512], start=False, stop=True)
                    (values0, turn0)[half]()
                if b >= 1:
                    pe.wait_ge(*at("ob", 4 * b))
                for c in range(2):
                    pe.matmul(PS[64 * c:64 * c + 64, 6, 0:NS], QBB[:, b, c, :], KT[:, 5 + c, 0:NS], start=True, stop=False)
                for c in range(2):
                    ins = pe.matmul(PS[64 * c:64 * c + 64, 6, 0:NS], spread[:, b, :], SELB[:, PAST:NK],
                                    start=False, stop=True)
                ins.then_inc(S("sb_mm"), 1)
                if b < DB - 1:
                    keys_turn(b + 1, 2)
                turn1()
                if b < DB - 1:
                    keys_turn(b + 1, 3)
                values1()
                pe.wait_ge(*at("expb_done", b + 1))
                for u in range(3):
                    for j in range(4 * u, min(4 * u + 4, 9)):
                        keys = min(128, NK - 128 * j)
                        c0 = (j % 4) * 128
                        ins = pe.transpose(PS[0:keys, AT_BANK_B[u], c0:c0 + 128], PR[:, 128 * j:128 * j + keys], ident)
                    ins.then_inc(S("bat_mm"), 1)
                if b < DB - 1:
                    pe.wait_ge(*at("po1", b * 2 + 2))
                    prompt_stages(1, b + 1)[0]()
                if bb == 0:
                    pe.wait_ge(landed[sv], stream.landed[nv])
                for j in range(NPAGE + 1):
                    keys = min(128, NK - 128 * j)
                    if j % 4 == 0:
                        pe.wait_ge(*at("bat_evac", b * 3 + (j // 4 + 1)))
                    for c in range(2):
                        v = vb[:, bb, j, c * 128:c * 128 + 128] if j < NPAGE else \
                            QKV[0:NS, 2, OFF_V + c * 128:OFF_V + c * 128 + 128]
                        ins = pe.matmul(PS[64 * c:64 * c + 64, 6, 256:384], AT[0:keys, j, 64 * c:64 * c + 64], v,
                                        start=(j == 0), stop=(j == NPAGE))
                ins.then_inc(S("pvb_mm"), 1)

            keys_turn(0, 2)
            keys_turn(0, 3)
            prompt_stages(1, 0)[0]()
            for b in range(DB):
                batch_b(b)

            pe.wait_ge(*at("kbt_evac", 4 * DB))
            pe.wait_ge(*at("po1", 16))
            transposed(1, "outputs", lambda t, k: QKV[:, t, 128 * k:128 * k + 128], lambda t: None, (0, 1))
            pe.wait_ge(*at("ob", 4 * DB))
            for u in range(2):
                for j in range(4):
                    ins = pe.transpose(PS[:, 4 + u, j * 128:j * 128 + 128],
                                       SMF[:, (4 * u + j) * 128:(4 * u + j + 1) * 128], ident)
                ins.then_inc(S("so_t1_mm"), 1)
            pe.wait_ge(*at("turn1_evac", TURNED[1]["outputs"] + 4))
            pe.wait_ge(*at("so_t1_evac", 4))
            project("out_mm1", [("b_out", j) for j in range(2)], [512] * 2, "out_evac1")
            router(1)
            positions(1)
            experts(1)
            gated_input(1)

        @block.scalar
        def _(act):
            def copy(dst, src, sem=None, scale=None):
                ins = act.activation(dst, src, ACT.Copy) if scale is None else \
                    act.activation(dst, src, ACT.Copy, scale=scale)
                if sem is not None:
                    ins.then_inc(S(sem), 1)

            def copy_transposed(layer, stage, dst, tiles=(0, 1, 2), scale=None, banks=(0, 1, 2, 3)):
                first = TURNED[layer][stage]
                for u in range(2 * len(tiles)):
                    t, half = tiles[u // 2], u % 2
                    t0, n = TILES[t]
                    act.wait_ge(*at(f"turn{layer}_mm", first + u + 1))
                    copy(dst[:, 4 * half:4 * half + 4, t0:t0 + n],
                         PS[:, banks[u % len(banks)], :].rearrange("p (j c) -> p j c", j=4)[:, :, 0:n],
                         f"turn{layer}_evac", scale)

            def copy_projection(tag, evac, widths, banks=(4, 5, 6, 7)):
                u = 0
                for j, w in enumerate(widths):
                    for t in range(3):
                        act.wait_ge(*at(tag, u + 1))
                        for n, (p0, p1, c0, c1) in enumerate(pieces(t, w)):
                            last = n == len(pieces(t, w)) - 1
                            copy(QKV[0:p1 - p0, t, 512 * j + c0:512 * j + c1], PS[p0:p1, banks[u % 4], 0:c1 - c0],
                                 evac if last else None)
                        u += 1

            def copy_query_chunk(tag, m):
                act.wait_ge(*at(tag + "_mm", m + 1))
                if m == 0:
                    act.wait_ge(*at(tag + "_zero", 1))
                for c in range(2):
                    copy(QZI[64 * c:64 * c + 64, m % 2, c, :], PS[64 * c:64 * c + 64, m % 2, 0:256],
                         tag + "_evac" if c else None)

            def prompt_stages(layer, m):
                def query():
                    act.wait_ge(*at(f"pq{layer}_mm", m + 1))
                    for c in range(2):
                        copy(QZ[64 * c:64 * c + 64, c, :], PS[64 * c:64 * c + 64, 7, 0:256],
                             f"pq{layer}_evac" if c else None)

                def exponentials(qt):
                    act.wait_ge(*at(f"pmax{layer}", m * 2 + (qt + 1)))
                    for c in range(2):
                        x, col = PSM[qt][:, c, :], 4 + 2 * qt + c
                        ins = act.activation(x, x, ACT.Exp, bias=NMAX[:, col:col + 1], accum_out=SUMS[:, col:col + 1])
                    ins.then_inc(S(f"pexp{layer}"), 1)

                def turned(qt):
                    act.wait_ge(*at(f"pat{layer}_mm", m * 2 + (qt + 1)))
                    kw = 128 * (qt + 1)
                    if layer == 0:
                        copy(ATP[:, 0, 0:kw], PS[:, 7, 0:kw], "pat0_evac")
                    else:
                        copy(ATP[:, :, 0:kw], PS[:, 7, :].rearrange("p (c k) -> p c k", c=2)[:, :, 0:kw], "pat1_evac")

                return query, exponentials, turned

            copy_transposed(0, "tokens", XT)
            copy_projection("qkv_mm0", "qkv_evac0", [512] * 6)
            copy_transposed(0, "keys", KT)
            act.wait_ge(*at("sums", 1))
            act.activation(small[:, 4:6], small[:, 6:8], ACT.Exp).then_inc(S("exp_or_root"), 1)
            def batch_a(b, par):
                query, exponentials, turned = prompt_stages(0, b)
                stages = {0: query, 2: lambda: exponentials(0), 3: lambda: (turned(0), exponentials(1))}
                for j in range(NPAGE):
                    act.wait_ge(*at("kt_page_mm", b * 16 + (2 * j + 1)))
                    act.wait_ge(*at("score_mm", b * 9 + (max(j - 1, 0) + 1)))
                    copy(KPG[:, j % 2, 0:4, :], PS[:, (2 * j) % 4, :].rearrange("p (k n) -> p k n", k=4), "kt_evac_act")
                    if j in stages:
                        stages[j]()
                turned(1)
                act.wait_ge(*at("row_max", b + 1))
                act.activation(PR[:, :], PSF[:, 2048:2048 + NK], ACT.Exp, bias=NMAX[:, par:par + 1], scale=SCALE,
                               accum_out=SUMS[:, par:par + 1]).then_inc(S("exp_done"), 1)
                for u in range(3):
                    act.wait_ge(*at("at_mm", b * 3 + (u + 1)))
                    keys, m = (128, 4) if u < 2 else (NS, 1)
                    copy(AT[0:keys, 4 * u:4 * u + m, :],
                         PS[0:keys, AT_BANK[u], 0:128 * m].rearrange("p (j r) -> p j r", j=m),
                         "at_evac")

            act.wait_ge(*at("pq0_zero", 1))
            act.sem_inc(S("kt_evac_act"), 2)
            act.sem_inc(S("exp_done"), 1)
            with act.Fori(0, DB // 2) as i:
                batch_a(i * 2, 0)
                batch_a(i * 2 + 1, 1)
            act.wait_ge(*at("score_mm", 9 * DB + 1))
            for t in range(4):
                act.wait_ge(*(at("po0", 16) if t < 2 else at("o_evac", DB + 1)))
                act.activation(SQUARES[t], QKV[:, t, 0:D] if t < 2 else OR[:, D * (t - 2):D * (t - 1)], ACT.Square)\
                   .then_inc(S("exp_or_root"), 1)
            act.wait_ge(*at("sums", 5))
            act.activation(RMS[:, 0:32], RMS[:, 0:32], ACT.Sqrt, bias=cst("eps"), scale=1.0 / 128)\
               .then_inc(S("exp_or_root"), 1)
            copy_transposed(0, "outputs", XT, (0, 1), small[:, 3:4])
            for u in range(4):
                act.wait_ge(*at("so_t0_mm", u + 1))
                for hp in range(2):
                    src = PS[:, 4 + u, :].rearrange("p (b c t r) -> p b c t r", b=2, c=2, t=4)[:, :, hp, :, 8 * hp:8 * hp + 8]
                    dst = XT[:, hp::2, SEQ + 16 * u:SEQ + 16 * u + 16].rearrange("p t (b q) -> p b t q", b=2)
                    copy(dst, src, "so_t0_evac", small[:, 3:4])

            def norm_root(layer, which):
                for t in range(3):
                    act.wait_ge(*at(f"var{layer}", 3 * which + t + 1))
                    act.activation(RSTD[:, t:t + 1], MV[:, t, 1:2], ACT.Sqrt, bias=cst("eps"), scale=1.0)\
                       .then_inc(S(f"std{layer}"), 1)

            def experts(layer):
                copy_transposed(layer, "router", XT)
                act.wait_ge(*at(f"logit_mm{layer}", 1))
                act.wait_ge(*at(f"aff_ones{layer}", 1))
                act.activation(G[:, 0, 0:32], PS[:, 4, 0:32], ACT.Sigmoid)
                act.activation(G[0:NS, 0, 32:48], PS[0:NS, 4, 32:48], ACT.Sigmoid).then_inc(S(f"aff{layer}"), 1)
                act.wait_ge(*at(f"pt_mm{layer}", 1))
                copy(PT, PS[:, 5:7, 0:TOK], f"pt_evac{layer}")
                act.wait_ge(*at(f"dispatch_ready{layer}", 1))
                most = act.value_load(COUNT[0:1, NE:NE + 1], min_val=0, max_val=TOK)
                with act.If(most > 128):
                    for name in ("rows_evac", "second_evac", "xe_evac", "sp_sig", "sp_ht_evac", "sp_y_act", "sp_y_a_stored", "sp_y_b_stored"):
                        act.sem_inc(S(f"{name}{layer}"), PER_LAYER[name + "#"])
                    experts_dense(layer)
                with act.Else():
                    for name in ("ht_evac", "sig"):
                        act.sem_inc(S(f"{name}{layer}"), PER_LAYER[name + "#"])
                    experts_sparse(layer)
                act.nop()

            def experts_sparse(layer):
                def copy_turned(first, sem):
                    copy(XE[:, :, first:first + 64].rearrange("p (h k) c -> p k h c", h=2),
                         PS[:, 5, :].rearrange("p (k h c) -> p k h c", k=4, h=2), sem)

                def expert(i, par, e, m):
                    if m == 128:
                        act.wait_ge(*at(f"second_mm{layer}", e * 2 + 1))
                        copy(XR, PS[:, 4, :], f"second_evac{layer}")
                        act.wait_ge(*at(f"second_mm{layer}", e * 2 + 2))
                        copy_turned(64, f"second_evac{layer}")
                    else:
                        act.sem_inc(S(f"second_evac{layer}"), 2)
                    act.wait_ge(*at(f"sp_gate_up_mm{layer}", e + 1))
                    act.activation(MSG[0:m, 0, :], PS[0:m, 0, :], ACT.Sigmoid).then_inc(S(f"sp_sig{layer}"), 1)
                    act.wait_ge(*at(f"rows_mm{layer}", e + 2))
                    copy(XR, PS[:, 4, :], f"rows_evac{layer}")
                    act.wait_ge(*at(f"sp_ht_mm{layer}", e + 1))
                    copy(MHT[:, 0, :, 0:m], PS[:, 2, :].rearrange("p (k c) -> p k c", k=FK)[:, :, 0:m],
                         f"sp_ht_evac{layer}")
                    act.wait_ge(*at(f"xe_mm{layer}", e + 2))
                    copy_turned(0, f"xe_evac{layer}")
                    act.wait_ge(*at(f"sp_y_mm{layer}", e + 1))
                    act.wait_ge(*at(f"sp_y_{'ab'[par]}_stored{layer}", i * 16 + 16))
                    copy(YS[par][0:m, 0:512], PS[0:m, 6, :], f"sp_y_act{layer}")
                    act.wait_ge(*at(f"sp_y_act{layer}", e + 2))
                    act.wait_ge(*at(f"sp_y_dve{layer}", e + 2))
                    act.dma_start(places[bass.ds(e * 128, m), :], YS[par][0:m, :])\
                       .then_inc(S(f"sp_y_{'ab'[par]}_stored{layer}"), 16)

                act.wait_ge(*at(f"rows_mm{layer}", 1))
                copy(XR, PS[:, 4, :], f"rows_evac{layer}")
                act.wait_ge(*at(f"xe_mm{layer}", 1))
                copy_turned(0, f"xe_evac{layer}")
                act.sem_inc(S(f"sp_y_act{layer}"), 1)
                for ab in "ab":
                    act.sem_inc(S(f"sp_y_{ab}_stored{layer}"), 16)
                with act.Fori(0, NE // 2) as i:
                    for par in range(2):
                        e = i * 2 + par
                        big = act.value_load(COUNT[0:1, bass.ds(e, 1)], min_val=0, max_val=TOK)
                        with act.If(big > 64):
                            expert(i, par, e, 128)
                        with act.Else():
                            expert(i, par, e, 64)
                        act.nop()

            def experts_dense(layer):
                act.wait_ge(*at(f"acc_zero{layer}", 1))
                act.sem_inc(S(f"ht_evac{layer}"), 2)
                with act.Fori(0, NE // 2) as i:
                    for u in range(7):
                        if u < 6:
                            n = TILES[u % 3][1]
                            act.wait_ge(*at(f"gate_up_mm{layer}", i * 6 + (u + 1)))
                            act.activation(MSG[0:n, u % 2, :], PS[0:n, 2 * (u % 2), :], ACT.Sigmoid)\
                               .then_inc(S(f"sig{layer}"), 1)
                        if u >= 1:
                            v = u - 1
                            n = TILES[v % 3][1]
                            act.wait_ge(*at(f"ht_mm{layer}", i * 6 + (v + 1)))
                            copy(MHT[:, v % 2, :, 0:n], PS[:, 4 + v % 2, :].rearrange("p (k c) -> p k c", k=FK)[:, :, 0:n],
                                 f"ht_evac{layer}")

            def gated_input(layer):
                copy_transposed(layer, "gate", XT, banks=(5, 6))
                for u in range(6):
                    n = TILES[u % 3][1]
                    act.wait_ge(*at(f"gate_biased{layer}", u + 1))
                    act.activation(MSG[0:n, u % 2, :], MSG[0:n, u % 2, :], ACT.Sigmoid).then_inc(S(f"gate_sig{layer}"), 1)

            norm_root(0, 0)
            experts(0)
            norm_root(0, 1)
            gated_input(0)

            copy_transposed(1, "tokens", XT)
            copy_projection("qkv_mm1", "qkv_evac1", [512] * 4 + [B_IN - 2048], PROJECT_BANK_B)
            for t, (t0, n) in enumerate(TILES):
                act.wait_ge(*at("bt_mm", t + 1))
                copy(KT[:, 0:4, t0:t0 + n], PS[:, t, :].rearrange("p (g c) -> p g c", g=4)[:, :, 0:n], "bt_evac_act")
            act.wait_ge(*at("bt_mm", 4))
            copy(KT[:, 4, :], PS[:, 3, 0:TOK], "bt_evac_act")
            act.wait_ge(*at("bt_mm", 5))
            copy(KT[:, 5:7, 0:NS], PS[:, 4, 0:2 * NS].rearrange("p (c n) -> p c n", c=2), "bt_evac_act")
            act.wait_ge(*at("bt_mm", 8))
            act.wait_ge(*at("bt_evac_dve", 12))
            copy(WS, PS[:, 7, 0:4 * NS].rearrange("p (u n) -> p u n", u=4), "bt_evac_act")
            for m in range(2):
                copy_query_chunk("pi", m)
            for u in range(8):
                act.wait_ge(*at("pis_mm", u + 1))
                if u >= 2:
                    act.wait_ge(*at("pi_added", u - 1))
                kw = 128 * (u % 2 + 1)
                act.activation(SM[:, u % 2, :].rearrange("p (c k) -> p c k", c=2)[:, :, 0:kw],
                               PS[:, 2 + u % 2, :].rearrange("p (c k) -> p c k", c=2)[:, :, 0:kw], ACT.Relu)\
                   .then_inc(S("pi_relu"), 1)
                if u % 2 == 1 and u // 2 + 2 < 4:
                    copy_query_chunk("pi", u // 2 + 2)
            def copy_index_keys(r):
                for half in range(2):
                    act.wait_ge(*at("kidx_mm", 2 * r + half + 1))
                    if r >= 2 and half == 0:
                        act.wait_ge(*at("sis_mm", 2 * (r - 2) + 3))
                    copy(KIT[:, r % 2, 512 * half:512 * half + 512], PS[:, half, :], "kidx_evac")

            copy_index_keys(0)
            act.wait_ge(*at("sis_mm", 1))
            act.activation(RELU_NEW, PS[:, 7, 0:4 * NS], ACT.Relu).then_inc(S("si_relu"), 1)
            for h in range(8):
                act.wait_ge(*at("sis_mm", h + 2))
                if h >= 2:
                    act.wait_ge(*at("si_sum_mm", h))
                half = h % 2
                act.activation(PR[:, 512 * half:512 * half + 512], PS[:, INDEX_BANK[h % 4], :], ACT.Relu)\
                   .then_inc(S("si_relu"), 1)
                if h % 2 == 0 and h < 6:
                    copy_index_keys(h // 2 + 1)
            act.wait_ge(*at("sort_mm", 1))
            copy(TURNED_SORTED, PS[:, 4, 0:256].rearrange("p (c r) -> p c r", c=2), "sort_evac")
            act.wait_ge(*at("pq1_zero", 1))
            def copy_keys(b, v):
                act.wait_ge(*at("kbt_mm", 4 * b + (v + 2) % 4 + 1))
                if b >= 1 and v == 2:
                    act.wait_ge(*at("sb_mm", b))
                copy(KBT[:, :, 256 * v:256 * v + 256], PS[:, v, :].rearrange("p (c n) -> p c n", c=2), "kbt_evac")

            copy_keys(0, 2)
            copy_keys(0, 3)
            prompt_stages(1, 0)[0]()
            for b in range(DB):
                _, exponentials, turned = prompt_stages(1, b)
                copy_keys(b, 0)
                copy_keys(b, 1)
                exponentials(0)
                exponentials(1)
                turned(0)
                if b < DB - 1:
                    copy_keys(b + 1, 2)
                turned(1)
                act.wait_ge(*at("row_maxb", b + 1))
                act.activation(PR[:, :], PSF[:, 2048:2048 + NK], ACT.Exp, bias=NMAX[:, b % 2:b % 2 + 1], scale=SCALE,
                               accum_out=SUMS[:, b % 2:b % 2 + 1]).then_inc(S("expb_done"), 1)
                for u in range(3):
                    act.wait_ge(*at("bat_mm", b * 3 + u + 1))
                    keys, m = (128, 4) if u < 2 else (NS, 1)
                    copy(AT[0:keys, 4 * u:4 * u + m, :],
                         PS[0:keys, AT_BANK_B[u], 0:128 * m].rearrange("p (j r) -> p j r", j=m),
                         "bat_evac")
                if b < DB - 1:
                    copy_keys(b + 1, 3)
                    prompt_stages(1, b + 1)[0]()
            copy_transposed(1, "outputs", XT, (0, 1))
            for u in range(2):
                act.wait_ge(*at("so_t1_mm", u + 1))
                for hp in range(2):
                    src = PS[64 * hp:64 * hp + 64, 4 + u, :].rearrange("p (b h c q) -> p b h c q", b=4, h=8, c=2)[:, :, :, hp, :]
                    for bb in range(4):
                        b = 4 * u + bb
                        copy(XT[64 * hp:64 * hp + 64, :, SEQ + 8 * b:SEQ + 8 * b + 8], src[:, bb],
                             "so_t1_evac" if bb == 3 else None)
            norm_root(1, 0)
            experts(1)
            norm_root(1, 1)
            gated_input(1)

        @block.vector
        def _(ve):
            chain = {"name": "vector_chain", "n": 0, "i": None, "per": 0}

            def link(ins):
                chain["n"] += 1
                ins.then_inc(S(chain["name"]), 1)
                ve.wait_ge(*at(chain["name"], chain["n"] if chain["i"] is None else
                               chain["i"] * chain["per"] + chain["n"]))

            def loop(i, per):
                chain.update(i=i, per=per, start=chain["n"])

            def loop_end(count):
                assert chain["n"] - chain["start"] == chain["per"], chain
                chain["n"] = chain["start"] + count * chain["per"]
                chain["i"] = None

            def rotate(t, c0, heads, half, cos, sin, tag):
                n = TILES[t][1]
                rot = 2 * half
                x = QKV[0:n, t, c0:c0 + heads * HD].rearrange("p (h d) -> p h d", h=heads)
                x4 = x[:, :, 0:rot].rearrange("p h (u f) -> p h u f", u=2)
                cs = cst(cos)[0:n, t * half:(t + 1) * half].unsqueeze(1).unsqueeze(1).to_broadcast([n, heads, 2, half])
                sn = cst(sin)[0:n, t * half:(t + 1) * half].unsqueeze(1).to_broadcast([n, heads, half])
                t1 = PR[0:n, 0:heads * rot].rearrange("p (h u f) -> p h u f", h=heads, u=2)
                t2 = PR[0:n, 512:512 + heads * rot].rearrange("p (h u f) -> p h u f", h=heads, u=2)
                ve.tensor_tensor(t2[:, :, 0, :], x4[:, :, 1, :], sn, ALU.mult)
                ve.tensor_tensor(t2[:, :, 1, :], x4[:, :, 0, :], sn, ALU.mult)
                link(ve.tensor_tensor(t1, x4, cs, ALU.mult))
                ve.tensor_tensor(x4[:, :, 0, :], t1[:, :, 0, :], t2[:, :, 0, :], ALU.subtract)
                ins = ve.tensor_tensor(x4[:, :, 1, :], t1[:, :, 1, :], t2[:, :, 1, :], ALU.add)
                if tag:
                    ins.then_inc(S(tag), 1)
                else:
                    link(ins)

            def prompt_stages(layer, m):
                def scores(qt):
                    kw = 128 * (qt + 1)
                    ve.wait_ge(*at(f"ps{layer}_mm", m * 2 + (qt + 1)))
                    s3 = PS[:, 7, :].rearrange("p (c k) -> p c k", c=2)[:, :, 0:kw]
                    bias = (causal if layer == 0 else PB)[:, qt, 0:kw].unsqueeze(1).to_broadcast([P, 2, kw])
                    ve.scalar_tensor_tensor(PSM[qt], s3, SCALE, bias, ALU.mult, ALU.add).then_inc(S(f"pmask{layer}"), 1)
                    ve.wait_ge(*at(f"pmask{layer}", m * 2 + (qt + 1)))
                    ve.tensor_reduce(NMAX[:, 4 + 2 * qt:6 + 2 * qt], PSM[qt], AX.X, ALU.max, negate=True)\
                      .then_inc(S(f"pmax{layer}"), 1)

                def weights(qt):
                    ve.wait_ge(*at(f"pexp{layer}", m * 2 + (qt + 1)))
                    rc = RC[:, 4 + 2 * qt:6 + 2 * qt]
                    link(ve.reciprocal(rc, SUMS[:, 4 + 2 * qt:6 + 2 * qt]))
                    p0, p1 = PSM[qt][:, 0, :], PSM[qt][:, 1, :]
                    if layer == 0:
                        link(ve.tensor_tensor(rc[:, 1:2], rc[:, 1:2], NLAM, ALU.mult))
                        link(ve.tensor_scalar(p0, p0, rc[:, 0:1], None, ALU.mult))
                        ve.scalar_tensor_tensor(p0, p1, rc[:, 1:2], p0, ALU.mult, ALU.add).then_inc(S("pw0"), 1)
                    else:
                        ve.tensor_scalar(p0, p0, rc[:, 0:1], None, ALU.mult)
                        ve.tensor_scalar(p1, p1, rc[:, 1:2], None, ALU.mult).then_inc(S("pw1"), 1)

                def outputs(qt):
                    ve.wait_ge(*at(f"po{layer}_mm", m * 2 + (qt + 1)))
                    ve.tensor_scalar(QKV[:, qt, bass.ds(m * 128, 128)], PS[:, 7, 0:128], 1.0, None, ALU.mult)\
                      .then_inc(S(f"po{layer}"), 1)

                return scores, weights, outputs

            link(ve.memset(small[:, 8:152], 1.0))
            link(ve.memset(X[NS:P, 2, :], 0.0))
            ve.memset(QB[:, :], 0.0).then_inc(S("qb_zero"), 1)
            ve.wait_ge(*at("const_landed", 16))
            ve.wait_ge(*at("lam_landed", 80))
            link(ve.tensor_scalar(small[:, 3:4], SUBLN, OUT_GAIN, None, ALU.mult))
            l2 = OR[:, 256:384].rearrange("p (m d) -> p m d", m=2)
            link(ve.tensor_tensor(l2, lamt[:, 0::2, :], lamt[:, 1::2, :], ALU.mult))
            ve.tensor_reduce(small[:, 6:8], l2, AX.X, ALU.add).then_inc(S("sums"), 1)
            ve.wait_ge(*at("sums", 1))
            ve.memset(OR[:, :], 0.0).then_inc(S("or_cleared"), 1)
            for t in range(3):
                ve.wait_ge(*at("qkv_evac0", 9 + t + 1))
                if t:
                    ve.wait_ge(*at("rotated0", t))
                rotate(t, 0, 32, 8, "cosA", "sinA", "rotated0")
            ve.wait_ge(*at("exp_or_root", 1))
            link(ve.tensor_tensor(NLAM, small[:, 5:6], small[:, 4:5], ALU.subtract))
            link(ve.tensor_scalar(NLAM, NLAM, -LAM_INIT, None, ALU.add))
            link(ve.scalar_tensor_tensor(SGN, cst("c1"), NLAM, cst("c0"), ALU.mult, ALU.add))
            ve.wait_ge(*at("qb0_mm", 1))
            ve.wait_ge(*at("qb_zero", 1))
            for c in range(2):
                for hp in range(2):
                    src = PS[64 * c:64 * c + 64, 0, :].rearrange("p (t h b q) -> p t h b q", t=4, h=2, b=DB)[:, :, hp]
                    dst = QBA[64 * c:64 * c + 64, :, hp::2, hp * 16 + c * 8:hp * 16 + c * 8 + 8]\
                        .rearrange("p b t q -> p t b q")
                    ve.tensor_copy(dst, src).then_inc(S("qb0"), 1)
            ve.wait_ge(*at("qkv_mm0", 18))
            ve.memset(QZ, 0.0).then_inc(S("pq0_zero"), 1)
            ve.wait_ge(*at("qb0", 4))

            def batch_a(b, par):
                scores, weights, outputs = prompt_stages(0, b)
                stages = {1: lambda: scores(0), 2: lambda: (weights(0), scores(1)), 3: lambda: weights(1),
                          4: lambda: outputs(0)}
                ve.tensor_copy(QCUR[:, par].rearrange("p h r -> p (h r)"), QB[:, bass.ds(b * 256, 256)])\
                  .then_inc(S("qcur"), 1)
                ve.tensor_copy(PSM[0], QKV[:, 0:2, bass.ds(b * 128, 128)]).then_inc(S("qchunk"), 1)
                for j in range(NPAGE):
                    ve.wait_ge(*at("kt_page_mm", b * 16 + (2 * j + 2)))
                    ve.wait_ge(*at("score_mm", b * 9 + (max(j - 1, 0) + 1)))
                    ve.tensor_copy(KPG[:, j % 2, 4:8, :], PS[:, (2 * j + 1) % 4, :].rearrange("p (k n) -> p k n", k=4))\
                      .then_inc(S("kt_evac_dve"), 1)
                    if j in stages:
                        stages[j]()
                ve.wait_ge(*at("score_mm", b * 9 + 5))
                link(ve.tensor_reduce(small[:, 4:5], PS[:, 4, :], AX.X, ALU.max))
                ve.wait_ge(*at("score_mm", b * 9 + 10))
                a0 = CONST["newmask"][0]
                link(ve.tensor_tensor(PS[:, 6, 0:NS], PS[:, 6, 0:NS], C[:, bass.ds(b * NS + a0, NS)], ALU.add))
                link(ve.tensor_reduce(small[:, 5:6], PSF[:, 2560:2048 + NK], AX.X, ALU.max))
                ve.tensor_scalar(NMAX[:, par:par + 1], small[:, 4:5], small[:, 5:6], -SCALE, ALU.max, ALU.mult)\
                  .then_inc(S("row_max"), 1)
                outputs(1)
                ve.wait_ge(*at("exp_done", b + 2))
                link(ve.reciprocal(RC[:, par:par + 1], SUMS[:, par:par + 1]))
                link(ve.tensor_tensor(RC[:, par:par + 1], RC[:, par:par + 1], SGN, ALU.mult))
                ve.tensor_scalar(FOLD[:, par, :], cst("fold"), RC[:, par:par + 1], None, ALU.mult)\
                  .then_inc(S("fold_ready"), 1)
                ve.wait_ge(*at("pv_mm", b + 1))
                ve.tensor_copy(OR[:, bass.ds(b * 256, 256)], PS[:, 6, 256:512]).then_inc(S("o_evac"), 1)

            ve.wait_ge(*at("places_zeroed", 128))
            ve.sem_inc(S("kt_evac_dve"), 2)
            ve.sem_inc(S("o_evac"), 1)
            with ve.Fori(0, DB // 2) as i:
                loop(i, 10 + 12)
                batch_a(i * 2, 0)
                batch_a(i * 2 + 1, 1)
            loop_end(DB // 2)

            for t in range(4):
                ve.wait_ge(*at("exp_or_root", t + 2))
                ve.tensor_reduce(RMS[:, 8 * t:8 * t + 8], SQUARES[t].rearrange("p (h d) -> p h d", h=8), AX.X, ALU.add)\
                  .then_inc(S("sums"), 1)
            ve.wait_ge(*at("exp_or_root", 6))
            link(ve.reciprocal(RMS[:, 0:32], RMS[:, 0:32]))
            for t in range(4):
                o = (QKV[:, t, 0:D] if t < 2 else OR[:, D * (t - 2):D * (t - 1)]).rearrange("p (h d) -> p h d", h=8)
                ve.tensor_tensor(o, o, RMS[:, 8 * t:8 * t + 8].unsqueeze(2).to_broadcast([P, 8, 128]), ALU.mult)\
                  .then_inc(S("or_normed"), 1)
            ve.wait_ge(*at("or_normed", 4))

            def moments(layer, t):
                n = TILES[t][1]
                for half in range(2):
                    ins = ve.bn_stats(STATS[0:n, t, 6 * half:6 * half + 6], X[0:n, t, 512 * half:512 * half + 512])
                link(ins)
                ve.bn_aggr(MV[0:n, t, :], STATS[0:n, t, :]).then_inc(S(f"var{layer}"), 1)

            def residual(layer):
                def part(j, t):
                    u = 3 * j + t
                    ve.wait_ge(*at(f"out_mm{layer}", u + 1))
                    for p0, p1, c0, c1 in pieces(t, 512):
                        x = X[0:p1 - p0, t, 512 * j + c0:512 * j + c1]
                        ins = ve.scalar_tensor_tensor(x, x, ALPHA, PS[p0:p1, 4 + u % 4, 0:c1 - c0], ALU.mult, ALU.add)
                    ins.then_inc(S(f"out_evac{layer}"), 1)

                def tile(t):
                    part(1, t)
                    ve.wait_ge(*at(f"out_evac{layer}", t + 4))
                    moments(layer, t)

                for t in range(3):
                    part(0, t)
                return tile

            def norm(layer, which, prepare):
                for u in range(4):
                    if u < 3:
                        prepare(u)
                    if u >= 1:
                        t, n = u - 1, TILES[u - 1][1]
                        x = X[0:n, t, :]
                        ve.wait_ge(*at(f"std{layer}", 3 * which + u))
                        link(ve.reciprocal(RSTD[:, t:t + 1], RSTD[:, t:t + 1]))
                        link(ve.tensor_scalar(x, x, MV[0:n, t, 0:1], RSTD[0:n, t:t + 1], ALU.subtract, ALU.mult))
                        ve.wait_ge(*at(f"norm_landed{layer}{which}", 32))
                        link(ve.tensor_tensor(x, x, GAIN[0:n], ALU.mult))
                        ve.tensor_tensor(x, x, SHIFT[0:n], ALU.add).then_inc(S(f"normed{layer}{which}"), 1)
                ve.wait_ge(*at(f"normed{layer}{which}", 3))

            def experts(layer):
                g3 = lambda m: G[:, m, 0:48].rearrange("p (t e) -> p t e", t=3)
                ve.memset(G[:, 0, :], 1.0).then_inc(S(f"aff_ones{layer}"), 1)
                ve.wait_ge(*at("stored", 96 if layer == 0 else 96 + 144))
                ve.wait_ge(*at(f"aff{layer}", 1))
                ve.wait_ge(*at("router_b_landed", 16))
                link(ve.tensor_tensor(g3(1), g3(0), G[:, 13, 0:NE].unsqueeze(1).to_broadcast([P, 3, NE]), ALU.add))
                s4 = G[:, 1, :].rearrange("p (g e) -> p g e", g=12)
                hi = G[:, 2, 0:24].rearrange("p (g e) -> p g e", g=12)
                lo = G[:, 2, 24:48].rearrange("p (g e) -> p g e", g=12)
                ve.tensor_tensor(hi, s4[:, :, 0::2], s4[:, :, 1::2], ALU.max)
                link(ve.tensor_tensor(lo, s4[:, :, 0::2], s4[:, :, 1::2], ALU.min))
                top, second, third = G[:, 3, 0:12], G[:, 3, 12:24], G[:, 3, 24:36]
                ve.tensor_tensor(top, hi[:, :, 0], hi[:, :, 1], ALU.max)
                ve.tensor_tensor(second, hi[:, :, 0], hi[:, :, 1], ALU.min)
                link(ve.tensor_tensor(third, lo[:, :, 0], lo[:, :, 1], ALU.max))
                link(ve.tensor_tensor(second, second, third, ALU.max))
                link(ve.tensor_tensor(top, top, second, ALU.add))

                def first_of_max(values, code, mx, out, w):
                    link(ve.tensor_reduce(mx, values, AX.X, ALU.max))
                    link(ve.tensor_tensor(out, values, mx.unsqueeze(2).to_broadcast([P, 3, w]), ALU.is_equal))
                    link(ve.tensor_tensor(out, out, code, ALU.mult))
                    link(ve.tensor_reduce(mx, out, AX.X, ALU.max))
                    link(ve.tensor_tensor(out, out, mx.unsqueeze(2).to_broadcast([P, 3, w]), ALU.is_equal))

                mx = G[:, 12, 0:3]
                grp = G[:, 4, 0:12]
                first_of_max(top.rearrange("p (t g) -> p t g", t=3), cst("grpcode").unsqueeze(1).to_broadcast([P, 3, NG]), mx,
                             grp.rearrange("p (t g) -> p t g", t=3), NG)
                link(ve.tensor_scalar(G[:, 4, 12:24], grp, -1.0, BIG, ALU.add, ALU.mult))
                sel4 = G[:, 5, :].rearrange("p (g e) -> p g e", g=12)
                link(ve.tensor_tensor(sel4, s4, grp.unsqueeze(2).to_broadcast([P, 12, EG]), ALU.mult))
                link(ve.tensor_tensor(sel4, sel4, G[:, 4, 12:24].unsqueeze(2).to_broadcast([P, 12, EG]), ALU.add))
                code = cst("expcode").unsqueeze(1).to_broadcast([P, 3, NE])
                first_of_max(g3(5), code, mx, g3(6), NE)
                link(ve.scalar_tensor_tensor(g3(5), g3(6), -3.0 * BIG, g3(5), ALU.mult, ALU.add))
                first_of_max(g3(5), code, mx, g3(7), NE)
                link(ve.tensor_tensor(g3(8), g3(6), g3(7), ALU.add))
                link(ve.tensor_tensor(g3(9), g3(8), g3(0), ALU.mult))
                link(ve.tensor_reduce(mx, g3(9), AX.X, ALU.add))
                link(ve.reciprocal(mx, mx))
                link(ve.tensor_tensor(g3(10), g3(9), mx.unsqueeze(2).to_broadcast([P, 3, NE]), ALU.mult))
                ve.memset(G[NS:P, 8, 32:48], 0.0).then_inc(S(f"mask_ready{layer}"), 1)
                link(ve.memset(MH[:, 0, :], 0.0))
                link(ve.memset(WHERE[:, 3 * NE:], -1.0))
                t0, t1 = g3(1), g3(2)
                for rank in range(2):
                    link(ve.tensor_tensor(t0, g3(6 + rank), g3(10), ALU.mult))
                    link(ve.tensor_reduce(GATES[:, rank, :], t0, AX.X, ALU.add))
                ve.wait_ge(*at(f"pos_mm{layer}", 1))
                link(ve.scalar_tensor_tensor(t1, PS[:, 3, 0:48].rearrange("p (t e) -> p t e", t=3), 1.0, g3(8),
                                             ALU.add, ALU.mult))
                link(ve.tensor_scalar(WHERE[:, 0:3 * NE].rearrange("p (e t) -> p t e", t=3), t1, -1.0, None, ALU.add))
                link(ve.tensor_tensor(t0, PS[:, 3, 0:48].rearrange("p (t e) -> p t e", t=3),
                                      cst("slotbase").unsqueeze(1).to_broadcast([P, 3, NE]), ALU.add))
                for rank in range(2):
                    link(ve.tensor_tensor(t1, t0, g3(6 + rank), ALU.mult))
                    link(ve.tensor_reduce(mx, t1, AX.X, ALU.add))
                    link(ve.tensor_copy(IDX[:, 3 * rank:3 * rank + 3], mx))
                link(ve.tensor_reduce(G[0:1, 11, 0:1], PS[0:1, 3, 48:48 + NE], AX.X, ALU.max))
                link(ve.tensor_copy(COUNT[0:1, 0:NE], PS[0:1, 3, 48:48 + NE]))
                ve.tensor_copy(COUNT[0:1, NE:NE + 1], G[0:1, 11, 0:1]).then_inc(S(f"dispatch_ready{layer}"), 1)
                ve.wait_ge(*at(f"dispatch_ready{layer}", 1))
                most = ve.value_load(COUNT[0:1, NE:NE + 1], min_val=0, max_val=TOK)
                outer = dict(chain)
                with ve.If(most > 128):
                    for name in ("sel_ready", "sp_hidden", "sp_y_dve", "chain_sparse"):
                        ve.sem_inc(S(f"{name}{layer}"), PER_LAYER[name + "#"])
                    chain.update(name=f"chain_dense{layer}", n=0)
                    experts_dense(layer)
                    assert chain["n"] == PER_LAYER["chain_dense#"], chain
                with ve.Else():
                    for name in ("h_ready", "y_used", "chain_dense", "acc_zero"):
                        ve.sem_inc(S(f"{name}{layer}"), PER_LAYER[name + "#"])
                    chain.update(name=f"chain_sparse{layer}", n=0)
                    experts_sparse(layer)
                    assert chain["n"] == PER_LAYER["chain_sparse#"], chain
                chain.update(outer)
                ve.nop()

            def experts_sparse(layer):
                def select(e, par):
                    ve.tensor_tensor(SEL[:, par], cst("place").unsqueeze(1).to_broadcast([P, 3, 128]),
                                     WHERE[:, bass.ds(e * 3, 3)].unsqueeze(2).to_broadcast([P, 3, 128]),
                                     ALU.is_equal).then_inc(S(f"sel_ready{layer}"), 1)

                def expert(i, par, e, m):
                    p1 = 0 if m == 128 else 64
                    select(e + 1, 1 - par)
                    ve.wait_ge(*at(f"sp_sig{layer}", e + 1))
                    link(ve.tensor_tensor(MSG[0:m, 0, :], MSG[0:m, 0, :], PS[0:m, 0, :], ALU.mult))
                    ve.tensor_tensor(MH[0:m, 0, :], MSG[0:m, 0, :], PS[p1:p1 + m, 1, :], ALU.mult)\
                      .then_inc(S(f"sp_hidden{layer}"), 1)
                    ve.wait_ge(*at(f"sp_y_mm{layer}", e + 1))
                    ve.wait_ge(*at(f"sp_y_{'ab'[par]}_stored{layer}", i * 16 + 16))
                    ve.tensor_copy(YS[par][0:m, 512:1024], PS[p1:p1 + m, 7, :]).then_inc(S(f"sp_y_dve{layer}"), 1)

                select(0, 0)
                ve.sem_inc(S(f"sp_y_dve{layer}"), 1)
                with ve.Fori(0, NE // 2) as i:
                    loop(i, 2)
                    for par in range(2):
                        e = i * 2 + par
                        big = ve.value_load(COUNT[0:1, bass.ds(e, 1)], min_val=0, max_val=TOK)
                        n = chain["n"]
                        with ve.If(big > 64):
                            expert(i, par, e, 128)
                        chain["n"] = n
                        with ve.Else():
                            expert(i, par, e, 64)
                        ve.nop()
                loop_end(NE // 2)
                for t, (t0, n) in enumerate(TILES):
                    link(ve.tensor_scalar(X[0:n, t, :], X[0:n, t, :], ALPHA, None, ALU.mult))
                def combine(t):
                    n = TILES[t][1]
                    x = X[0:n, t, :]
                    ve.wait_ge(*at(f"tile{t}_moved{layer}", 32))
                    for rank in range(2):
                        link(ve.scalar_tensor_tensor(x, YG[0:n, rank, t, :], GATES[0:n, rank, t:t + 1], x,
                                                     ALU.mult, ALU.add))
                    moments(layer, t)

                norm(layer, 1, combine)

            def experts_dense(layer):
                ve.memset(ACC, 0.0).then_inc(S(f"acc_zero{layer}"), 1)
                ve.wait_ge(*at(f"acc_zero{layer}", 1))
                ve.sem_inc(S(f"h_ready{layer}"), 2)
                ve.sem_inc(S(f"y_used{layer}"), 1)
                with ve.Fori(0, NE // 2) as i:
                    loop(i, 6 + 4 + 2)
                    for u in range(7):
                        if u < 6:
                            t = u % 3
                            n = TILES[t][1]
                            p0 = 0 if t < 2 else NS
                            ve.wait_ge(*at(f"sig{layer}", i * 6 + (u + 1)))
                            sg, b0 = MSG[0:n, u % 2, :], 2 * (u % 2)
                            link(ve.tensor_tensor(sg, sg, PS[0:n, b0, :], ALU.mult))
                            ve.tensor_tensor(MH[0:n, u % 2, :], sg, PS[p0:p0 + n, b0 + 1, :], ALU.mult)\
                              .then_inc(S(f"h_ready{layer}"), 1)
                        if u >= 1:
                            v = u - 1
                            t = v % 3
                            n = TILES[t][1]
                            ve.wait_ge(*at(f"y_mm{layer}", i * 6 + (v + 1)))
                            comb = G[0:n, 10, bass.ds(i * 2 + (t * NE + v // 3), 1)]
                            for half in range(2):
                                p0 = 0 if t < 2 or half == 0 else NS
                                acc = ACC[0:n, t, 512 * half:512 * half + 512]
                                ins = ve.scalar_tensor_tensor(acc, PS[p0:p0 + n, 6 + half, :], comb, acc,
                                                              ALU.mult, ALU.add)
                                if half:
                                    ins.then_inc(S(f"y_used{layer}"), 1)
                                else:
                                    link(ins)
                loop_end(NE // 2)
                ve.wait_ge(*at(f"y_used{layer}", 3 * NE + 1))
                def combine(t):
                    n = TILES[t][1]
                    x = X[0:n, t, :]
                    link(ve.scalar_tensor_tensor(x, x, ALPHA, ACC[0:n, t, :], ALU.mult, ALU.add))
                    moments(layer, t)

                norm(layer, 1, combine)

            def gated_input(layer):
                ve.wait_ge(*at(f"gate_b_landed{layer}", 16))
                ve.wait_ge(*at(f"pp_mm{layer}", 1))
                for u in range(7):
                    if u < 6:
                        j, t = u // 3, u % 3
                        ve.wait_ge(*at(f"ple_mm{layer}", u + 1))
                        if u >= 2:
                            ve.wait_ge(*at(f"gated{layer}", u - 1))
                        for n, (p0, p1, c0, c1) in enumerate(pieces(t, 512)):
                            ins = ve.tensor_tensor(MSG[0:p1 - p0, u % 2, c0:c1], PS[p0:p1, GATE_BANK[u % 3], 0:c1 - c0],
                                                   GATE_BIAS[0:p1 - p0, 512 * j + c0:512 * j + c1], ALU.add)
                        ins.then_inc(S(f"gate_biased{layer}"), 1)
                    if u >= 1:
                        v = u - 1
                        j, t = v // 3, v % 3
                        ve.wait_ge(*at(f"gate_sig{layer}", v + 1))
                        n = TILES[t][1]
                        pp = PS[0:n, 2 * t + j, :] if t < 2 else PS[NS * j:NS * j + NS, 4, :]
                        link(ve.tensor_tensor(MSG[0:n, v % 2, :], MSG[0:n, v % 2, :], pp, ALU.mult))
                        x = X[0:n, t, 512 * j:512 * j + 512]
                        ins = ve.tensor_tensor(x, x, MSG[0:n, v % 2, :], ALU.add)
                        ins.then_inc(S(f"gated{layer}"), 1)
                ve.wait_ge(*at(f"gated{layer}", 6))

            norm(0, 0, residual(0))
            experts(0)
            gated_input(0)

            ve.memset(QB[:, 0:1792], 0.0).then_inc(S("qb_zero"), 1)
            ve.memset(OR[:, 0:NK], 0.0).then_inc(S("or_zero"), 1)
            ve.memset(QZI, 0.0).then_inc(S("pi_zero"), 1)
            for t, (t0, n) in enumerate(TILES):
                ve.wait_ge(*at("qkv_evac1", 6 + t + 1))
                rotate(t, 0, HB + KVB, 8, "cosA", "sinA", None)
                k = QKV[0:n, t, OFF_K:OFF_V].rearrange("p (g d) -> p g d", g=KVB)
                dk = QKV[0:n, t, DUP_K:DUP_K + 512].rearrange("p (g u d) -> p g u d", g=KVB, u=2)
                for u in range(2):
                    ve.tensor_copy(dk[:, :, u, :], k)
            for t, (t0, n) in enumerate(TILES):
                ve.wait_ge(*at("qkv_evac1", 12 + t + 1))
                rotate(t, OFF_QI, HI + 1, 16, "cosI", "sinI", "rotated1")
                ve.wait_ge(*at("rotated1", t + 1))
                ve.tensor_scalar(WI[0:n, t, :], QKV[0:n, t, OFF_WI:B_IN], IDX_SCALE, None, ALU.mult)
                ki = QKV[0:n, t, OFF_KI:OFF_WI].unsqueeze(1).to_broadcast([n, 2, HD])
                ve.tensor_copy(QKV[0:n, t, DUP_I:DUP_I + 128].rearrange("p (u d) -> p u d", u=2), ki)\
                  .then_inc(S("doubled"), 1)
            ve.wait_ge(*at("doubled", 3))
            ve.wait_ge(*at("spread_landed", 16))
            for u in range(4):
                for bb in range(2):
                    w = WI[0:NS, 2, :].unsqueeze(2).to_broadcast([NS, HI, DQ])
                    sp = spread[0:NS, 2 * u + bb, :].rearrange("p (h q) -> p h q", h=HI)
                    ins = ve.tensor_tensor(AT[0:NS, u, 64 * bb:64 * bb + 64].rearrange("p (h q) -> p h q", h=HI),
                                           w, sp, ALU.mult)
                ins.then_inc(S("ws_rows"), 1)
            ve.wait_ge(*at("bt_mm", 6))
            ve.wait_ge(*at("qb_zero", 2))
            for c in range(2):
                for h2 in range(2):
                    for g2 in range(2):
                        src = PS[64 * h2:64 * h2 + 64, 5, :].rearrange("p (c g k b q) -> p c g k b q", c=2, g=2, k=2, b=DB)
                        dst = QBB[64 * g2:64 * g2 + 64, :, c, :]\
                            .rearrange("p b (g k h q) -> p b g k h q", g=2, k=2, h=2)[:, :, g2, :, h2, :]
                        ve.tensor_copy(dst, src[:, c, g2].rearrange("p k b q -> p b k q")).then_inc(S("bt_evac_dve"), 1)
            ve.wait_ge(*at("bt_mm", 7))
            for h2 in range(2):
                for b2 in range(2):
                    src = PS[64 * h2:64 * h2 + 64, 6, 0:256].rearrange("p (c r b q) -> p c r b q", c=4, r=4, b=2)[:, :, :, b2]
                    dst = QIB[64 * b2:64 * b2 + 64, :, 64 * b2:64 * b2 + 64]\
                        .rearrange("p r (c h q) -> p r c h q", c=4, h=2)[:, :, :, h2, :]
                    ve.tensor_copy(dst, src.rearrange("p c r q -> p r c q")).then_inc(S("bt_evac_dve"), 1)

            for u in range(8):
                m, t = u // 2, u % 2
                kw = 128 * (t + 1)
                ve.wait_ge(*at("pi_relu", u + 1))
                for c in range(2):
                    s, w, acc = SM[:, u % 2, 256 * c:256 * c + kw], WI[:, t, 2 * m + c:2 * m + c + 1], PB[:, t, 0:kw]
                    start = causal[:, t, 0:kw] if m == 0 and c == 0 else acc
                    ins = ve.scalar_tensor_tensor(acc, s, w, start, ALU.mult, ALU.add)
                    if c:
                        ins.then_inc(S("pi_added"), 1)
                        ve.wait_ge(*at("pi_added", u + 1))
                    else:
                        link(ins)
            for r in range(SEL_PROMPT // 8):
                for t in range(2):
                    ins = ve.max(TOP8[:, t, :], PB[:, t, 0:128 * (t + 1)])
                link(ins)
                for t in range(2):
                    row = PB[:, t, 0:128 * (t + 1)]
                    ins = ve.match_replace(row, TOP8[:, t, :], row, PICKED)
                link(ins)
            for t in range(2):
                row = PB[:, t, 0:128 * (t + 1)]
                link(ve.tensor_scalar(row, row, -2.5e38, -BIG, ALU.is_gt, ALU.mult))
                link(ve.tensor_tensor(row, row, causal[:, t, 0:128 * (t + 1)], ALU.add))
            ve.wait_ge(*at("si_sum_mm", 9))
            ve.wait_ge(*at("or_zero", 1))
            ve.tensor_copy(SCORE[:, 0:512], PS[:, 5, :])
            ve.memset(SCORE[0:NS, 512:HALF], PICKED)
            link(ve.tensor_tensor(SCORE[NS:P, 512:HALF], PS[0:NS, 6, 0:NS], cst("selnew", NS), ALU.add))
            ve.wait_ge(*at("kidx_evac", 8))
            ve.wait_ge(*at("sis_mm", 9))
            ve.memset(QZ, 0.0).then_inc(S("pq1_zero"), 1)
            for r in range(SEL_SAMPLE // 8):
                largest, left = SORTED[:, 8 * r:8 * r + 8], SCORE if r == 0 else PICK
                ve.max(largest, left).then_inc(S("sorted"), 1)
                ve.wait_ge(*at("sorted", r + 1))
                link(ve.match_replace(PICK, largest, left, PICKED))
            ve.wait_ge(*at("sort_mm", 2))
            first, second = SORTED[0:NS, :], PS[0:NS, 5, 0:SEL_SAMPLE]
            taken, other = PICK[0:NS, 0:SEL_SAMPLE], PICK[0:NS, SEL_SAMPLE:2 * SEL_SAMPLE]
            for rank, (values, least, ties) in enumerate((
                    (first, LEAST[0:NS], TIES[0:NS]), (second, small[0:NS, 150:151], small[0:NS, 151:152]))):
                link(ve.tensor_tensor(taken, first, second, ALU.is_ge if rank == 0 else ALU.is_lt))
                link(ve.tensor_scalar(other, taken, -1.0, PICKED, ALU.add, ALU.mult))
                link(ve.tensor_tensor(taken, taken, values, ALU.mult))
                link(ve.tensor_tensor(other, other, taken, ALU.add))
                link(ve.tensor_reduce(least, other, AX.X, ALU.min))
                link(ve.tensor_scalar(other, other, least, None, ALU.is_equal))
                link(ve.tensor_reduce(ties, other, AX.X, ALU.add))
            link(ve.tensor_copy(small[NS:P, 148:150], small[0:NS, 150:152]))
            ve.tensor_scalar(ABOVE, SCORE, LEAST, None, ALU.is_gt)
            link(ve.tensor_scalar(EQUAL, SCORE, LEAST, None, ALU.is_equal))
            link(ve.tensor_tensor_scan(PICK, EQUAL, EQUAL, 0.0, ALU.add, ALU.max))
            link(ve.scalar_tensor_tensor(PICK, PICK, TIES, EQUAL, ALU.is_le, ALU.mult))
            link(ve.scalar_tensor_tensor(PICK, ABOVE, -1.0, PICK, ALU.add, ALU.add))
            ve.tensor_scalar(SELB[0:NS, 0:512], PICK[0:NS, 0:512], BIG, None, ALU.mult)
            ve.tensor_scalar(SELB[NS:P, 512:NK], PICK[NS:P, :], BIG, None, ALU.mult).then_inc(S("selection"), 1)

            for b in range(DB):
                scores, weights, outputs = prompt_stages(1, b)
                for qt in range(2):
                    scores(qt)
                    weights(qt)
                outputs(0)
                ve.wait_ge(*at("sb_mm", b + 1))
                link(ve.tensor_reduce(small[:, 4:5], PSF[:, 2048:2048 + NK], AX.X, ALU.max))
                ve.tensor_scalar(NMAX[:, b % 2:b % 2 + 1], small[:, 4:5], -SCALE, None, ALU.mult)\
                  .then_inc(S("row_maxb"), 1)
                outputs(1)
                ve.wait_ge(*at("expb_done", b + 1))
                link(ve.reciprocal(RC[:, 0:1], SUMS[:, b % 2:b % 2 + 1]))
                ve.wait_ge(*at("pvb_mm", b + 1))
                for j in range(4):
                    c0 = 256 + (j % 2) * 64
                    src = PS[32 * j:32 * j + 32, 6, c0:c0 + 64].unsqueeze(1).to_broadcast([32, 2, 64])
                    ve.tensor_scalar(OB[32 * j:32 * j + 32, b, :, :], src, RC[32 * j:32 * j + 32, 0:1], None, ALU.mult)\
                      .then_inc(S("ob"), 1)

            norm(1, 0, residual(1))
            experts(1)
            gated_input(1)


_INS = ["x_prompt", "x_sample", "cache_a_k", "cache_a_v", "cache_b_k", "cache_b_v", "cache_b_kidx", "page_table",
        "p_prompt", "p_sample", "a_w_in", "a_w_out", "a_lam_q1", "a_lam_k1", "a_lam_q2", "a_lam_k2", "a_subln",
        "b_w_in", "b_w_out", "ln_g", "ln_b", "router_w", "router_b", "moe_w_gate", "moe_w_up", "moe_w_down",
        "ple_proj", "ple_gate_w", "ple_gate_b"]
_OUTS = [(1, SEQ, D), (DB, DQ, D), (1, 1, SEQ, 2 * HA, HD), (1, 1, SEQ, HA, 2 * HD), (1, 1, SEQ, KVB, HD),
         (1, 1, SEQ, KVB, HD), (1, 1, SEQ, HD), (1, DB, DQ, 2 * HA, HD), (1, DB, DQ, HA, 2 * HD),
         (1, DB, DQ, KVB, HD), (1, DB, DQ, KVB, HD), (1, DB, DQ, HD)]


def program(nc, shapes):
    args = [nc.dram_tensor(f"in_{n}", shapes[n][0], mybir.dt.from_np(shapes[n][1]), kind="ExternalInput").ap()
            for n in _INS + ["consts", "spread"]]
    outs = [nc.dram_tensor(f"out_{i}", shape, F32, kind="ExternalOutput").ap() for i, shape in enumerate(_OUTS)]
    build(nc, *args, outs)


def kernel(**inputs):
    import concourse.bacc as _bacc
    from concourse.bass_utils import run_bass_kernel_spmd as _run

    nc = _bacc.Bacc("TRN2", target_bir_lowering=False, num_devices=1)
    arrays = {n: np.ascontiguousarray(inputs[n]) for n in _INS}
    arrays["consts"], arrays["spread"] = constants()
    program(nc, {n: (a.shape, a.dtype) for n, a in arrays.items()})
    r = _run(nc, [{f"in_{n}": a for n, a in arrays.items()}], core_ids=[0])
    return tuple(r.results[0][f"out_{i}"] for i in range(len(_OUTS)))
```
